# Optimizing a Trainium2 kernel written in Bass

```python
import math
import jax, jax.numpy as jnp
from jax import lax
import numpy as np

D_MODEL = 1024
BATCH = 1
SEQ = 512
DEPTH = 2

D_MLSTM = D_MODEL
N_MLSTM_HEADS = 4
MLSTM_HEAD_DIM = D_MLSTM // N_MLSTM_HEADS
D_CONV = D_MODEL
N_CONV_GROUPS = 8
D_MIX = D_MLSTM + D_CONV
D_IN_PROJ = 2 * D_MLSTM + 2 * D_CONV
MLSTM_CONV_K = 4
CONFORMER_CONV_K = 31
CHUNK = 128
D_FF = 4 * D_MODEL
N_ADA = 6
EPS = 1e-6


def rms_norm(x, g):
    xf = x.astype(jnp.float32)
    y = xf * lax.rsqrt(jnp.mean(xf * xf, axis=-1, keepdims=True) + EPS)
    return (y * g.astype(jnp.float32)).astype(x.dtype)

def group_layer_norm(x, n_groups, g, b=None):
    shp = x.shape
    xf = x.astype(jnp.float32).reshape(*shp[:-1], n_groups, shp[-1] // n_groups)
    mu = jnp.mean(xf, axis=-1, keepdims=True)
    xc = xf - mu
    var = jnp.mean(xc * xc, axis=-1, keepdims=True)
    y = (xc * lax.rsqrt(var + EPS)).reshape(shp) * g.astype(jnp.float32)
    if b is not None:
        y = y + b.astype(jnp.float32)
    return y.astype(x.dtype)

def causal_depthwise_conv(x, w, b):
    K, C = w.shape
    y = lax.conv_general_dilated(
        x, w[:, None, :].astype(x.dtype), window_strides=(1,), padding=[(K - 1, 0)],
        dimension_numbers=("NWC", "WIO", "NWC"), feature_group_count=C)
    return y + b.astype(x.dtype)

def mlstm_chunkwise(q, k, v, ig, lf):
    B, T, H, Dh = q.shape
    nc = T // CHUNK

    def to_chunks(a):
        a = a.astype(jnp.float32).reshape(B, nc, CHUNK, H, *a.shape[3:])
        return jnp.moveaxis(a, (1, 3), (0, 2))

    xs = (to_chunks(q), to_chunks(k), to_chunks(v), to_chunks(ig), to_chunks(lf))
    causal = jnp.tril(jnp.ones((CHUNK, CHUNK), dtype=bool))

    def body(carry, inp):
        C, n, m = carry
        qc, kc, vc, igc, lfc = inp
        b = jnp.cumsum(lfc, axis=-1)
        logw = b[..., :, None] - b[..., None, :] + igc[..., None, :]
        logw = jnp.where(causal, logw, -jnp.inf)
        g = b + m[..., None]
        m_t = jnp.maximum(g, jnp.max(logw, axis=-1))
        w = jnp.exp(logw - m_t[..., None])
        inter = jnp.exp(g - m_t)
        s = jnp.einsum("bhtd,bhsd->bhts", qc, kc) * w
        num = jnp.einsum("bhts,bhse->bhte", s, vc) + inter[..., None] * jnp.einsum("bhtd,bhde->bhte", qc, C)
        den = jnp.sum(s, axis=-1) + inter * jnp.einsum("bhtd,bhd->bht", qc, n)
        h = num / jnp.maximum(jnp.abs(den), jnp.exp(-m_t))[..., None]
        b_last = b[..., -1]
        a = b_last[..., None] - b + igc
        m_new = jnp.maximum(b_last + m, jnp.max(a, axis=-1))
        wk = jnp.exp(a - m_new[..., None])
        decay = jnp.exp(b_last + m - m_new)
        C_new = decay[..., None, None] * C + jnp.einsum("bhs,bhsd,bhse->bhde", wk, kc, vc)
        n_new = decay[..., None] * n + jnp.einsum("bhs,bhsd->bhd", wk, kc)
        return (C_new, n_new, m_new), h

    init = (jnp.zeros((B, H, Dh, Dh), jnp.float32), jnp.zeros((B, H, Dh), jnp.float32),
            jnp.zeros((B, H), jnp.float32))
    _, hs = lax.scan(body, init, xs)
    return jnp.moveaxis(hs, (0, 2), (1, 3)).reshape(B, T, H, Dh)

def mixer(h, w_in, w_conv_m, b_conv_m, w_q, w_k, w_v, w_gates, b_gates, g_mh,
          w_dw, b_dw, g_cn, b_cn, w_out):
    B, T, _ = h.shape
    H, Dh = N_MLSTM_HEADS, MLSTM_HEAD_DIM
    u = h @ w_in.astype(h.dtype)
    x_m, z, glu_a, glu_b = jnp.split(u, [D_MLSTM, 2 * D_MLSTM, 2 * D_MLSTM + D_CONV], axis=-1)

    x_c = jax.nn.silu(causal_depthwise_conv(x_m, w_conv_m, b_conv_m))
    xc_h = x_c.reshape(B, T, H, Dh)
    xm_h = x_m.reshape(B, T, H, Dh)
    q = jnp.einsum("bthd,hde->bthe", xc_h, w_q.astype(h.dtype))
    k = jnp.einsum("bthd,hde->bthe", xc_h, w_k.astype(h.dtype))
    v = jnp.einsum("bthd,hde->bthe", xm_h, w_v.astype(h.dtype))
    qkv = jnp.concatenate([q, k, v], axis=-1).reshape(B, T, H, 3 * Dh)
    qkv = jnp.moveaxis(qkv, 2, 3).reshape(B, T, 3 * D_MLSTM)
    gates = (qkv @ w_gates.astype(h.dtype) + b_gates.astype(h.dtype)).astype(jnp.float32)
    ig, fg = gates[..., :H], gates[..., H:]
    lf = jax.nn.log_sigmoid(fg)
    h_m = mlstm_chunkwise(q, k * (Dh ** -0.5), v, ig, lf)
    h_m = group_layer_norm(h_m.reshape(B, T, D_MLSTM), H, g_mh).astype(h.dtype)
    h_m = jax.nn.sigmoid(z) * h_m

    a = glu_a * jax.nn.sigmoid(glu_b)
    a = causal_depthwise_conv(a, w_dw, b_dw)
    a = jax.nn.silu(group_layer_norm(a, N_CONV_GROUPS, g_cn, b_cn))

    return jnp.concatenate([h_m, a], axis=-1) @ w_out.astype(h.dtype)

def first_inputs(seed: int = 0) -> dict:
    key = jax.random.key(seed)
    ks = jax.random.split(key, 26)
    f32 = jnp.float32

    def nrm(k, shape, fan_in, scale=1.0):
        return jax.random.normal(k, shape, f32) * (scale * fan_in ** -0.5)

    def gain(k, shape):
        return 1.0 + 0.05 * jax.random.normal(k, shape, f32)

    def small(k, shape):
        return 0.02 * jax.random.normal(k, shape, f32)

    H = N_MLSTM_HEADS
    ig_bias = 0.1 * jax.random.normal(ks[24], (DEPTH, H), f32)
    fg_bias = jnp.linspace(3.0, 6.0, H, dtype=f32)[None, :] + 0.1 * jax.random.normal(ks[25], (DEPTH, H), f32)
    return {
        "x": jax.random.normal(ks[0], (BATCH, SEQ, D_MODEL), f32),
        "c": jax.random.normal(ks[1], (BATCH, D_MODEL), f32),
        "w_ada": nrm(ks[2], (DEPTH, D_MODEL, N_ADA * D_MODEL), D_MODEL, 0.5),
        "b_ada": small(ks[3], (DEPTH, N_ADA * D_MODEL)),
        "g_pre_mix": gain(ks[4], (DEPTH, D_MODEL)),
        "g_post_mix": gain(ks[5], (DEPTH, D_MODEL)),
        "g_pre_mlp": gain(ks[6], (DEPTH, D_MODEL)),
        "g_post_mlp": gain(ks[7], (DEPTH, D_MODEL)),
        "w_in": nrm(ks[8], (DEPTH, D_MODEL, D_IN_PROJ), D_MODEL),
        "w_conv_m": nrm(ks[9], (DEPTH, MLSTM_CONV_K, D_MLSTM), MLSTM_CONV_K),
        "b_conv_m": small(ks[10], (DEPTH, D_MLSTM)),
        "w_q": nrm(ks[11], (DEPTH, H, MLSTM_HEAD_DIM, MLSTM_HEAD_DIM), MLSTM_HEAD_DIM),
        "w_k": nrm(ks[12], (DEPTH, H, MLSTM_HEAD_DIM, MLSTM_HEAD_DIM), MLSTM_HEAD_DIM),
        "w_v": nrm(ks[13], (DEPTH, H, MLSTM_HEAD_DIM, MLSTM_HEAD_DIM), MLSTM_HEAD_DIM),
        "w_gates": nrm(ks[14], (DEPTH, 3 * D_MLSTM, 2 * H), 3 * D_MLSTM),
        "b_gates": jnp.concatenate([ig_bias, fg_bias], axis=-1),
        "g_mh": gain(ks[15], (DEPTH, D_MLSTM)),
        "w_dw": nrm(ks[16], (DEPTH, CONFORMER_CONV_K, D_CONV), CONFORMER_CONV_K),
        "b_dw": small(ks[17], (DEPTH, D_CONV)),
        "g_cn": gain(ks[18], (DEPTH, D_CONV)),
        "b_cn": small(ks[19], (DEPTH, D_CONV)),
        "w_out": nrm(ks[20], (DEPTH, D_MIX, D_MODEL), D_MIX),
        "w_ff1": nrm(ks[21], (DEPTH, D_MODEL, D_FF), D_MODEL),
        "w_ff2": nrm(ks[22], (DEPTH, D_FF, D_MODEL), D_FF),
    }

def first_block(x, c, w_ada, b_ada, g_pre_mix, g_post_mix, g_pre_mlp, g_post_mlp, w_in,
              w_conv_m, b_conv_m, w_q, w_k, w_v, w_gates, b_gates, g_mh, w_dw, b_dw,
              g_cn, b_cn, w_out, w_ff1, w_ff2):
    c_act = jax.nn.silu(c.astype(jnp.float32))
    for l in range(DEPTH):
        mod = (c_act @ w_ada[l].astype(jnp.float32) + b_ada[l].astype(jnp.float32)).astype(x.dtype)
        sh_mix, sc_mix, gt_mix, sh_mlp, sc_mlp, gt_mlp = [m[:, None, :] for m in jnp.split(mod, N_ADA, axis=-1)]

        h = rms_norm(x, g_pre_mix[l]) * (1 + sc_mix) + sh_mix
        y = mixer(h, w_in[l], w_conv_m[l], b_conv_m[l], w_q[l], w_k[l], w_v[l], w_gates[l], b_gates[l],
                  g_mh[l], w_dw[l], b_dw[l], g_cn[l], b_cn[l], w_out[l])
        x = x + gt_mix * rms_norm(y, g_post_mix[l])

        h = rms_norm(x, g_pre_mlp[l]) * (1 + sc_mlp) + sh_mlp
        f = jnp.square(jax.nn.relu(h @ w_ff1[l].astype(h.dtype))) @ w_ff2[l].astype(h.dtype)
        x = x + gt_mlp * rms_norm(f, g_post_mlp[l])
    return x


DEPTH_2 = 1

HEAD_DIM = 64
A_HEADS = 8
A_KV_HEADS = 2
IDX_HEADS = 8
IDX_DIM = 64
TOPK_MAX = 256
B_HEADS = 8
B_KV_HEADS = 2
WINDOW = 128
Q_BLOCK = 128
D_FF_2 = 4 * D_MODEL
ROPE_THETA = 10000.0
RMS_EPS = 1e-6
LN_EPS = 1e-6

A_Q = A_HEADS * HEAD_DIM
A_KV = A_KV_HEADS * HEAD_DIM
IDX_Q = IDX_HEADS * IDX_DIM
B_Q = B_HEADS * HEAD_DIM
B_KV = B_KV_HEADS * HEAD_DIM
SPLIT_SIZES = (A_Q, A_KV, A_KV, IDX_Q, IDX_DIM, IDX_HEADS, B_Q, B_KV, B_KV, D_MODEL, D_MODEL)
D_IN = sum(SPLIT_SIZES)


def rmsnorm(x, g):
    xf = x.astype(jnp.float32)
    y = xf * lax.rsqrt(jnp.mean(xf * xf, axis=-1, keepdims=True) + RMS_EPS)
    return (y * g.astype(jnp.float32)).astype(x.dtype)

def layernorm(x, w, b):
    xf = x.astype(jnp.float32)
    mu = jnp.mean(xf, axis=-1, keepdims=True)
    var = jnp.mean(jnp.square(xf - mu), axis=-1, keepdims=True)
    y = (xf - mu) * lax.rsqrt(var + LN_EPS)
    return (y * w.astype(jnp.float32) + b.astype(jnp.float32)).astype(x.dtype)

def rope_tables(L, dim):
    inv = 1.0 / (ROPE_THETA ** (jnp.arange(0, dim, 2, dtype=jnp.float32) / dim))
    ang = jnp.arange(L, dtype=jnp.float32)[:, None] * inv[None, :]
    return jnp.cos(ang), jnp.sin(ang)

def apply_rope(x, cos, sin):
    xf = x.astype(jnp.float32)
    x1, x2 = jnp.split(xf, 2, axis=-1)
    c = cos[None, :, None, :]
    s = sin[None, :, None, :]
    return jnp.concatenate([x1 * c - x2 * s, x2 * c + x1 * s], axis=-1).astype(x.dtype)

def dsa_branch(q, k, v, q_idx, k_idx, w_idx, topk):
    Bn, L, H, dh = q.shape
    G = k.shape[2]
    R = H // G
    nb = L // Q_BLOCK
    kpos = jnp.arange(L)
    k_idx32 = k_idx.astype(jnp.float32)
    scale = HEAD_DIM ** -0.5

    def one_block(i):
        start = i * Q_BLOCK
        qb = lax.dynamic_slice_in_dim(q, start, Q_BLOCK, axis=1)
        qib = lax.dynamic_slice_in_dim(q_idx, start, Q_BLOCK, axis=1)
        wb = lax.dynamic_slice_in_dim(w_idx, start, Q_BLOCK, axis=1)
        qpos = start + jnp.arange(Q_BLOCK)
        s = jnp.einsum('bqhd,bkd->bqhk', qib.astype(jnp.float32), k_idx32)
        score = jnp.einsum('bqhk,bqh->bqk', jax.nn.relu(s), wb.astype(jnp.float32))
        causal = kpos[None, :] <= qpos[:, None]
        score = jnp.where(causal[None], score, -jnp.inf)
        _, sel = lax.top_k(score, topk)
        ks = jax.vmap(lambda kk, ii: kk[ii])(k, sel)
        vs = jax.vmap(lambda vv, ii: vv[ii])(v, sel)
        valid = sel <= qpos[None, :, None]
        qg = qb.reshape(Bn, Q_BLOCK, G, R, dh).astype(jnp.float32)
        logits = jnp.einsum('bqgrd,bqkgd->bqgrk', qg, ks.astype(jnp.float32)) * scale
        logits = jnp.where(valid[:, :, None, None, :], logits, -jnp.inf)
        p = jax.nn.softmax(logits, axis=-1)
        o = jnp.einsum('bqgrk,bqkgd->bqgrd', p, vs.astype(jnp.float32))
        return o.reshape(Bn, Q_BLOCK, H * dh).astype(q.dtype)

    out = lax.map(one_block, jnp.arange(nb))
    return jnp.transpose(out, (1, 0, 2, 3)).reshape(Bn, L, H * dh)

def swa_branch(q, k, v, sinks):
    Bn, L, H, dh = q.shape
    G = k.shape[2]
    R = H // G
    W = WINDOW
    nb = L // W
    qb = q.reshape(Bn, nb, W, G, R, dh).astype(jnp.float32)
    pad = ((0, 0), (W, 0), (0, 0), (0, 0))
    kp = jnp.pad(k, pad).reshape(Bn, nb + 1, W, G, dh)
    vp = jnp.pad(v, pad).reshape(Bn, nb + 1, W, G, dh)
    kb = jnp.concatenate([kp[:, :-1], kp[:, 1:]], axis=2).astype(jnp.float32)
    vb = jnp.concatenate([vp[:, :-1], vp[:, 1:]], axis=2).astype(jnp.float32)
    logits = jnp.einsum('bnqgrd,bnkgd->bngrqk', qb, kb) * (HEAD_DIM ** -0.5)
    rel = jnp.arange(W)[:, None] + W - jnp.arange(2 * W)[None, :]
    kabs = jnp.arange(nb)[:, None] * W - W + jnp.arange(2 * W)[None, :]
    mask = ((rel >= 0) & (rel < W))[None, :, :] & (kabs >= 0)[:, None, :]
    logits = jnp.where(mask[None, :, None, None, :, :], logits, -jnp.inf)
    sink = jnp.broadcast_to(sinks.astype(jnp.float32).reshape(1, 1, G, R, 1, 1), logits.shape[:-1] + (1,))
    p = jax.nn.softmax(jnp.concatenate([logits, sink], axis=-1), axis=-1)[..., :-1]
    o = jnp.einsum('bngrqk,bnkgd->bnqgrd', p, vb)
    return o.reshape(Bn, L, H * dh).astype(q.dtype)

def second_inputs(seed: int = 0) -> dict:
    key = jax.random.key(seed)
    ks = jax.random.split(key, 14)
    f32 = jnp.float32
    nrm = lambda k, shape: jax.random.normal(k, shape, dtype=f32)
    return {
        "x": nrm(ks[0], (BATCH, SEQ, D_MODEL)),
        "attn_norm_w": 1.0 + 0.02 * nrm(ks[1], (DEPTH_2, D_MODEL)),
        "w_in": nrm(ks[2], (DEPTH_2, D_MODEL, D_IN)) * D_MODEL ** -0.5,
        "idx_k_norm_w": 1.0 + 0.02 * nrm(ks[3], (DEPTH_2, IDX_DIM)),
        "idx_k_norm_b": 0.02 * nrm(ks[4], (DEPTH_2, IDX_DIM)),
        "sinks": 0.5 * nrm(ks[5], (DEPTH_2, B_HEADS)),
        "w_branch_a": nrm(ks[6], (DEPTH_2, A_Q, D_MODEL)) * A_Q ** -0.5,
        "w_branch_b": nrm(ks[7], (DEPTH_2, B_Q, D_MODEL)) * B_Q ** -0.5,
        "w_out": nrm(ks[8], (DEPTH_2, D_MODEL, D_MODEL)) * D_MODEL ** -0.5,
        "mlp_norm_w": 1.0 + 0.02 * nrm(ks[9], (DEPTH_2, D_MODEL)),
        "w_up": nrm(ks[10], (DEPTH_2, D_MODEL, D_FF_2)) * D_MODEL ** -0.5,
        "w_down": nrm(ks[11], (DEPTH_2, D_FF_2, D_MODEL)) * D_FF_2 ** -0.5,
        "final_norm_w": 1.0 + 0.02 * nrm(ks[12], (D_MODEL,)),
    }

def second_block(x, attn_norm_w, w_in, idx_k_norm_w, idx_k_norm_b, sinks, w_branch_a, w_branch_b,
              w_out, mlp_norm_w, w_up, w_down, final_norm_w):
    Bn, L, _ = x.shape
    topk = min(TOPK_MAX, L // 4)
    cos, sin = rope_tables(L, HEAD_DIM)
    cos_i, sin_i = rope_tables(L, IDX_DIM)
    offsets = [sum(SPLIT_SIZES[:i + 1]) for i in range(len(SPLIT_SIZES) - 1)]
    w_scale = (IDX_HEADS ** -0.5) * (IDX_DIM ** -0.5)

    for l in range(DEPTH_2):
        h = rmsnorm(x, attn_norm_w[l])
        proj = jnp.einsum('bld,de->ble', h, w_in[l])
        a_q, a_k, a_v, i_q, i_k, i_w, b_q, b_k, b_v, g_a, g_b = jnp.split(proj, offsets, axis=-1)

        a_q = apply_rope(a_q.reshape(Bn, L, A_HEADS, HEAD_DIM), cos, sin)
        a_k = apply_rope(a_k.reshape(Bn, L, A_KV_HEADS, HEAD_DIM), cos, sin)
        a_v = a_v.reshape(Bn, L, A_KV_HEADS, HEAD_DIM)
        i_q = apply_rope(i_q.reshape(Bn, L, IDX_HEADS, IDX_DIM), cos_i, sin_i)
        i_k = layernorm(i_k, idx_k_norm_w[l], idx_k_norm_b[l])
        i_k = apply_rope(i_k[:, :, None, :], cos_i, sin_i)[:, :, 0, :]
        i_w = i_w * w_scale
        o_a = dsa_branch(a_q, a_k, a_v, i_q, i_k, i_w, topk)

        b_q = apply_rope(b_q.reshape(Bn, L, B_HEADS, HEAD_DIM), cos, sin)
        b_k = apply_rope(b_k.reshape(Bn, L, B_KV_HEADS, HEAD_DIM), cos, sin)
        b_v = b_v.reshape(Bn, L, B_KV_HEADS, HEAD_DIM)
        o_b = swa_branch(b_q, b_k, b_v, sinks[l])

        y_a = jnp.einsum('ble,ed->bld', o_a, w_branch_a[l])
        y_b = jnp.einsum('ble,ed->bld', o_b, w_branch_b[l])
        mix = jax.nn.sigmoid(g_a) * y_a + jax.nn.sigmoid(g_b) * y_b
        x = x + jnp.einsum('bld,de->ble', mix, w_out[l])

        h2 = rmsnorm(x, mlp_norm_w[l])
        u = jax.nn.relu(jnp.einsum('bld,df->blf', h2, w_up[l]))
        x = x + jnp.einsum('blf,fd->bld', u * u, w_down[l])

    return rmsnorm(x, final_norm_w)


def setup_inputs(seed=0):
    out = dict(first_inputs(seed))
    for name, value in second_inputs(seed + 1).items():
        if name != "x":
            out[name + "_2"] = value
    return out


def reference(
    x, c, w_ada, b_ada, g_pre_mix, g_post_mix, g_pre_mlp, g_post_mlp, w_in, w_conv_m, b_conv_m,
    w_q, w_k, w_v, w_gates, b_gates, g_mh, w_dw, b_dw, g_cn, b_cn, w_out, w_ff1, w_ff2,
    attn_norm_w_2, w_in_2, idx_k_norm_w_2, idx_k_norm_b_2, sinks_2, w_branch_a_2, w_branch_b_2,
    w_out_2, mlp_norm_w_2, w_up_2, w_down_2, final_norm_w_2,
):
    x = first_block(
        x, c, w_ada, b_ada, g_pre_mix, g_post_mix, g_pre_mlp, g_post_mlp, w_in, w_conv_m,
        b_conv_m, w_q, w_k, w_v, w_gates, b_gates, g_mh, w_dw, b_dw, g_cn, b_cn, w_out, w_ff1,
        w_ff2,
    )
    return second_block(
        x, attn_norm_w_2, w_in_2, idx_k_norm_w_2, idx_k_norm_b_2, sinks_2, w_branch_a_2,
        w_branch_b_2, w_out_2, mlp_norm_w_2, w_up_2, w_down_2, final_norm_w_2,
    )


_drawn_inputs = setup_inputs


def setup_inputs(seed=0):
    import zlib

    import numpy as np

    out = dict(_drawn_inputs(seed))
    spreads = {}
    factors = {'b_conv_m': 4.332,
     'g_mh': 3.299,
     'b_dw': 3.629,
     'b_cn': 6.398,
     'attn_norm_w_2': 5.682,
     'idx_k_norm_w_2': 8.0,
     'idx_k_norm_b_2': 8.0,
     'sinks_2': 33.28,
     'mlp_norm_w_2': 3.331,
     'final_norm_w_2': 8.011}
    for name, (base, spread) in spreads.items():
        noise = np.random.default_rng([zlib.crc32(name.encode()), seed]).standard_normal(out[name].shape)
        drawn = base * np.exp(spread * noise) if base else spread * noise
        out[name] = __import__('jax').numpy.asarray(drawn.astype(out[name].dtype))
    for name, factor in factors.items():
        out[name] = (out[name] * factor).astype(out[name].dtype)
    return out
```

```python
from contextlib import ExitStack

import numpy as np

import concourse.bass as bass
from concourse import mybir

ALU = mybir.AluOpType
ACT = mybir.ActivationFunctionType
F32 = mybir.dt.float32
F32R = mybir.dt.float32r

P = 128
T = 512
D = 1024
NT = D // P
LAYERS = 2
HEADS = 4
BLK = T // P
FF = 4
EPS = 1e-6
ACT_LAYER, DVE_LAYER, DVE_GROUP = 19, 441, 7
NEG = -1e30
CONV_M, CONV_C = 4, 31

RING = 4
KC = 4
CW = 256
AHEAD = 3

I_IN, I_V, I_Q, I_K, I_GATE, I_OUT, I_FF = 0, 32, 34, 36, 38, 40, 56
FF_CHUNKS = 16
LAYER_CHUNKS = I_FF + FF * FF_CHUNKS
GATE_CHUNKS = (I_GATE, I_GATE + 1)
O_GLUB, O_GLUA, O_XM, O_Z, O_V, O_Q, O_K, O_HEAD, O_OUTA, O_OUTH, O_FF = 0, 8, 16, 24, 32, 40, 48, 56, 72, 80, 88
FF_TILES = 16
LAYER_TILES = O_FF + FF * FF_TILES
ADA_UNITS, ADA_FIRST, ADA_MIXER = 12, 4, 8

V_BADA, V_GPREM, V_GPOSTM, V_GPREF, V_GPOSTF, V_BCM, V_GMH, V_BDW, V_GCN, V_BCN = 0, 48, 56, 64, 72, 80, 88, 96, 104, 112
V_WCM, V_WDW = 128, 160
PARAM_DMAS = 15


class Signal:

    def __init__(self, sem, layer=0, group=0):
        self.sem, self.layer, self.group = sem, layer, group


class Place:

    def __init__(self, layer=0, group=None):
        self.layer, self.group = layer, group

    def value(self, signal, n):
        v = n
        if signal.layer:
            v = self.layer * signal.layer + v
        if signal.group and self.group is not None:
            v = self.group * signal.group + v
        return v


class Steps:

    def __init__(self, eng, sem):
        self.eng, self.sem, self.n, self.loops, self.began = eng, sem, 0, [], []

    def did(self, instruction):
        instruction.then_inc(self.sem, 1)
        self.n += 1
        return self.n

    def wait(self, n=None):
        v = self.n if n is None else n
        for register, per in self.loops:
            v = register * per + v
        self.eng.wait_ge(self.sem, v)

    def enter(self, register, per):
        self.loops.append((register, per))
        self.began.append(self.n)

    def leave(self, times):
        _, per = self.loops.pop()
        start = self.began.pop()
        assert self.n - start == per, (self.eng, self.n - start, per)
        self.n = start + per * times


class Region:

    def __init__(self, tensors, starts):
        self.tensors, self.starts = tensors, starts

    def __getitem__(self, at):
        rows, columns = at
        k = max(k for k in range(len(self.tensors)) if self.starts[k] <= columns.start)
        start = self.starts[k]
        assert columns.stop <= self.starts[k + 1]
        return self.tensors[k][rows, columns.start - start:columns.stop - start]


def rope_tables():
    inv = np.float32(1.0) / np.power(np.float32(10000.0), np.arange(0, 64, 2, dtype=np.float32) / np.float32(64))
    angle = np.arange(T, dtype=np.float32)[None, :] * inv.astype(np.float32)[:, None]
    return np.cos(angle).astype(np.float32), np.sin(angle).astype(np.float32)


class Plan:

    def __init__(self, plain=(), width={}):
        self.plain, self.width = plain, width
        self.used, self.tile = [0], {}

    def split(self, i):
        return i + 1 - sum(g <= i for g in self.plain)

    def chunk(self, tiles, finished=()):
        for at, n in finished:
            self.tile[n] = self.used[-1] + at + 1
        self.used.append(self.used[-1] + tiles)

    def pair(self, n):
        self.chunk(2)
        self.chunk(2, [(0, n), (1, n + 1)])


def layer_plan():
    plan = Plan(GATE_CHUNKS)
    for p in range(16):
        plan.pair(2 * p)
    for c in range(6):
        plan.chunk(4, [(j, O_V + 4 * c + j) for j in range(4)])
    plan.chunk(1)
    plan.chunk(1)
    for p in range(8):
        plan.pair(O_OUTA + 2 * p)
    for p in range(FF * FF_CHUNKS // 2):
        plan.pair(O_FF + 2 * p)
    assert len(plan.used) == LAYER_CHUNKS + 1
    return plan


LAYER = layer_plan()

HD, IH, TOPK = 64, 8, 128
IK = HD + IH
W_SCALE = IH ** -0.5 * HD ** -0.5
SELECTED = float(np.float32(-3e38))
PROJ = ([(768, CW), (1024, CW), (1280, IK), (0, CW), (256, CW), (512, CW), (1352, CW), (1608, CW), (1864, CW)]
        + [(2120 + p * CW, CW) for p in range(8)])
J_BRANCH = 2 * len(PROJ)
J_OUT = J_BRANCH + 8
J_FF = J_OUT + 8
U_IQ, U_IK, U_AQ, U_AK, U_AV, U_BQ, U_BK, U_BV, U_GA = 0, 4, 5, 9, 10, 11, 15, 16, 17
U_ATT, U_BR, U_OUT, U_FF = 33, 49, 65, 73
U_LAST = U_FF + FF * FF_TILES
UNITS = 2 * BLK * 8
FIRST_OF = [2 * p - (p > 2) for p in range(len(PROJ))]
PAIR_OF = {o + m: p for p, o in enumerate(FIRST_OF) for m in range(2 if p != 2 else 1)}
ROPED = [0, 1, 2, 3, 5, 6, 7, 8, U_AK, 11, 12, 13, 14, U_BK]
ROPE_SUMS = []
for _o in ROPED:
    ROPE_SUMS.append((ROPE_SUMS[-1] if ROPE_SUMS else 0) + (4 if _o in (U_AK, U_BK) else 1))
_cuts = [0, 4, 8, 10, 13, 16, 19, 22, 24]
SCORES_AFTER = list(zip(_cuts, _cuts[1:]))


def unit_keys(u):
    qb = u // 8 % BLK
    return (min(qb + 1, 2) if u < UNITS // 2 else qb + 1) * P


def second_plan():
    plan = Plan(width={4: IK, 5: IK})
    for p, o in enumerate(FIRST_OF):
        if PROJ[p][1] == CW:
            plan.pair(o)
        else:
            plan.chunk(1)
            plan.chunk(1, [(0, o)])
    for c in range(8):
        plan.chunk(2, [(m, U_BR + 2 * c + m) for m in range(2)])
    for p in range(4):
        plan.pair(U_OUT + 2 * p)
    for p in range(FF * FF_CHUNKS // 2):
        plan.pair(U_FF + 2 * p)
    return plan


SECOND = second_plan()
USED_FIRST = 2 * RING


def program(nc, w, out):
    ctx = ExitStack()
    with ctx:
        def sb(name, shape, dt=F32):
            return ctx.enter_context(nc.sbuf_tensor(name, shape, dt))

        def ps(name):
            return ctx.enter_context(nc.psum_tensor(name, [P, T], F32))

        def sem(name):
            return ctx.enter_context(nc.semaphore(name))

        SLOT = NT * T
        AROW, XROW = T + CONV_C - 1, T + CONV_M - 1
        SA, SB_, SC, SD = 0, SLOT, 2 * SLOT, 3 * SLOT
        SE = SD + NT * AROW
        SF = SE + NT * XROW
        SG, SH = SF + SLOT, SF + 2 * SLOT
        starts = [SA, SB_, SC, SD, SE, SF, SG, SH, SH + SLOT]
        slots_f, slots_r = [], []
        for k, (start, end) in enumerate(zip(starts, starts[1:])):
            with nc.sbuf_tensor(f"slot{k}_f", [P, end - start], F32) as slot_f:
                slots_f.append(slot_f)
            slots_r.append(sb(f"slot{k}_r", [P, end - start], F32R))
        region_f, region_r = Region(slots_f, starts), Region(slots_r, starts)

        def tile(slot, t, n=T):
            return region_f[:, slot + t * T:slot + t * T + n]

        def tile_r(slot, t):
            return region_r[:, slot + t * T:slot + (t + 1) * T]

        with nc.sbuf_tensor("ring_f", [P, RING, KC, CW], F32) as ring_f:
            pass
        ring_low = sb("ring_low", [P, RING, KC, CW], F32R)
        ring_high = sb("ring_high", [P, RING, KC, CW], F32R)
        X = sb("X", [P, NT, T])
        ident = sb("ident", [P, P])
        ones = sb("ones", [P, P])
        upper = sb("upper", [P, P])
        cols = sb("cols", [P, T])
        root = sb("root", [P, BLK * NT])
        var_cols = sb("var_cols", [P, BLK * NT])
        inv_cols = sb("inv_cols", [P, BLK * NT])
        tmp_cols = sb("tmp_cols", [P, BLK * NT])
        sqt = sb("sqt", [P, 2, T])
        va = sb("va", [P, 2, T])
        mod = sb("mod", [P, 48])
        scale = sb("scale", [P, 4 * NT])
        shift = sb("shift", [P, 2 * NT])
        cact = sb("cact", [P, NT])
        small = sb("small", [P, 64])
        zero = small[:, 0:1]
        bgate = small[0:8, 1:2]
        eps_col = small[:, 2:3]
        one_col = small[:, 3:4]
        idle = small[:, 4:5]
        a_cols = small[:, 8:24]
        em_cols = small[:, 24:40]
        rden_cols = small[:, 40:44]

        PB = [ps(f"product{i}") for i in range(4)]
        PM = [ps(f"side{i}") for i in range(4)]

        rb = PM[2][:]

        x_rows = region_f[:, SA:SA + BLK * D].rearrange("p (s d) -> p s d", s=BLK)
        c_rows = va[0:NT, 0, 0:P]

        def gate_weights(slot, n):
            return slot.rearrange("p k c -> p (k c)")[:, 0:n * 8 * HEADS].rearrange("p (a c) -> p a c", a=n)

        def gated(t, a=0, n=AROW):
            return region_f[:, SD + t * AROW + a:SD + t * AROW + a + n]

        def xm(t, a=0, n=XROW):
            return region_f[:, SE + t * XROW + a:SE + t * XROW + a + n]

        rows = region_f[:, SH:SH + T].rearrange("p (r c) -> p r c", r=4)
        ada_acc = region_f[:, SH + T:SH + 2 * T]
        ada_raw = [region_f[:, SG + b * 4 * T:SG + (b + 1) * 4 * T].rearrange("p (k c) -> p k c", k=4)
                   for b in range(2)]
        vtok = region_f[:, SA:SA + BLK * D].rearrange("p (s c) -> p s c", s=BLK)
        a_row = region_f[0:HEADS, SB_:SB_ + T]
        negM = region_f[0:HEADS, SB_ + T:SB_ + 2 * T]
        m_row = region_f[0:HEADS, SB_ + 2 * T:SB_ + 3 * T]
        one_row = region_f[0:HEADS, SB_ + 3 * T:SB_ + 4 * T]
        prob = region_f[:, SB_ + 4 * T:SB_ + 8 * T].rearrange("p (j c) -> p j c", j=BLK)
        wexp = [region_f[:, SE + b * T:SE + (b + 1) * T] for b in range(2)]
        rden = [region_f[:, SE + (2 + b) * T:SE + (3 + b) * T] for b in range(2)]
        dg = [region_f[:, SE + 6 * T + b * P:SE + 6 * T + (b + 1) * P] for b in range(4)]
        gt, gu, glf, gb = sqt[0:8, 0, :], sqt[0:HEADS, 1, :], va[0:HEADS, 0, :], va[0:HEADS, 1, :]

        C4, S4, IKD = tile(SC, 0), tile(SC, 1), tile(SC, 2)
        VT = [tile(SC, 3), tile(SC, 4)]
        score = tile(SC, 5)
        relu_s = [tile(SC, 6), tile(SC, 7)]
        OSB = [tile(SC, 5), tile(SC, 6)]
        AM = [None, tile(SH, 0), tile(SH, 1), tile(SH, 2)]
        mask_pair = tile(SH, 3, 2 * P)
        mask_before, mask_own = mask_pair[:, 0:P], mask_pair[:, P:2 * P]
        vectors_2 = region_f[:, SH + 3 * T + 2 * P:SH + 4 * T]
        index_w = vectors_2[:, 0:BLK * IH]
        stats = vectors_2[:, 32:64]
        neg_sink, sink_exp, recip, top8 = (vectors_2[:, 64 + 8 * k:72 + 8 * k] for k in range(4))
        idx_gain, idx_move = vectors_2[0:HD, 96:97], vectors_2[0:HD, 97:98]
        sink_row = vectors_2[0:1, 100:108]
        ik_raw, ik_tmp, ik_rstd, ik_c = (tile(SH, 4 + k)[0:IK if k == 0 else HD, :] for k in range(4))
        rows_2 = region_f[0:3 * NT, SH + 7 * T:SH + 7 * T + P]
        PT = [tile(SH, 4 + k) for k in range(4)]
        LG = [sqt[:, 0, :], sqt[:, 1, :], va[:, 0, :], va[:, 1, :]]
        out_rows = region_f[:, SC:SC + BLK * D].rearrange("p (s d) -> p s d", s=BLK)

        def AKD(g):
            return tile(SD, 4 + g)

        def BKD(g):
            return tile(SD, 6 + g)

        def neg_max(u):
            return stats[:, u // 8 % 2 * 8 + u % 8:u // 8 % 2 * 8 + u % 8 + 1]

        def exp_sum(u):
            return stats[:, 16 + u // 8 % 2 * 8 + u % 8:16 + u // 8 % 2 * 8 + u % 8 + 1]

        def ot_part(region, slot, wd):
            at = slot + (4 if wd < 4 else 0) * T
            return region[:, at:at + 4 * T].rearrange("p (j t) -> p j t", j=4)[:, :, wd % 4 * P:(wd % 4 + 1) * P]

        per = LAYER_CHUNKS // RING
        loaded = [Signal(sem(f"chunk_loaded{s}"), 16 * per, 16 * FF_CHUNKS // RING) for s in range(RING)]
        high_ready = Signal(sem("weight_high_ready"), LAYER_CHUNKS - len(GATE_CHUNKS), FF_CHUNKS)
        low_ready = Signal(sem("weight_low_ready"), LAYER_CHUNKS - len(GATE_CHUNKS), FF_CHUNKS)
        done = Signal(sem("product_done"), LAYER.used[-1], 2 * FF_CHUNKS)
        head_done = Signal(sem("head_product_done"), 3 * HEADS)
        taken = [Signal(sem(f"product_taken{b}"), LAYER_TILES // 4, FF_TILES // 4) for b in range(4)]
        consts = Signal(sem("constants_ready"))
        x_loaded = Signal(sem("x_loaded"))
        c_cols = Signal(sem("c_columns"))
        c_act = Signal(sem("c_activated"))
        xt_done = Signal(sem("x_transposed"))
        params_loaded = Signal(sem("params_loaded"), 16 * PARAM_DMAS)
        cols_done = Signal(sem("param_columns_done"), 1)
        ada_loaded = [Signal(sem(f"ada_loaded{b}"), 16 * ADA_UNITS, 16) for b in range(2)]
        ada_used = Signal(sem("ada_used"), ADA_UNITS, 1)
        ada_summed = Signal(sem("ada_summed"), ADA_UNITS, 1)
        ada_cols = Signal(sem("ada_columns"), ADA_UNITS, 1)
        sq_ready = Signal(sem("square_ready"), 32)
        sq_used = Signal(sem("square_used"), 32)
        r_ready = Signal(sem("rstd_ready"), 4)
        x_ready = Signal(sem("x_ready"), 16)
        hv_ready = Signal(sem("h_value_ready"), 16)
        hh_ready = Signal(sem("h_high_ready"), 16)
        hs_ready = Signal(sem("h_split_ready"), 16)
        xmh_ready = Signal(sem("xm_high_ready"), 8)
        xms_ready = Signal(sem("xm_split_ready"), 8)
        c4_ready = Signal(sem("short_conv_ready"), 8)
        xc_ready = Signal(sem("xc_ready"), 8)
        xch_ready = Signal(sem("xc_high_ready"), 8)
        xcs_ready = Signal(sem("xc_split_ready"), 8)
        gates_done = Signal(sem("gates_done"), 1)
        gates_biased = Signal(sem("gates_biased"), 1)
        fg_done = Signal(sem("forget_rows_done"), 1)
        lsig_ready = Signal(sem("softplus_ready"), 1)
        mrow_ready = Signal(sem("stabilizer_rows_ready"), 1)
        acol_done = Signal(sem("a_columns_done"), 1)
        acol_ready = Signal(sem("a_columns_ready"), 2)
        vtr_done = Signal(sem("value_transposes_done"), 8)
        v_ready = Signal(sem("values_ready"), 8)
        bc_done = Signal(sem("stabilizer_broadcast_done"), HEADS)
        dg_ready = Signal(sem("diagonal_exponent_ready"), 4 * HEADS)
        w_ready = Signal(sem("decay_weights_ready"), 4 * HEADS)
        qk_done = Signal(sem("qk_done"), 4 * HEADS)
        p_ready = Signal(sem("weighted_scores_ready"), 4 * HEADS)
        rden_ready = Signal(sem("denominator_inverse"), HEADS)
        den_spread = Signal(sem("denominator_spread"), HEADS)
        root_ready = Signal(sem("root_ready"), 4)
        r_small = Signal(sem("token_rstd_ready"), 4)
        croot_ready = Signal(sem("group_root_ready"), 1)
        crn_small = Signal(sem("group_token_rstd"), 1)
        hroot_ready = Signal(sem("head_root_ready"), 1)
        hrn_small = Signal(sem("head_token_rstd"), 1)
        hrn_ready = Signal(sem("head_rstd_spread"), 1)
        hm_mean = Signal(sem("head_mean_done"), HEADS)
        xcn_ready = Signal(sem("head_centred"), 8)
        sqn_ready = Signal(sem("head_squares"), 8)
        hm_var = Signal(sem("head_variance_done"), 8)
        hy_ready = Signal(sem("head_out_ready"), 8)
        hyh_ready = Signal(sem("head_out_high"), 8)
        hys_ready = Signal(sem("head_out_split"), 8)
        cv_ready = Signal(sem("long_conv_ready"), 8)
        cmean = Signal(sem("group_mean_done"), 8)
        cxc_ready = Signal(sem("group_centred"), 8)
        csq_ready = Signal(sem("group_squares"), 8)
        cvar = Signal(sem("group_variance_done"), 8)
        crn_ready = Signal(sem("group_rstd_ready"), 8)
        cy_ready = Signal(sem("group_normed"), 8)
        ca_ready = Signal(sem("conv_out_ready"), 8)
        cah_ready = Signal(sem("conv_out_high"), 8)
        cas_ready = Signal(sem("conv_out_split"), 8)
        relu_ready = Signal(sem("relu_ready"), 8 * FF, 8)
        fh_ready = Signal(sem("hidden_high"), 8 * FF, 8)
        fs_ready = Signal(sem("hidden_split"), 8 * FF, 8)
        y_cleared = Signal(sem("y_cleared"), 1)
        params_2 = Signal(sem("second_params_loaded"))
        rope_loaded = Signal(sem("rope_tables_loaded"))
        masks_ready = Signal(sem("masks_ready"))
        cols_2 = Signal(sem("second_columns_done"))
        swapped = Signal(sem("rope_swapped"))
        roped = Signal(sem("rope_sums"))
        iw_done = Signal(sem("index_weights_done"))
        ik_mean = Signal(sem("index_key_mean"))
        ik_centred = Signal(sem("index_key_centred"))
        ik_squared = Signal(sem("index_key_squares"))
        ik_var = Signal(sem("index_key_variance"))
        ik_rstd_ready = Signal(sem("index_key_rstd"))
        ik_normed = Signal(sem("index_key_normed"))
        ik_swapped = Signal(sem("index_key_swapped"))
        ik_ready = Signal(sem("index_key_ready"))
        vt_done = Signal(sem("token_values_done"))
        vt_ready = Signal(sem("token_values_ready"))
        score_done = Signal(sem("index_score_done"))
        score_relu = Signal(sem("index_relu_ready"))
        relu_used = Signal(sem("index_relu_used"))
        qk_2 = Signal(sem("logits_done"))
        logit_ready = Signal(sem("masked_logits_ready"))
        exp_ready = Signal(sem("exp_ready"))
        pt_done = Signal(sem("probs_transposed"))
        pv_done = Signal(sem("attention_product_done"))
        sink_diff = Signal(sem("sink_difference"))
        sink_ready = Signal(sem("sink_exp_ready"))
        ot_done = Signal(sem("output_transposed"))
        ot_high = Signal(sem("output_high"))
        mix_value = Signal(sem("mixed_value"))
        mix_high = Signal(sem("mixed_high"))
        mix_split = Signal(sem("mixed_split"))
        final_ready = Signal(sem("final_norm_ready"))
        rows_done = Signal(sem("result_rows_done"))
        pt_ready = [Signal(sem(f"transposed_probs_ready{e}")) for e in range(2)]
        out_ready = [Signal(sem(f"result_rows_ready{e}")) for e in range(2)]
        act_sem = sem("scalar_steps")
        dve_sem = sem("vector_steps")
        pool_sem = sem("gpsimd_steps")
        stored = sem("stored")
        passed = sem("waits_passed")

        def chunk_slot(i):
            return i % RING

        def wait(eng, place, signal, n):
            eng.wait_ge(signal.sem, place.value(signal, n))

        def settled(eng):
            eng.sem_inc(passed, 1)

        def wait_loaded(eng, place, i):
            wait(eng, place, loaded[chunk_slot(i)], 16 * (i // RING + 1))

        def wait_used(eng, place, plan, i):
            counted = plan.used[i + 1] if i >= 0 else 2 * (i + 1)
            wait(eng, place, done, USED_FIRST + counted)

        def wait_done(eng, place, plan, o):
            wait(eng, place, done, USED_FIRST + plan.tile[o])

        def wait_taken(eng, place, o):
            wait(eng, place, taken[o % 4], o // 4 + 2)

        def wait_bank(eng, place, o):
            wait(eng, place, taken[o % 4], o // 4 + 1)

        def bank(o):
            return PB[o % 4]

        def taken_by(instruction, o):
            instruction.then_inc(taken[o % 4].sem, 1)

        block = ctx.enter_context(nc.Block())

        @block.sync
        def _(sp):
            place = Place()

            def rows_of(ap):
                return ap.rearrange("(k p) c -> p k c", p=P)

            def load(plan, i, src, dst=None):
                wait_used(sp, place, plan, i - RING)
                settled(sp)
                slot = ring_f[:, chunk_slot(i), :, :]
                sp.dma_start(slot if dst is None else dst(slot), src).then_inc(loaded[chunk_slot(i)].sem, 16)

            def load_pair(plan, i, matrix, row, col):
                for kh in range(2):
                    load(plan, i + kh, rows_of(matrix(row + kh * KC * P, col)))

            def load_ada(layer, unit, k):
                for b in range(2):
                    wait(sp, place, (ada_used, ada_summed)[b], k + 1)
                    settled(sp)
                    src = w["w_ada"][layer, b * 4 * P:(b + 1) * 4 * P, unit_cols(unit)]
                    sp.dma_start(ada_raw[b], rows_of(src)).then_inc(ada_loaded[b].sem, 16)

            def unit_cols(unit):
                return bass.ds(unit * T, T)

            def load_group(plan, i0, first, second, g, k_ada=None):
                for p in range(4):
                    load_pair(plan, i0 + 2 * p, lambda r, c: first(r, c), 0, g * D + p * CW)
                    if k_ada is not None and p == 1:
                        load_ada(1, g, k_ada)
                for p in range(4):
                    load_pair(plan, i0 + 8 + 2 * p, lambda r, c: second(r, c), g * D, p * CW)

            sp.dma_start(x_rows, w["x"][0].rearrange("(s p) d -> p s d", p=P)).then_inc(x_loaded.sem, 16)
            sp.dma_start(c_rows, w["c"][0].rearrange("(t p) -> t p", p=P)).then_inc(x_loaded.sem, 16)
            for unit in range(ADA_FIRST):
                load_ada(0, unit, unit)

            with sp.Fori(0, LAYERS) as l:
                place = Place(l)
                vectors = [("b_ada", V_BADA), ("g_pre_mix", V_GPREM), ("g_post_mix", V_GPOSTM),
                           ("g_pre_mlp", V_GPREF), ("g_post_mlp", V_GPOSTF), ("b_conv_m", V_BCM),
                           ("g_mh", V_GMH), ("b_dw", V_BDW), ("g_cn", V_GCN), ("b_cn", V_BCN)]

                def param(dst, src):
                    sp.dma_start(dst, src).then_inc(params_loaded.sem, 16)

                wait_used(sp, place, LAYER, -RING)
                for name, at in vectors:
                    src = w[name][l].rearrange("(t p) -> t p", p=P)
                    param(rows[at:at + src.shape[0], 0, :], src)
                param(rows[0:32, 1, :], w["w_conv_m"][l].rearrange("k (t p) -> (k t) p", p=P))
                for r, k0, k1, at in ((1, 0, 12, 32), (2, 12, 28, 0), (3, 28, CONV_C, 0)):
                    param(rows[at:at + (k1 - k0) * NT, r, :],
                          w["w_dw"][l, k0:k1].rearrange("k (t p) -> (k t) p", p=P))
                param(bgate, w["b_gates"][l].rearrange("(g a) -> g a", a=1))

                def w_in(r, c):
                    return w["w_in"][l, r:r + KC * P, c:c + CW]

                for p in range(16):
                    col = (3 * D, 2 * D, 0, D)[p // 4] + p % 4 * CW
                    load_pair(LAYER, 2 * p, w_in, 0, col)
                    if p < ADA_MIXER:
                        load_ada(l, ADA_FIRST + p, ADA_FIRST + p)
                for i0, name in ((I_V, "w_v"), (I_Q, "w_q"), (I_K, "w_k")):
                    for c in range(2):
                        load(LAYER, i0 + c, w[name][l, 2 * c:2 * c + 2].rearrange("h (k p) e -> p (h k) e", p=P))
                for c, (r0, r1) in enumerate(((0, 2048), (2048, 3072))):
                    n = (r1 - r0) // T
                    load(LAYER, I_GATE + c,
                         w["w_gates"][l, r0:r1, :].rearrange("(a p h) g -> p a (h g)", p=P, h=HEADS),
                         lambda slot: gate_weights(slot, n))
                for part, row in ((I_OUT, D), (I_OUT + 8, 0)):
                    for p in range(4):
                        load_pair(LAYER, part + 2 * p, lambda r, c: w["w_out"][l, r:r + KC * P, c:c + CW], row, p * CW)
                with sp.Fori(0, FF) as g:
                    place = Place(l, g)
                    load_group(LAYER, I_FF,
                               lambda r, c: w["w_ff1"][l, r:r + KC * P, bass.ds(c, CW)],
                               lambda r, c: w["w_ff2"][l, bass.ds(r, KC * P), c:c + CW],
                               g, ADA_FIRST + ADA_MIXER)
                place = Place(l)
            place = Place(LAYERS)

            def w_in_2(n):
                def rows(r, c):
                    return w["w_in_2"][0, r:r + KC * P, c:c + n]
                return rows

            for p, (col, n) in enumerate(PROJ):
                if n == CW:
                    load_pair(SECOND, 2 * p, w_in_2(n), 0, col)
                else:
                    for kh in range(2):
                        load(SECOND, 2 * p + kh, rows_of(w_in_2(n)(kh * KC * P, col)), lambda slot: slot[:, :, 0:n])
                if p == 1:
                    for r, name in enumerate(("attn_norm_w_2", "mlp_norm_w_2", "final_norm_w_2")):
                        src = w[name][0] if r < 2 else w[name]
                        sp.dma_start(rows_2[r * NT:(r + 1) * NT, :],
                                     src.rearrange("(t p) -> t p", p=P)).then_inc(params_2.sem, 16)
                    sp.dma_start(idx_gain, w["idx_k_norm_w_2"][0].rearrange("(g a) -> g a", a=1)).then_inc(params_2.sem, 16)
                    sp.dma_start(idx_move, w["idx_k_norm_b_2"][0].rearrange("(g a) -> g a", a=1)).then_inc(params_2.sem, 16)
                    sp.dma_start(sink_row, w["sinks_2"]).then_inc(params_2.sem, 16)
                    for q in range(4):
                        sp.dma_start(C4[q * 32:(q + 1) * 32, :], w["rope_cos"][:, :]).then_inc(rope_loaded.sem, 16)
                        sp.dma_start(S4[q * 32:(q + 1) * 32, :], w["rope_sin"][:, :]).then_inc(rope_loaded.sem, 16)
            for p in range(4):
                for b, name in enumerate(("w_branch_a_2", "w_branch_b_2")):
                    load(SECOND, J_BRANCH + 2 * p + b, rows_of(w[name][0, :, p * CW:(p + 1) * CW]))
            for p in range(4):
                load_pair(SECOND, J_OUT + 2 * p, lambda r, c: w["w_out_2"][0, r:r + KC * P, c:c + CW], 0, p * CW)
            with sp.Fori(0, FF) as g:
                place = Place(LAYERS, g)
                load_group(SECOND, J_FF,
                           lambda r, c: w["w_up_2"][0, r:r + KC * P, bass.ds(c, CW)],
                           lambda r, c: w["w_down_2"][0, bass.ds(r, KC * P), c:c + CW], g)
            for half in range(2):
                for e in range(2):
                    sp.wait_ge(out_ready[e].sem, 2 * (half + 1))
                sp.dma_start(out[0, :, half * T:(half + 1) * T].rearrange("(s p) d -> p s d", p=P),
                             out_rows[:, :, half * T:(half + 1) * T]).then_inc(stored, 16)
            sp.wait_ge(stored, 32)

        @block.gpsimd
        def _(pool):
            pool.memset(ones[:], 1.0).then_inc(pool_sem, 1)
            pool.memset(ident[:], 0.0).then_inc(pool_sem, 1)
            pool.memset(upper[:], 0.0).then_inc(pool_sem, 1)
            pool.memset(small[:], 0.0).then_inc(pool_sem, 1)
            pool.wait_ge(pool_sem, 4)
            pool.memset(eps_col, EPS).then_inc(pool_sem, 1)
            pool.memset(one_col, 1.0).then_inc(pool_sem, 1)
            pool.affine_select(out=ident[:], in_=ident[:], compare_op=ALU.not_equal, fill=1.0, base=0,
                               pattern=[[-1, P]], channel_multiplier=1).then_inc(pool_sem, 1)
            pool.affine_select(out=upper[:], in_=upper[:], compare_op=ALU.is_ge, fill=NEG, base=0,
                               pattern=[[1, P]], channel_multiplier=-1).then_inc(pool_sem, 1)
            pool.wait_ge(pool_sem, 8)
            pool.sem_inc(consts.sem, 1)
            pool.sem_inc(done.sem, USED_FIRST)
            pool.sem_inc(ada_used.sem, 1)
            pool.sem_inc(ada_summed.sem, 1)
            for b in range(4):
                pool.sem_inc(taken[b].sem, 1)

            def low_part(place, plan, i):
                if i in plan.plain:
                    return
                n = plan.width.get(i, CW)
                s = chunk_slot(i)
                wait(pool, place, high_ready, plan.split(i))
                pool.tensor_tensor(ring_low[:, s, :, 0:n], ring_f[:, s, :, 0:n], ring_high[:, s, :, 0:n].bitcast(F32),
                                   ALU.subtract).then_inc(low_ready.sem, 1)

            with pool.Fori(0, LAYERS) as l:
                for i in range(I_FF):
                    low_part(Place(l), LAYER, i)
                with pool.Fori(0, FF) as g:
                    for i in range(I_FF, I_FF + FF_CHUNKS):
                        low_part(Place(l, g), LAYER, i)
            place = Place(LAYERS)
            low_part(place, SECOND, 0)
            pool.memset(mask_pair, 0.0).then_inc(pool_sem, 1)
            pool.wait_ge(pool_sem, 9)
            pool.affine_select(out=mask_own, in_=mask_own, compare_op=ALU.is_ge, fill=NEG, base=0,
                               pattern=[[-1, P]], channel_multiplier=1).then_inc(masks_ready.sem, 1)
            pool.affine_select(out=mask_before, in_=mask_before, compare_op=ALU.is_ge, fill=NEG, base=-1,
                               pattern=[[1, P]], channel_multiplier=-1).then_inc(masks_ready.sem, 1)
            for i in range(1, J_FF):
                low_part(place, SECOND, i)
            with pool.Fori(0, FF) as g:
                for i in range(J_FF, J_FF + FF_CHUNKS):
                    low_part(Place(LAYERS, g), SECOND, i)

        @block.scalar
        def _(act):
            steps = Steps(act, act_sem)

            def high_part(place, plan, i):
                if i in plan.plain:
                    return
                n = plan.width.get(i, CW)
                s = chunk_slot(i)
                wait_loaded(act, place, i)
                act.activation(ring_high[:, s, :, 0:n], ring_f[:, s, :, 0:n], ACT.Copy).then_inc(high_ready.sem, 1)

            class Ahead:

                def __init__(self, plan, made):
                    self.plan, self.made = plan, made

                def of(self, place, i, last=None):
                    upto = i + AHEAD + 1
                    if last is not None:
                        upto = min(upto, last)
                    while self.made < upto:
                        high_part(place, self.plan, self.made)
                        self.made += 1

            def square_root_next():
                steps.did(act.activation(idle, zero, ACT.Sqrt))
                steps.wait()

            def deviation(place, sums, n, signal):
                act.activation(root[:, 0:sums.shape[1]], sums, ACT.Sqrt, bias=eps_col,
                               scale=1.0 / n).then_inc(signal.sem, 1)

            def norm_stats(place, m, src, ready):
                for t in range(NT):
                    ready(t)
                    if m or t >= 2:
                        wait(act, place, sq_used, 8 * m + t - 1)
                    act.activation(sqt[:, t % 2, :], src(t), ACT.Square).then_inc(sq_ready.sem, 1)
                square_root_next()
                wait(act, place, sq_used, 8 * m + NT)
                deviation(place, PM[3][:, 0:BLK], D, root_ready)

            def split_high(place, n, dst=None):
                for t in range(NT):
                    wait(act, place, hv_ready, 8 * n + t + 1)
                    act.activation(tile_r(SA, t), va[:, t % 2, :], ACT.Copy).then_inc(hh_ready.sem, 1)

            def mlp_group(place, plan, ahead, i0, o0, group, last=None):
                for t in range(NT):
                    ahead.of(place, i0 + t, last)
                    wait_done(act, place, plan, o0 + t)
                    if t >= 2:
                        wait_taken(act, place, o0 + t - 2)
                    act.activation(sqt[:, t % 2, :], bank(o0 + t)[:], ACT.Relu).then_inc(relu_ready.sem, 1)
                    if t:
                        hidden_high(place, o0, t - 1)
                hidden_high(place, o0, NT - 1)
                ahead.of(place, i0 + FF_CHUNKS - 1, last)

            def hidden_high(place, o0, t):
                wait_taken(act, place, o0 + t)
                act.activation(tile_r(SC, t), va[:, t % 2, :], ACT.Copy).then_inc(fh_ready.sem, 1)

            def conv_high(place, t):
                wait(act, place, ca_ready, t + 1)
                act.activation(tile_r(SD, t), tile(SC, t), ACT.Copy).then_inc(cah_ready.sem, 1)

            act.wait_ge(consts.sem, 1)
            act.wait_ge(c_cols.sem, 1)
            act.activation(cact[:], PM[0][:, 0:NT], ACT.Silu).then_inc(c_act.sem, 1)
            for i in range(AHEAD):
                high_part(Place(), LAYER, i)

            with act.Fori(0, LAYERS) as l:
                place = Place(l)
                steps.enter(l, ACT_LAYER)
                ahead = Ahead(LAYER, AHEAD)
                norm_stats(place, 0, lambda t: X[:, t, :], lambda t: wait(act, place, x_ready, t + 1))
                split_high(place, 0)
                for t in range(NT):
                    ahead.of(place, t)
                    wait_done(act, place, LAYER, O_GLUB + t)
                    act.activation(tile(SC, t), bank(t)[:], ACT.Sigmoid).then_inc(taken[t % 4].sem, 1)
                for t in range(NT):
                    ahead.of(place, 16 + t)
                    wait_done(act, place, LAYER, O_XM + t)
                    act.activation(xm(t, CONV_M - 1, T), bank(t)[:], ACT.Copy).then_inc(taken[t % 4].sem, 1)
                for t in range(NT):
                    ahead.of(place, 24 + t)
                    wait_done(act, place, LAYER, O_Z + t)
                    act.activation(tile(SH, t), bank(t)[:], ACT.Sigmoid).then_inc(taken[t % 4].sem, 1)
                for t in range(NT):
                    act.activation(tile_r(SA, t), xm(t, CONV_M - 1, T), ACT.Copy).then_inc(xmh_ready.sem, 1)
                ahead.of(place, 33)
                for t in range(NT):
                    wait(act, place, c4_ready, t + 1)
                    act.activation(tile(SF, t), tile(SF, t), ACT.Silu,
                                   bias=cols[:, V_BCM + t:V_BCM + t + 1]).then_inc(xc_ready.sem, 1)
                for t in range(NT):
                    wait_done(act, place, LAYER, O_V + t)
                    wait(act, place, xms_ready, t + 1)
                    act.activation(xm(t, CONV_M - 1, T), bank(t)[:], ACT.Copy).then_inc(taken[t % 4].sem, 1)
                for t in range(NT):
                    wait(act, place, xc_ready, t + 1)
                    act.activation(tile_r(SA, t), tile(SF, t), ACT.Copy).then_inc(xch_ready.sem, 1)
                for t in range(NT):
                    ahead.of(place, I_Q + t // 4)
                    wait_done(act, place, LAYER, O_Q + t)
                    act.activation(tile(SG, t), bank(t)[:], ACT.Copy).then_inc(taken[t % 4].sem, 1)
                wait(act, place, xcs_ready, NT)
                for t in range(NT):
                    ahead.of(place, I_K + t // 4)
                    wait_done(act, place, LAYER, O_K + t)
                    act.activation(tile(SF, t), bank(t)[:], ACT.Copy).then_inc(taken[t % 4].sem, 1)
                wait(act, place, fg_done, 1)
                steps.did(act.activation(gu, PM[1][0:HEADS, :], ACT.Abs))
                steps.wait()
                steps.did(act.activation(gu, gu, ACT.Exp, scale=-1.0))
                steps.wait()
                act.activation(gu, gu, ACT.Ln, bias=one_col[0:HEADS]).then_inc(lsig_ready.sem, 1)
                for j in range(8):
                    wait(act, place, vtr_done, j + 1)
                    act.activation(vtok[:, j // 2, j % 2 * T:(j % 2 + 1) * T], PM[2 + j % 2][:],
                                   ACT.Copy).then_inc(v_ready.sem, 1)
                wait(act, place, acol_done, 1)
                act.activation(a_cols, PM[1][:, 0:BLK * HEADS], ACT.Copy).then_inc(acol_ready.sem, 1)
                act.activation(em_cols, PM[1][:, BLK * HEADS:2 * BLK * HEADS], ACT.Exp, scale=-1.0).then_inc(acol_ready.sem, 1)
                ahead.of(place, I_OUT - 1)

                def decay(h, j):
                    u = 4 * h + j
                    a_col = a_cols[:, j * HEADS + h:j * HEADS + h + 1]
                    if u >= 2:
                        wait(act, place, p_ready, u - 1)
                    if j == 0:
                        wait(act, place, dg_ready, 4 * h + BLK)
                    if j < BLK - 1:
                        steps.did(act.activation(wexp[u % 2][:, P:T - j * P], PM[0][:, (j + 1) * P:T],
                                                 ACT.Exp, bias=a_col))
                        steps.wait()
                    act.activation(wexp[u % 2][:, 0:P], dg[j], ACT.Exp).then_inc(w_ready.sem, 1)

                wait(act, place, acol_ready, 2)
                decay(0, 0)
                decay(0, 1)
                for h in range(HEADS):
                    decay(h, 2)
                    decay(h, 3)
                    if h < HEADS - 1:
                        decay(h + 1, 0)
                        decay(h + 1, 1)
                    wait(act, place, den_spread, h + 1)
                    if h >= 2:
                        wait_taken(act, place, O_HEAD + 4 * h - 8)
                        wait_taken(act, place, O_HEAD + 4 * h - 7)
                    o = O_HEAD + 4 * h + 3
                    act.activation(rden[h % 2], bank(o)[:], ACT.Copy).then_inc(taken[o % 4].sem, 1)
                for t in range(NT):
                    wait(act, place, cxc_ready, t + 1)
                    if t >= 2:
                        wait(act, place, cvar, t - 1)
                    act.activation(sqt[:, t % 2, :], tile(SC, t), ACT.Square).then_inc(csq_ready.sem, 1)
                square_root_next()
                wait(act, place, cvar, NT)
                deviation(place, PM[3][:, 0:BLK * NT], P, croot_ready)
                for t in range(NT):
                    wait(act, place, xcn_ready, t + 1)
                    if t >= 2:
                        wait(act, place, hm_var, t - 1)
                    act.activation(sqt[:, t % 2, :], tile(SF, t), ACT.Square).then_inc(sqn_ready.sem, 1)
                wait(act, place, hm_var, NT)
                wait(act, place, crn_small, 1)
                deviation(place, PM[2][:, 0:BLK * HEADS], 2 * P, hroot_ready)
                for t in range(NT):
                    wait(act, place, cy_ready, t + 1)
                    act.activation(tile(SC, t), tile(SC, t), ACT.Silu, scale=cols[:, V_GCN + t:V_GCN + t + 1],
                                   bias=cols[:, V_BCN + t:V_BCN + t + 1]).then_inc(ca_ready.sem, 1)
                    if t:
                        conv_high(place, t - 1)
                conv_high(place, NT - 1)
                for t in range(NT):
                    wait(act, place, hy_ready, t + 1)
                    act.activation(tile_r(SG, t), va[:, t % 2, :], ACT.Copy).then_inc(hyh_ready.sem, 1)
                for t in range(NT):
                    ahead.of(place, I_OUT + t)
                    wait_done(act, place, LAYER, O_OUTA + t)
                    act.activation(tile(SE, t), bank(t)[:], ACT.Copy).then_inc(taken[t % 4].sem, 1)
                ahead.of(place, I_OUT + 15)
                norm_stats(place, 1, lambda t: tile(SE, t), lambda t: wait_taken(act, place, O_OUTH + t))
                norm_stats(place, 2, lambda t: X[:, t, :], lambda t: wait(act, place, x_ready, 8 + t + 1))
                split_high(place, 1)
                with act.Fori(0, FF) as g:
                    steps.enter(g, 0)
                    mlp_group(Place(l, g), LAYER, Ahead(LAYER, I_FF + AHEAD), I_FF, O_FF, g)
                    steps.leave(FF)
                last = O_FF + (FF - 1) * FF_TILES + 8
                norm_stats(place, 3, lambda t: tile(SE, t), lambda t: wait_taken(act, place, last + t))
                steps.leave(LAYERS)
            place = Place(LAYERS)
            ahead = Ahead(SECOND, AHEAD)
            norm_stats(place, 0, lambda t: X[:, t, :], lambda t: wait(act, place, x_ready, t + 1))
            split_high(place, 0)

            def swap(src, dst, signal, quadrants=4):
                for q in range(quadrants):
                    p0, p1 = q * 32, (q ^ 1) * 32
                    act.activation(dst[p0:p0 + 32, :], src[p1:p1 + 32, :], ACT.Copy).then_inc(signal.sem, 1)

            def rope(r):
                o = ROPED[r]
                ahead.of(place, 2 * PAIR_OF[o])
                wait_done(act, place, SECOND, o)
                if r >= 2:
                    act.wait_ge(roped.sem, ROPE_SUMS[r - 2])
                swap(bank(o), sqt[:, r % 2, :], swapped)

            for r in range(4):
                rope(r)
            wait_done(act, place, SECOND, U_IK)
            act.activation(ik_raw, bank(U_IK)[0:IK, :], ACT.Copy).then_inc(taken[U_IK % 4].sem, 1)
            rope(4)
            rope(5)
            act.wait_ge(ik_centred.sem, 1)
            act.activation(ik_tmp, ik_c, ACT.Square).then_inc(ik_squared.sem, 1)
            rope(6)
            rope(7)
            act.wait_ge(ik_var.sem, 1)
            steps.did(act.activation(ik_rstd, PM[2][0:HD, :], ACT.Ln, bias=eps_col[0:HD], scale=1.0 / HD))
            steps.wait()
            act.activation(ik_rstd, ik_rstd, ACT.Exp, scale=-0.5).then_inc(ik_rstd_ready.sem, 1)
            act.wait_ge(ik_normed.sem, 1)
            swap(ik_c, ik_tmp, ik_swapped, 2)
            rope(8)

            def token_values(k, o):
                ahead.of(place, 2 * PAIR_OF[o])
                wait_done(act, place, SECOND, o)
                act.activation(relu_s[k], bank(o)[:], ACT.Copy).then_inc(taken[o % 4].sem, 1)

            def values_out(k):
                act.wait_ge(vt_done.sem, k + 1)
                act.activation(VT[k], PM[3][:], ACT.Copy).then_inc(vt_ready.sem, 1)

            token_values(0, U_AV)
            rope(9)
            rope(10)
            values_out(0)
            rope(11)
            rope(12)
            rope(13)
            token_values(1, U_BV)
            u = 0
            for t in range(2 * NT):
                o = U_GA + t
                ahead.of(place, 2 * PAIR_OF[o])
                wait_done(act, place, SECOND, o)
                act.activation(tile(SF, t), bank(o)[:], ACT.Sigmoid).then_inc(taken[o % 4].sem, 1)
                if t == 1:
                    values_out(1)
                if t % 2:
                    for u in range(*SCORES_AFTER[t // 2]):
                        n = (u // 8 + 2) * P
                        act.wait_ge(score_done.sem, u + 1)
                        if u >= 2:
                            act.wait_ge(relu_used.sem, u - 1)
                        else:
                            act.wait_ge(vt_ready.sem, 2)
                        act.activation(relu_s[u % 2][:, 0:n], PM[u % 2][:, 0:n], ACT.Relu).then_inc(score_relu.sem, 1)
            ahead.of(place, J_BRANCH - 1)

            def scores_out(u):
                n = unit_keys(u)
                act.wait_ge(pt_done.sem, u + 1)
                if u >= 4:
                    act.wait_ge(pv_done.sem, u - 3)
                act.activation(PT[u % 4][:, 0:n], PM[2 + u % 2][:, 0:n], ACT.Copy).then_inc(pt_ready[0].sem, 1)

            def out_high(wd):
                act.wait_ge(ot_done.sem, wd + 1)
                o = U_ATT + 2 * wd + 1
                act.activation(ot_part(region_r, SA, wd), bank(o)[:].rearrange("p (j q) -> p j q", j=4),
                               ACT.Copy).then_inc(ot_high.sem, 1)

            for u in range(UNITS + 3):
                wd, h = u // 8, u % 8
                if u < UNITS:
                    n = unit_keys(u)
                    act.wait_ge(logit_ready.sem, u + 1)
                    act.activation(LG[u % 4][:, 0:n], LG[u % 4][:, 0:n], ACT.Exp, bias=neg_max(u), scale=-1.0,
                                   accum_out=exp_sum(u)).then_inc(exp_ready.sem, 1)
                if u % 2 == 1 and u - 1 < UNITS:
                    scores_out(u - 1)
                if u < UNITS and h == 7 and wd < 4:
                    act.wait_ge(sink_diff.sem, wd + 1)
                    act.activation(sink_exp, sink_exp, ACT.Exp).then_inc(sink_ready.sem, 1)
                if h == 5 and wd:
                    out_high(wd - 1)
            out_high(7)
            for t in range(NT):
                o = U_BR + 4 * (t // 2) + t % 2
                ahead.of(place, J_BRANCH + t // 2 * 2 + 1)
                act.wait_ge(mix_value.sem, t + 1)
                act.activation(tile_r(SC, t), va[:, t % 2, :], ACT.Copy).then_inc(mix_high.sem, 1)
            ahead.of(place, J_FF - 1)
            norm_stats(place, 1, lambda t: X[:, t, :], lambda t: wait_taken(act, place, U_OUT + t))
            split_high(place, 1)
            with act.Fori(0, FF - 1) as g:
                steps.enter(g, 0)
                mlp_group(Place(LAYERS, g), SECOND, Ahead(SECOND, J_FF + AHEAD), J_FF, U_FF, g)
                steps.leave(FF - 1)
            mlp_group(Place(LAYERS, FF - 1), SECOND, Ahead(SECOND, J_FF + AHEAD), J_FF, U_FF, FF - 1, J_FF + FF_CHUNKS)
            last = U_FF + (FF - 1) * FF_TILES + NT
            norm_stats(place, 2, lambda t: X[:, t, :], lambda t: wait_taken(act, place, last + t))
            for t in range(0, NT, 2):
                act.wait_ge(rows_done.sem, t + 1)
                o = U_LAST + t
                act.activation(out_rows[:, :, t * P:(t + 1) * P], bank(o)[:].rearrange("p (s c) -> p s c", s=BLK),
                               ACT.Copy).then_inc(out_ready[0].sem, 1)

        @block.vector
        def _(dve):
            steps = Steps(dve, dve_sem)

            def ada_unit(place, k, dst):
                for b in range(2):
                    wait(dve, place, ada_loaded[b], 16 * (k + 1))
                    for kk in range(4):
                        c_col = cact[:, 4 * b + kk:4 * b + kk + 1]
                        if b + kk:
                            if kk:
                                steps.wait()
                            else:
                                wait(dve, place, ada_used, k + 2)
                            ins = dve.scalar_tensor_tensor(ada_acc, ada_raw[b][:, kk, :], c_col, ada_acc,
                                                           ALU.mult, ALU.add)
                        else:
                            ins = dve.tensor_scalar(ada_acc, ada_raw[b][:, kk, :], c_col, None, ALU.mult)
                        if kk < 3:
                            steps.did(ins)
                        elif b == 0:
                            ins.then_inc(ada_used.sem, 1)
                        else:
                            ins.then_inc(ada_summed.sem, 1)
                wait(dve, place, ada_cols, k + 1)
                settled(dve)
                steps.did(dve.tensor_copy(dst, PM[1][:, 0:4]))

            def refine(sums, n, count, signal):
                r, v, y, q = (a[:, 0:count] for a in (root, var_cols, inv_cols, tmp_cols))
                steps.did(dve.tensor_scalar(v, sums[:, 0:count], 1.0 / n, EPS, ALU.mult, ALU.add))
                steps.did(dve.reciprocal(y, r))
                steps.wait()
                steps.did(dve.tensor_tensor(q, y, y, ALU.mult))
                steps.wait()
                steps.did(dve.tensor_tensor(q, q, v, ALU.mult))
                steps.wait()
                steps.did(dve.tensor_scalar(q, q, -0.5, 1.5, ALU.mult, ALU.add))
                steps.wait()
                dve.tensor_tensor(y, y, q, ALU.mult).then_inc(signal.sem, 1)

            def token_rstd(place, m):
                wait(dve, place, root_ready, m + 1)
                settled(dve)
                refine(PM[3], D, BLK, r_small)
                wait(dve, place, r_ready, m + 1)

            def normalise(place, m, n, gain, move):
                token_rstd(place, m)

                def value(t):
                    v = va[:, t % 2, :]
                    steps.did(dve.tensor_tensor(v, X[:, t, :], rb, ALU.mult))
                    steps.wait()
                    dve.tensor_scalar(v, v, gain(t), move(t), ALU.mult, ALU.add).then_inc(hv_ready.sem, 1)

                def low(t):
                    wait(dve, place, hh_ready, 8 * n + t + 1)
                    dve.tensor_tensor(tile_r(SB_, t), va[:, t % 2, :], tile_r(SA, t).bitcast(F32),
                                      ALU.subtract).then_inc(hs_ready.sem, 1)

                value(0)
                for t in range(NT):
                    if t + 1 < NT:
                        if t:
                            wait(dve, place, hs_ready, 8 * n + t)
                        value(t + 1)
                    low(t)

            def residual(place, m, gain):
                token_rstd(place, m)
                for t in range(0, NT, 2):
                    for u in (t, t + 1):
                        steps.did(dve.tensor_tensor(tile(SE, u), tile(SE, u), rb, ALU.mult))
                    for u in (t, t + 1):
                        steps.wait(steps.n - 1 + u - t)
                        dve.scalar_tensor_tensor(X[:, u, :], tile(SE, u), gain(u), X[:, u, :],
                                                 ALU.mult, ALU.add).then_inc(x_ready.sem, 1)

            def mlp_group(place, plan, o0, k0, between=None, dst=lambda t: tile(SE, t)):
                def low(t):
                    wait(dve, place, fh_ready, k0 + t + 1)
                    dve.tensor_tensor(tile_r(SD, t), va[:, t % 2, :], tile_r(SC, t).bitcast(F32),
                                      ALU.subtract).then_inc(fs_ready.sem, 1)

                for t in range(NT):
                    wait(dve, place, relu_ready, k0 + t + 1)
                    if t >= 2:
                        wait(dve, place, fs_ready, k0 + t - 1)
                    dve.scalar_tensor_tensor(va[:, t % 2, :], bank(o0 + t)[:], 0.0, sqt[:, t % 2, :],
                                             ALU.max, ALU.mult).then_inc(taken[(o0 + t) % 4].sem, 1)
                    if t:
                        low(t - 1)
                low(NT - 1)
                if between is not None:
                    between()
                for t in range(NT):
                    o = o0 + NT + t
                    wait_done(dve, place, plan, o)
                    dve.tensor_tensor(dst(t), bank(o)[:], dst(t), ALU.add).then_inc(taken[o % 4].sem, 1)

            def clear_y(place):
                steps.did(dve.memset(region_f[:, SE:SE + SLOT], 0.0))

            def conv_pair(place, t0, taps, weight, src, dst, bias, signal):
                for k in range(taps):
                    for t in (t0, t0 + 1):
                        wk = cols[:, weight + k * NT + t:weight + k * NT + t + 1]
                        if k == 0:
                            ins = dve.tensor_scalar(tile(dst, t), src(t, k, T), wk, bias(t), ALU.mult, ALU.add)
                        else:
                            steps.wait(steps.n - 1 if k < taps - 1 or t == t0 else steps.n)
                            ins = dve.scalar_tensor_tensor(tile(dst, t), src(t, k, T), wk, tile(dst, t),
                                                           ALU.mult, ALU.add)
                        if k < taps - 1:
                            steps.did(ins)
                        else:
                            ins.then_inc(signal.sem, 1)

            def long_conv(place, t0):
                conv_pair(place, t0, CONV_C, V_WDW, gated, SC, lambda t: cols[:, V_BDW + t:V_BDW + t + 1], cv_ready)

            dve.wait_ge(consts.sem, 1)
            for t in range(NT):
                wait(dve, Place(), xt_done, t + 1)
                dve.tensor_copy(X[:, t, :], PB[t % 4][:]).then_inc(x_ready.sem, 1)
            dve.wait_ge(c_act.sem, 1)
            for k in range(ADA_FIRST):
                ada_unit(Place(), k, mod[:, 4 * k:4 * k + 4])

            with dve.Fori(0, LAYERS) as l:
                place = Place(l)
                steps.enter(l, DVE_LAYER)
                wait(dve, place, cols_done, 1)
                steps.did(dve.tensor_copy(cols[:, 0:V_BCN + NT], PM[0][:, 0:V_BCN + NT]))
                steps.did(dve.tensor_copy(cols[:, V_WCM:V_WDW + CONV_C * NT], PM[0][:, V_WCM:V_WDW + CONV_C * NT]))
                steps.wait()
                steps.did(dve.tensor_tensor(mod[:, 0:16], mod[:, 0:16], cols[:, V_BADA:V_BADA + 16], ALU.add))
                steps.wait()
                steps.did(dve.scalar_tensor_tensor(scale[:, 0:NT], mod[:, 8:16], 1.0, cols[:, V_GPREM:V_GPREM + NT],
                                                   ALU.add, ALU.mult))
                steps.did(dve.tensor_copy(shift[:, 0:NT], mod[:, 0:NT]))
                steps.wait()
                normalise(place, 0, 0, lambda t: scale[:, t:t + 1], lambda t: shift[:, t:t + 1])
                steps.did(dve.memset(region_f[:, SD:SE].rearrange("p (t c) -> p t c", t=NT)[:, :, 0:CONV_C - 1], 0.0))
                steps.did(dve.memset(region_f[:, SE:SF].rearrange("p (t c) -> p t c", t=NT)[:, :, 0:CONV_M - 1], 0.0))
                for p in range(ADA_MIXER):
                    k = ADA_FIRST + p
                    ada_unit(place, k, mod[:, 4 * k:4 * k + 4])
                    if p >= 4:
                        for t in (2 * (p - 4), 2 * (p - 4) + 1):
                            wait_taken(dve, place, O_GLUB + t)
                            wait_done(dve, place, LAYER, O_GLUA + t)
                            dve.tensor_tensor(gated(t, CONV_C - 1, T), bank(t)[:], tile(SC, t),
                                              ALU.mult).then_inc(taken[t % 4].sem, 1)
                steps.wait()
                steps.did(dve.tensor_tensor(mod[:, 16:48], mod[:, 16:48], cols[:, V_BADA + 16:V_BADA + 48], ALU.add))
                steps.wait()
                for dst, m, g in ((1, 2, V_GPOSTM), (3, 5, V_GPOSTF)):
                    steps.did(dve.tensor_tensor(scale[:, dst * NT:(dst + 1) * NT], mod[:, m * NT:(m + 1) * NT],
                                                cols[:, g:g + NT], ALU.mult))
                steps.did(dve.scalar_tensor_tensor(scale[:, 2 * NT:3 * NT], mod[:, 4 * NT:5 * NT], 1.0,
                                                   cols[:, V_GPREF:V_GPREF + NT], ALU.add, ALU.mult))
                steps.did(dve.tensor_copy(shift[:, NT:2 * NT], mod[:, 3 * NT:4 * NT]))
                wait_taken(dve, place, O_GLUA + 6)
                wait_taken(dve, place, O_GLUA + 7)
                long_conv(place, 0)
                for t in range(0, NT, 2):
                    for u in (t, t + 1):
                        wait_taken(dve, place, O_XM + u)
                    conv_pair(place, t, CONV_M, V_WCM, xm, SF, lambda u: zero, c4_ready)
                for t in range(NT):
                    wait(dve, place, xmh_ready, t + 1)
                    dve.tensor_tensor(tile_r(SB_, t), xm(t, CONV_M - 1, T), tile_r(SA, t).bitcast(F32),
                                      ALU.subtract).then_inc(xms_ready.sem, 1)
                long_conv(place, 2)
                for t in range(NT):
                    wait(dve, place, xch_ready, t + 1)
                    dve.tensor_tensor(tile_r(SB_, t), tile(SF, t), tile_r(SA, t).bitcast(F32),
                                      ALU.subtract).then_inc(xcs_ready.sem, 1)
                long_conv(place, 4)
                wait(dve, place, gates_done, 1)
                dve.tensor_scalar(gt, PM[0][0:8, :], bgate, None, ALU.add).then_inc(gates_biased.sem, 1)
                steps.did(dve.memset(one_row, 1.0))
                wait(dve, place, lsig_ready, 1)
                steps.did(dve.scalar_tensor_tensor(glf, PM[1][0:HEADS, :], 0.0, gu, ALU.min, ALU.subtract))
                steps.wait()
                steps.did(dve.tensor_tensor_scan(gb, one_row, glf, 0.0, ALU.mult, ALU.add))
                steps.wait()
                wait(dve, place, gates_biased, 1)
                steps.did(dve.tensor_tensor(a_row, gt[0:HEADS], gb, ALU.subtract))
                steps.wait()
                steps.did(dve.tensor_tensor_scan(negM, a_row, a_row, 0.0, ALU.max, ALU.max))
                steps.wait()
                steps.did(dve.tensor_tensor(m_row, gb, negM, ALU.add))
                steps.wait()
                dve.tensor_scalar(negM, negM, -1.0, None, ALU.mult).then_inc(mrow_ready.sem, 1)
                long_conv(place, 6)

                def diagonal(h):
                    wait(dve, place, bc_done, h + 1)
                    for j in range(BLK):
                        a_col = a_cols[:, j * HEADS + h:j * HEADS + h + 1]
                        dve.scalar_tensor_tensor(dg[j], PM[0][:, j * P:(j + 1) * P], a_col, upper[:],
                                                 ALU.add, ALU.add).then_inc(dg_ready.sem, 1)

                wait(dve, place, acol_ready, 2)
                diagonal(0)
                for h in range(HEADS):
                    for j in range(BLK):
                        u = 4 * h + j
                        wait(dve, place, w_ready, u + 1)
                        wait(dve, place, qk_done, u + 1)
                        if h and j == 0:
                            wait(dve, place, head_done, 3 * h)
                        dve.scalar_tensor_tensor(prob[:, j, j * P:T], PM[2 + j % 2][:, 0:T - j * P], 1.0 / 16,
                                                 wexp[u % 2][:, 0:T - j * P], ALU.mult,
                                                 ALU.mult).then_inc(p_ready.sem, 1)
                    for t in (2 * h, 2 * h + 1):
                        wait(dve, place, cmean, t + 1)
                        dve.scalar_tensor_tensor(tile(SC, t), PM[1][:], -1.0 / P, tile(SC, t), ALU.mult,
                                                 ALU.add).then_inc(cxc_ready.sem, 1)
                    o = O_HEAD + 4 * h
                    wait(dve, place, head_done, 3 * h + 3)
                    den = tmp_cols[:, 0:BLK]
                    steps.did(dve.scalar_tensor_tensor(den, bank(o + 2)[:, 0:BLK], -1.0,
                                                       em_cols.rearrange("p (s h) -> p s h", h=HEADS)[:, :, h],
                                                       ALU.mult, ALU.max))
                    steps.wait()
                    dve.tensor_tensor(den, bank(o + 2)[:, 0:BLK], den, ALU.max).then_inc(taken[(o + 2) % 4].sem, 1)
                    wait_taken(dve, place, o + 2)
                    if h:
                        wait(dve, place, den_spread, h)
                    dve.reciprocal(rden_cols, den).then_inc(rden_ready.sem, 1)
                    if h < HEADS - 1:
                        diagonal(h + 1)
                    wait_taken(dve, place, o + 3)
                    for e in range(2):
                        t = 2 * h + e
                        dve.tensor_tensor(tile(SF, t), bank(o + e)[:], rden[h % 2], ALU.mult).then_inc(
                            taken[(o + e) % 4].sem, 1)
                for t in range(NT):
                    wait(dve, place, hm_mean, t // 2 + 1)
                    wait_taken(dve, place, O_HEAD + 4 * (t // 2) + t % 2)
                    dve.scalar_tensor_tensor(tile(SF, t), PM[t // 2 % 2][:], -1.0 / (2 * P), tile(SF, t), ALU.mult,
                                             ALU.add).then_inc(xcn_ready.sem, 1)
                wait(dve, place, croot_ready, 1)
                settled(dve)
                refine(PM[3], P, BLK * NT, crn_small)
                for t in range(NT):
                    wait(dve, place, crn_ready, t + 1)
                    wait(dve, place, cxc_ready, t + 1)
                    dve.tensor_tensor(tile(SC, t), tile(SC, t), PM[t % 2][:], ALU.mult).then_inc(cy_ready.sem, 1)
                wait(dve, place, hroot_ready, 1)
                settled(dve)
                refine(PM[2], 2 * P, BLK * HEADS, hrn_small)
                for t in range(NT):
                    wait(dve, place, cah_ready, t + 1)
                    dve.tensor_tensor(region_r[:, SC + t * T:SC + (t + 1) * T], tile(SC, t),
                                      tile_r(SD, t).bitcast(F32), ALU.subtract).then_inc(cas_ready.sem, 1)
                wait(dve, place, hrn_ready, 1)

                def head_low(t):
                    wait(dve, place, hyh_ready, t + 1)
                    dve.tensor_tensor(tile_r(SF, t), va[:, t % 2, :], tile_r(SG, t).bitcast(F32),
                                      ALU.subtract).then_inc(hys_ready.sem, 1)

                for t in range(NT):
                    if t >= 2:
                        wait(dve, place, hys_ready, t - 1)
                    steps.did(dve.tensor_tensor(va[:, t % 2, :], tile(SF, t), PM[t // 2][:], ALU.mult))
                    steps.wait()
                    dve.scalar_tensor_tensor(va[:, t % 2, :], va[:, t % 2, :], cols[:, V_GMH + t:V_GMH + t + 1],
                                             tile(SH, t), ALU.mult, ALU.mult).then_inc(hy_ready.sem, 1)
                    if t:
                        head_low(t - 1)
                head_low(NT - 1)
                for t in range(NT):
                    wait_taken(dve, place, O_OUTA + t)
                    wait_done(dve, place, LAYER, O_OUTH + t)
                    dve.tensor_tensor(tile(SE, t), bank(t)[:], tile(SE, t), ALU.add).then_inc(taken[t % 4].sem, 1)
                residual(place, 1, lambda t: scale[:, NT + t:NT + t + 1])
                normalise(place, 2, 1, lambda t: scale[:, 2 * NT + t:2 * NT + t + 1],
                          lambda t: shift[:, NT + t:NT + t + 1])
                clear_y(place)
                with dve.Fori(0, FF) as g:
                    steps.enter(g, DVE_GROUP)
                    inner = Place(l, g)
                    mlp_group(inner, LAYER, O_FF, 0,
                              lambda: ada_unit(inner, ADA_FIRST + ADA_MIXER, mod[:, bass.ds(g * 4, 4)]))
                    steps.leave(FF)
                residual(place, 3, lambda t: scale[:, 3 * NT + t:3 * NT + t + 1])
                steps.leave(LAYERS)
            place = Place(LAYERS)
            dve.wait_ge(cols_2.sem, 1)
            steps.did(dve.tensor_copy(cols[:, 0:3 * NT], PM[0][:, 0:3 * NT]))
            steps.did(dve.tensor_scalar(neg_sink, PM[0][:, 3 * NT:4 * NT], -1.0, None, ALU.mult))
            steps.wait()

            def normalise_2(m, n, gain):
                token_rstd(place, m)

                def value(t):
                    dve.scalar_tensor_tensor(va[:, t % 2, :], X[:, t, :], cols[:, gain + t:gain + t + 1], rb,
                                             ALU.mult, ALU.mult).then_inc(hv_ready.sem, 1)

                value(0)
                for t in range(NT):
                    if t + 1 < NT:
                        if t:
                            wait(dve, place, hs_ready, 8 * n + t)
                        value(t + 1)
                    wait(dve, place, hh_ready, 8 * n + t + 1)
                    dve.tensor_tensor(tile_r(SB_, t), va[:, t % 2, :], tile_r(SA, t).bitcast(F32),
                                      ALU.subtract).then_inc(hs_ready.sem, 1)

            normalise_2(0, 0, 0)
            wait(dve, place, hs_ready, NT)

            def rope(r, dst):
                o = ROPED[r]
                v, s = va[:, r % 2, :], sqt[:, r % 2, :]
                dve.wait_ge(swapped.sem, 4 * (r + 1))
                if r >= 2:
                    dve.wait_ge(roped.sem, ROPE_SUMS[r - 2])
                dve.tensor_tensor(v, bank(o)[:], C4, ALU.mult).then_inc(taken[o % 4].sem, 1)
                steps.did(dve.tensor_tensor(s, s, S4, ALU.mult))
                steps.wait()
                wait_taken(dve, place, o)
                for to, p0, p1 in dst:
                    dve.tensor_tensor(to, v[p0:p1, :], s[p0:p1, :], ALU.add).then_inc(roped.sem, 1)

            def key_parts(kd):
                return [(kd(g)[e * HD:(e + 1) * HD, :], g * HD, (g + 1) * HD) for g in range(2) for e in range(2)]

            dve.wait_ge(rope_loaded.sem, 16 * 8)
            for q in (0, 2):
                s = S4[q * 32:(q + 1) * 32, :]
                steps.did(dve.tensor_scalar(s, s, -1.0, None, ALU.mult))
            steps.wait()
            for r in range(4):
                rope(r, [(tile(SE, r), 0, P)])
            dve.wait_ge(ik_mean.sem, 1)
            dve.wait_ge(iw_done.sem, 1)
            steps.did(dve.tensor_scalar(index_w, PM[0][:, 0:BLK * IH], W_SCALE, None, ALU.mult))
            dve.scalar_tensor_tensor(ik_c, PM[1][0:HD, :], -1.0 / HD, ik_raw[0:HD, :], ALU.mult,
                                     ALU.add).then_inc(ik_centred.sem, 1)
            for r in range(4, 8):
                rope(r, [(tile(SD, r - 4), 0, P)])
            dve.wait_ge(ik_rstd_ready.sem, 1)
            steps.did(dve.tensor_tensor(ik_c, ik_c, ik_rstd, ALU.mult))
            steps.wait()
            dve.tensor_scalar(ik_c, ik_c, idx_gain, idx_move, ALU.mult, ALU.add).then_inc(ik_normed.sem, 1)
            dve.wait_ge(ik_swapped.sem, 2)
            steps.did(dve.tensor_tensor(ik_c, ik_c, C4[0:HD, :], ALU.mult))
            steps.did(dve.tensor_tensor(ik_tmp, ik_tmp, S4[0:HD, :], ALU.mult))
            steps.wait()
            for e in range(2):
                dve.tensor_tensor(IKD[e * HD:(e + 1) * HD, :], ik_c, ik_tmp, ALU.add).then_inc(ik_ready.sem, 1)
            rope(8, key_parts(AKD))
            for r in range(9, 13):
                rope(r, [(tile(SE, r - 5), 0, P)])
            rope(13, key_parts(BKD))

            dve.wait_ge(masks_ready.sem, 2)
            for u in range(3 * IH):
                qb, h = u // IH + 1, u % IH
                n = (qb + 1) * P
                sc = score[:, 0:n]
                wcol = index_w[:, qb * IH + h:qb * IH + h + 1]
                dve.wait_ge(score_relu.sem, u + 1)
                if h == 0:
                    if u:
                        steps.wait()
                    ins = dve.tensor_scalar(sc, relu_s[u % 2][:, 0:n], wcol, None, ALU.mult)
                else:
                    dve.wait_ge(relu_used.sem, u)
                    ins = dve.scalar_tensor_tensor(sc, relu_s[u % 2][:, 0:n], wcol, sc, ALU.mult, ALU.add)
                ins.then_inc(relu_used.sem, 1)
                if h < IH - 1:
                    continue
                dve.wait_ge(relu_used.sem, u + 1)
                own = score[:, n - P:n]
                steps.did(dve.tensor_tensor(own, own, mask_own, ALU.add))
                for k in range(TOPK // 8):
                    steps.wait()
                    steps.did(dve.max(top8, sc))
                    steps.wait()
                    steps.did(dve.match_replace(sc, top8, sc, SELECTED))
                steps.wait()
                steps.did(dve.tensor_scalar(AM[qb][:, 0:n], sc, SELECTED, NEG, ALU.is_gt, ALU.mult))
            steps.wait()

            def logits(u):
                n = unit_keys(u)
                wd, h = u // 8, u % 8
                qb = wd % 4
                if wd < 4:
                    mask = mask_own if qb == 0 else mask_pair
                    first = neg_sink[:, h:h + 1]
                else:
                    mask = mask_own if qb == 0 else AM[qb][:, 0:n]
                    first = -SELECTED
                dve.wait_ge(qk_2.sem, u + 1)
                if u >= 4:
                    dve.wait_ge(pt_done.sem, u - 3)
                dve.tensor_tensor_reduce(LG[u % 4][:, 0:n], PM[u % 2][:, 0:n], mask, -1.0 / 8, first,
                                         ALU.add, ALU.min, neg_max(u)).then_inc(logit_ready.sem, 1)

            def scores_out(u):
                n = unit_keys(u)
                dve.wait_ge(pt_done.sem, u + 1)
                if u >= 4:
                    dve.wait_ge(pv_done.sem, u - 3)
                dve.tensor_copy(PT[u % 4][:, 0:n], PM[2 + u % 2][:, 0:n]).then_inc(pt_ready[1].sem, 1)

            def block_out(wd):
                par = wd % 2 * 8
                sums = stats[:, 16 + par:24 + par]
                dve.wait_ge(exp_ready.sem, 8 * wd + 8)
                if wd < 4:
                    dve.wait_ge(sink_ready.sem, wd + 1)
                    steps.did(dve.tensor_tensor(sums, sums, sink_exp, ALU.add))
                    steps.wait()
                steps.did(dve.reciprocal(recip, sums))
                steps.wait()
                o = U_ATT + 2 * wd
                dve.wait_ge(pv_done.sem, 8 * wd + 8)
                if wd >= 2:
                    dve.wait_ge(ot_done.sem, wd - 1)
                dve.tensor_tensor(OSB[wd % 2].rearrange("p (h d) -> p h d", h=8),
                                  bank(o)[:].rearrange("p (h d) -> p h d", h=8),
                                  recip.unsqueeze(2).to_broadcast([P, 8, HD]), ALU.mult).then_inc(taken[o % 4].sem, 1)

            def out_low(wd):
                o = U_ATT + 2 * wd + 1
                dve.wait_ge(ot_high.sem, wd + 1)
                dve.tensor_tensor(ot_part(region_r, SB_, wd), bank(o)[:].rearrange("p (j q) -> p j q", j=4),
                                  ot_part(region_r, SA, wd).bitcast(F32), ALU.subtract).then_inc(taken[o % 4].sem, 1)

            for u in range(UNITS + 4):
                wd, h = u // 8, u % 8
                if u < UNITS:
                    logits(u)
                    if h == 7 and wd < 4:
                        dve.wait_ge(logit_ready.sem, u + 1)
                        par = wd % 2 * 8
                        dve.tensor_tensor(sink_exp, stats[:, par:8 + par], neg_sink, ALU.subtract).then_inc(sink_diff.sem, 1)
                if u % 2 == 0 and 0 <= u - 1 < UNITS:
                    scores_out(u - 1)
                if wd and h == 2:
                    block_out(wd - 1)
                if wd and h == 6:
                    out_low(wd - 1)
            out_low(7)
            for t in range(NT + 1):
                if t < NT:
                    ya = U_BR + 4 * (t // 2) + t % 2
                    yb = ya + 2
                    if t >= 2:
                        dve.wait_ge(mix_split.sem, t - 1)
                    wait_done(dve, place, SECOND, ya)
                    dve.tensor_tensor(va[:, t % 2, :], bank(ya)[:], tile(SF, t), ALU.mult).then_inc(taken[ya % 4].sem, 1)
                    wait_done(dve, place, SECOND, yb)
                    dve.tensor_tensor(sqt[:, t % 2, :], bank(yb)[:], tile(SG, t), ALU.mult).then_inc(taken[yb % 4].sem, 1)
                    wait_taken(dve, place, ya)
                    wait_taken(dve, place, yb)
                    dve.tensor_tensor(va[:, t % 2, :], va[:, t % 2, :], sqt[:, t % 2, :], ALU.add).then_inc(mix_value.sem, 1)
                if t:
                    dve.wait_ge(mix_high.sem, t)
                    dve.tensor_tensor(tile_r(SD, t - 1), va[:, (t - 1) % 2, :], tile_r(SC, t - 1).bitcast(F32),
                                      ALU.subtract).then_inc(mix_split.sem, 1)
            for t in range(NT):
                o = U_OUT + t
                wait_done(dve, place, SECOND, o)
                dve.tensor_tensor(X[:, t, :], bank(o)[:], X[:, t, :], ALU.add).then_inc(taken[o % 4].sem, 1)
            normalise_2(1, 1, NT)
            with dve.Fori(0, FF - 1) as g:
                steps.enter(g, 0)
                mlp_group(Place(LAYERS, g), SECOND, U_FF, 0, dst=lambda t: X[:, t, :])
                steps.leave(FF - 1)
            mlp_group(Place(LAYERS, FF - 1), SECOND, U_FF, 0, dst=lambda t: X[:, t, :])

            def rows_out(t):
                o = U_LAST + t
                dve.wait_ge(rows_done.sem, t + 1)
                dve.tensor_copy(out_rows[:, :, t * P:(t + 1) * P],
                                bank(o)[:].rearrange("p (s c) -> p s c", s=BLK)).then_inc(out_ready[1].sem, 1)

            token_rstd(place, 2)
            for t in range(NT):
                dve.scalar_tensor_tensor(tile(SE, t), X[:, t, :], cols[:, 2 * NT + t:2 * NT + t + 1], rb,
                                         ALU.mult, ALU.mult).then_inc(final_ready.sem, 1)
                if t % 2 and t >= 3:
                    rows_out(t - 2)
            rows_out(NT - 1)

        @block.tensor
        def _(pe):
            def product(out_ap, high, low, rhs_high, rhs_low, start, stop):
                pe.matmul(out_ap, high, rhs_high, start=start, stop=False)
                pe.matmul(out_ap, low, rhs_high, start=False, stop=False)
                return pe.matmul(out_ap, high, rhs_low, start=False, stop=stop)

            def use_chunk(place, plan, i, jobs, need=None, width=P):
                wait(pe, place, low_ready, plan.split(i))
                s = chunk_slot(i)
                for o, parts, start, stop in jobs:
                    if start:
                        wait_bank(pe, place, o)
                    for n, (kk, c, (hs, ls), k) in enumerate(parts):
                        if need is not None:
                            need(k)
                        ins = product(bank(o)[0:width, :], ring_high[:, s, kk, c:c + width], ring_low[:, s, kk, c:c + width],
                                      tile_r(hs, k), tile_r(ls, k), start and n == 0, stop and n == len(parts) - 1)
                    ins.then_inc(done.sem, 1)

            def use_pair(place, plan, i, o, slots, need=None):
                for kh in range(2):
                    use_chunk(place, plan, i + kh,
                              [(o + m, [(kk, m * P, slots, KC * kh + kk) for kk in range(KC)], kh == 0, kh == 1)
                               for m in range(2)], need)

            class Need:

                def __init__(self, waiting):
                    self.waiting, self.seen = waiting, set()

                def __call__(self, k):
                    if k not in self.seen:
                        self.seen.add(k)
                        self.waiting(k)

            def token_sums(sums, squares, start, stop):
                for s in range(BLK):
                    ins = pe.matmul(sums[:, s:s + 1], squares[:, s * P:(s + 1) * P], ones[:, 0:1],
                                    start=start and s == 0, stop=stop and s == BLK - 1)
                return ins

            def spread(dst, columns):
                for s in range(BLK):
                    ins = pe.matmul(dst[:, s * P:(s + 1) * P], columns[:, s:s + 1].to_broadcast([P, P]), ident[:],
                                    start=True, stop=True)
                return ins

            def norm_sums(place, m):
                for t in range(NT):
                    wait(pe, place, sq_ready, 8 * m + t + 1)
                    token_sums(PM[3], sqt[:, t % 2, :], t == 0, t == NT - 1).then_inc(sq_used.sem, 1)
                wait(pe, place, r_small, m + 1)
                spread(PM[2], inv_cols).then_inc(r_ready.sem, 1)

            def ada_columns(place, k):
                wait(pe, place, ada_summed, k + 2)
                for c in range(4):
                    ins = pe.matmul(PM[1][:, c:c + 1], ada_acc[:, c * P:(c + 1) * P], ones[:, 0:1], start=True, stop=True)
                ins.then_inc(ada_cols.sem, 1)

            def mlp_group(place, plan, i0, o0, k0, between=None):
                h = Need(lambda k: wait(pe, place, hs_ready, 8 + k + 1))
                for p in range(4):
                    use_pair(place, plan, i0 + 2 * p, o0 + 2 * p, (SA, SB_), h)
                f = Need(lambda k: wait(pe, place, fs_ready, k0 + k + 1))
                for p in range(4):
                    use_pair(place, plan, i0 + 8 + 2 * p, o0 + NT + 2 * p, (SC, SD), f)
                    if p == 0 and between is not None:
                        between()

            pe.wait_ge(consts.sem, 1)
            pe.wait_ge(x_loaded.sem, 32)
            pe.transpose(PM[0][:, 0:NT], c_rows, ident[0:NT, 0:NT]).then_inc(c_cols.sem, 1)
            for t in range(NT):
                if t >= 4:
                    pe.wait_ge(x_ready.sem, t - 3)
                for s in range(BLK):
                    ins = pe.transpose(PB[t % 4][:, s * P:(s + 1) * P], x_rows[:, s, t * P:(t + 1) * P], ident[:])
                ins.then_inc(xt_done.sem, 1)
            for k in range(ADA_FIRST):
                ada_columns(Place(), k)

            with pe.Fori(0, LAYERS) as l:
                place = Place(l)
                wait(pe, place, params_loaded, 16 * PARAM_DMAS)
                settled(pe)
                for r, n in ((0, V_BCN + NT), (1, P), (2, P), (3, (CONV_C - 28) * NT)):
                    ins = pe.transpose(PM[0][:, r * P:r * P + n], rows[0:n, r, :], ident[0:n, 0:n])
                ins.then_inc(cols_done.sem, 1)
                norm_sums(place, 0)
                h = Need(lambda k: wait(pe, place, hs_ready, k + 1))
                for p in range(16):
                    use_pair(place, LAYER, 2 * p, 2 * p, (SA, SB_), h)
                    if p < ADA_MIXER:
                        ada_columns(place, ADA_FIRST + p)
                for i0, o0, ready in ((I_V, O_V, xms_ready), (I_Q, O_Q, xcs_ready), (I_K, O_K, xcs_ready)):
                    x = Need(lambda k: wait(pe, place, ready, k + 1))
                    for c in range(2):
                        use_chunk(place, LAYER, i0 + c,
                                  [(o0 + 2 * hd + e, [(2 * (hd - 2 * c) + kt, e * P, (SA, SB_), 2 * hd + kt)
                                                      for kt in range(2)], True, True)
                                   for hd in (2 * c, 2 * c + 1) for e in range(2)], x)
                n = 0
                for i, kinds in ((I_GATE, (0, 1)), (I_GATE + 1, (2,))):
                    wait_loaded(pe, place, i)
                    weights = gate_weights(ring_f[:, chunk_slot(i), :, :], 2 * len(kinds))
                    for a, kind in enumerate(kinds):
                        o0 = (O_Q, O_K, O_V)[kind]
                        for dt in range(2):
                            for hd in range(HEADS):
                                t = 2 * hd + dt
                                wait_taken(pe, place, o0 + t)
                                src = (tile(SG, t), tile(SF, t), xm(t, CONV_M - 1, T))[kind]
                                ins = pe.matmul(PM[0][0:8, :], weights[:, 2 * a + dt, 8 * hd:8 * hd + 8], src,
                                                start=n == 0, stop=n == 3 * NT - 1)
                                n += 1
                    ins.then_inc(done.sem, 1)
                wait_used(pe, place, LAYER, I_GATE + 1)
                pe.sem_inc(gates_done.sem, 1)
                wait(pe, place, gates_biased, 1)
                pe.matmul(PM[1][0:P - HEADS, :], ident[0:8, HEADS:P], gt, start=True, stop=True).then_inc(fg_done.sem, 1)
                for j in range(8):
                    if j >= 2:
                        wait(pe, place, v_ready, j - 1)
                    for q in range(4):
                        ins = pe.transpose(PM[2 + j % 2][:, q * P:(q + 1) * P],
                                           xm(4 * (j % 2) + q, CONV_M - 1 + j // 2 * P, P), ident[:])
                    ins.then_inc(vtr_done.sem, 1)
                wait(pe, place, mrow_ready, 1)
                settled(pe)
                for s in range(BLK):
                    for n, row in enumerate((a_row, m_row)):
                        at = (n * BLK + s) * HEADS
                        ins = pe.transpose(PM[1][:, at:at + HEADS], row[:, s * P:(s + 1) * P], ident[0:HEADS, 0:HEADS])
                ins.then_inc(acol_done.sem, 1)
                wait(pe, place, v_ready, 8)

                def stabiliser(hd):
                    if hd:
                        wait(pe, place, w_ready, 4 * hd)
                    pe.matmul(PM[0][:], ident[0:HEADS, hd:hd + 1].to_broadcast([HEADS, P]), negM,
                              start=True, stop=True).then_inc(bc_done.sem, 1)

                def scores(hd, j):
                    u = 4 * hd + j
                    if u >= 2:
                        wait(pe, place, p_ready, u - 1)
                    for e in range(2):
                        ins = pe.matmul(PM[2 + j % 2][:, 0:T - j * P], tile(SF, 2 * hd + e)[:, j * P:(j + 1) * P],
                                        tile(SG, 2 * hd + e)[:, j * P:T], start=e == 0, stop=e == 1)
                    ins.then_inc(qk_done.sem, 1)

                def conv_mean(t):
                    wait(pe, place, cv_ready, t + 1)
                    if t:
                        wait(pe, place, cxc_ready, t)
                    else:
                        wait(pe, place, acol_ready, 2)
                    pe.matmul(PM[1][:], ones[:], tile(SC, t), start=True, stop=True).then_inc(cmean.sem, 1)

                stabiliser(0)
                scores(0, 0)
                scores(0, 1)
                for hd in range(HEADS):
                    o = O_HEAD + 4 * hd
                    conv_mean(2 * hd)
                    for e in range(2):
                        wait_bank(pe, place, o + e)
                    for j in range(BLK):
                        wait(pe, place, p_ready, 4 * hd + j + 1)
                        for e in range(2):
                            ins = pe.matmul(bank(o + e)[:, j * P:T], vtok[:, j, (2 * hd + e) * P:(2 * hd + e + 1) * P],
                                            prob[:, j, j * P:T], start=j == 0, stop=j == BLK - 1)
                            if j == BLK - 1:
                                ins.then_inc(head_done.sem, 1)
                        if j + 2 < BLK:
                            scores(hd, j + 2)
                    wait_bank(pe, place, o + 2)
                    for s in range(BLK):
                        for j in range(s + 1):
                            ins = pe.matmul(bank(o + 2)[:, s:s + 1], prob[:, j, s * P:(s + 1) * P], ones[:, 0:1],
                                            start=j == 0, stop=j == s)
                    ins.then_inc(head_done.sem, 1)
                    conv_mean(2 * hd + 1)
                    if hd < HEADS - 1:
                        stabiliser(hd + 1)
                        scores(hd + 1, 0)
                        scores(hd + 1, 1)
                    wait(pe, place, rden_ready, hd + 1)
                    wait_bank(pe, place, o + 3)
                    spread(bank(o + 3), rden_cols).then_inc(den_spread.sem, 1)
                wait(pe, place, w_ready, 4 * HEADS)
                for hd in range(HEADS):
                    for e in range(2):
                        wait_taken(pe, place, O_HEAD + 4 * hd + e)
                    if hd >= 2:
                        wait(pe, place, xcn_ready, 2 * hd - 2)
                    else:
                        wait(pe, place, cxc_ready, NT)
                    for e in range(2):
                        ins = pe.matmul(PM[hd % 2][:], ones[:], tile(SF, 2 * hd + e), start=e == 0, stop=e == 1)
                    ins.then_inc(hm_mean.sem, 1)
                for t in range(NT):
                    wait(pe, place, csq_ready, t + 1)
                    token_sums(PM[3][:, t * BLK:(t + 1) * BLK], sqt[:, t % 2, :], True, True).then_inc(cvar.sem, 1)
                wait(pe, place, crn_small, 1)
                for t in range(NT):
                    if t >= 2:
                        wait(pe, place, cy_ready, t - 1)
                    else:
                        wait(pe, place, xcn_ready, NT)
                    spread(PM[t % 2], inv_cols[:, t * BLK:(t + 1) * BLK]).then_inc(crn_ready.sem, 1)
                for t in range(NT):
                    wait(pe, place, sqn_ready, t + 1)
                    token_sums(PM[2][:, t // 2 * BLK:(t // 2 + 1) * BLK], sqt[:, t % 2, :],
                               t % 2 == 0, t % 2 == 1).then_inc(hm_var.sem, 1)
                a = Need(lambda k: wait(pe, place, cas_ready, k + 1))
                for p in range(4):
                    use_pair(place, LAYER, I_OUT + 2 * p, O_OUTA + 2 * p, (SD, SC), a)
                    if p == 0:
                        wait(pe, place, cy_ready, NT)
                        wait(pe, place, hrn_small, 1)
                        for hd in range(HEADS):
                            ins = spread(PM[hd], inv_cols[:, hd * BLK:(hd + 1) * BLK])
                        ins.then_inc(hrn_ready.sem, 1)
                y = Need(lambda k: wait(pe, place, hys_ready, k + 1))
                for p in range(4):
                    use_pair(place, LAYER, I_OUT + 8 + 2 * p, O_OUTH + 2 * p, (SG, SF), y)
                norm_sums(place, 1)
                norm_sums(place, 2)
                with pe.Fori(0, FF) as g:
                    inner = Place(l, g)
                    mlp_group(inner, LAYER, I_FF, O_FF, 0, lambda: ada_columns(inner, ADA_FIRST + ADA_MIXER))
                norm_sums(place, 3)
            place = Place(LAYERS)
            pe.wait_ge(params_2.sem, 16 * 6)
            pe.transpose(PM[0][:, 0:3 * NT], rows_2, ident[0:3 * NT, 0:3 * NT])
            pe.matmul(PM[0][:, 3 * NT:4 * NT], ones[0:1, :], sink_row, start=True, stop=True).then_inc(cols_2.sem, 1)
            norm_sums(place, 0)
            need = Need(lambda k: wait(pe, place, hs_ready, k + 1))

            def values(k):
                o = (U_AV, U_BV)[k]
                wait_taken(pe, place, o)
                if k:
                    pe.wait_ge(vt_ready.sem, k)
                for s in range(BLK):
                    ins = pe.transpose(PM[3][:, s * P:(s + 1) * P], relu_s[k][:, s * P:(s + 1) * P], ident[:])
                ins.then_inc(vt_done.sem, 1)

            for p, (col, n) in enumerate(PROJ):
                o = FIRST_OF[p]
                if n == CW:
                    use_pair(place, SECOND, 2 * p, o, (SA, SB_), need)
                else:
                    for kh in range(2):
                        use_chunk(place, SECOND, 2 * p + kh,
                                  [(o, [(kk, 0, (SA, SB_), KC * kh + kk) for kk in range(KC)], kh == 0, kh == 1)],
                                  need, n)
                if p == 3:
                    wait_taken(pe, place, U_IK)
                    for s in range(BLK):
                        ins = pe.transpose(PM[0][:, s * IH:(s + 1) * IH], ik_raw[HD:IK, s * P:(s + 1) * P],
                                           ident[HD:IK, HD:IK])
                    ins.then_inc(iw_done.sem, 1)
                    pe.matmul(PM[1][0:HD, :], ones[0:HD, 0:HD], ik_raw[0:HD, :], start=True, stop=True).then_inc(ik_mean.sem, 1)
                if p == 4:
                    pe.wait_ge(ik_squared.sem, 1)
                    pe.matmul(PM[2][0:HD, :], ones[0:HD, 0:HD], ik_tmp, start=True, stop=True).then_inc(ik_var.sem, 1)
                if p == 6:
                    values(0)
                if p == 9:
                    values(1)
                if p >= 9:
                    for u in range(*SCORES_AFTER[p - 9]):
                        qb, h = u // IH + 1, u % IH
                        b = h % 2 * HD
                        if u == 0:
                            pe.wait_ge(ik_ready.sem, 2)
                        if u >= 2:
                            pe.wait_ge(score_relu.sem, u - 1)
                        pe.matmul(PM[u % 2][:, 0:(qb + 1) * P], tile(SE, h // 2)[b:b + HD, qb * P:(qb + 1) * P],
                                  IKD[b:b + HD, 0:(qb + 1) * P], start=True, stop=True).then_inc(score_done.sem, 1)

            def unit(u):
                wd, h = u // 8, u % 8
                return wd, h, wd % 4, h // 4, wd >= 4

            def qk(u):
                wd, h, qb, kv, a = unit(u)
                n = unit_keys(u)
                b = h % 2 * HD
                q = tile(SD if a else SE, h // 2 + (0 if a else 4))[b:b + HD, qb * P:(qb + 1) * P]
                k0 = 0 if a else max(qb - 1, 0) * P
                if u >= 2:
                    pe.wait_ge(logit_ready.sem, u - 1)
                else:
                    pe.wait_ge(roped.sem, ROPE_SUMS[-1])
                    pe.wait_ge(score_relu.sem, 3 * IH)
                pe.matmul(PM[u % 2][:, 0:n], q, (AKD if a else BKD)(kv)[b:b + HD, k0:k0 + n],
                          start=True, stop=True).then_inc(qk_2.sem, 1)

            def transposes(u):
                pe.wait_ge(exp_ready.sem, u + 1)
                if u >= 2:
                    pe.wait_ge(pt_ready[u % 2].sem, u // 2)
                else:
                    pe.wait_ge(vt_ready.sem, 2)
                for s in range(unit_keys(u) // P):
                    ins = pe.transpose(PM[2 + u % 2][:, s * P:(s + 1) * P], LG[u % 4][:, s * P:(s + 1) * P], ident[:])
                ins.then_inc(pt_done.sem, 1)

            def pv(u):
                wd, h, qb, kv, a = unit(u)
                n = unit_keys(u) // P
                o = U_ATT + 2 * wd
                pe.wait_ge(pt_ready[u % 2].sem, u // 2 + 1)
                if h == 0:
                    wait_bank(pe, place, o)
                k0 = 0 if a else max(qb - 1, 0)
                for s in range(n):
                    ins = pe.matmul(bank(o)[:, h * HD:(h + 1) * HD], PT[u % 4][:, s * P:(s + 1) * P],
                                    VT[0 if a else 1][:, (k0 + s) * P + kv * HD:(k0 + s) * P + (kv + 1) * HD],
                                    start=s == 0, stop=s == n - 1)
                ins.then_inc(pv_done.sem, 1)

            def back(wd):
                o = U_ATT + 2 * wd
                wait_taken(pe, place, o)
                wait_bank(pe, place, o + 1)
                for j in range(4):
                    ins = pe.transpose(bank(o + 1)[:, j * P:(j + 1) * P], OSB[wd % 2][:, j * P:(j + 1) * P], ident[:])
                ins.then_inc(ot_done.sem, 1)

            qk(0)
            qk(1)
            for u in range(UNITS + 5):
                if u + 2 < UNITS:
                    qk(u + 2)
                if u < UNITS:
                    transposes(u)
                if 0 <= u - 1 < UNITS:
                    pv(u - 1)
                if u >= 8 and u % 8 == 4:
                    back(u // 8 - 1)
            for wd in range(8):
                wait_taken(pe, place, U_ATT + 2 * wd + 1)
            for p in range(4):
                for b in range(2):
                    o = U_BR + 4 * p + 2 * b
                    use_chunk(place, SECOND, J_BRANCH + 2 * p + b,
                              [(o + m, [(kk, m * P, (SA, SB_), 4 * b + kk) for kk in range(KC)], True, True)
                               for m in range(2)])
            mixed = Need(lambda k: pe.wait_ge(mix_split.sem, k + 1))
            for p in range(4):
                use_pair(place, SECOND, J_OUT + 2 * p, U_OUT + 2 * p, (SC, SD), mixed)
            norm_sums(place, 1)
            with pe.Fori(0, FF - 1) as g:
                mlp_group(Place(LAYERS, g), SECOND, J_FF, U_FF, 0)
            mlp_group(Place(LAYERS, FF - 1), SECOND, J_FF, U_FF, 0)
            norm_sums(place, 2)
            for t in range(NT):
                o = U_LAST + t
                pe.wait_ge(final_ready.sem, t + 1)
                if t < 4:
                    wait_bank(pe, place, o)
                else:
                    pe.wait_ge(out_ready[t % 2].sem, (t - 4) // 2 + 1)
                for s in range(BLK):
                    ins = pe.transpose(bank(o)[:, s * P:(s + 1) * P], tile(SE, t)[:, s * P:(s + 1) * P], ident[:])
                ins.then_inc(rows_done.sem, 1)



_INS = ['x', 'c', 'w_ada', 'b_ada', 'g_pre_mix', 'g_post_mix', 'g_pre_mlp', 'g_post_mlp', 'w_in', 'w_conv_m', 'b_conv_m',
        'w_q', 'w_k', 'w_v', 'w_gates', 'b_gates', 'g_mh', 'w_dw', 'b_dw', 'g_cn', 'b_cn', 'w_out', 'w_ff1', 'w_ff2',
        'attn_norm_w_2', 'w_in_2', 'idx_k_norm_w_2', 'idx_k_norm_b_2', 'sinks_2', 'w_branch_a_2', 'w_branch_b_2',
        'w_out_2', 'mlp_norm_w_2', 'w_up_2', 'w_down_2', 'final_norm_w_2']


def kernel(**inputs):
    import concourse.bacc as _bacc
    from concourse.bass_utils import run_bass_kernel_spmd as _run

    nc = _bacc.Bacc("TRN2", target_bir_lowering=False, num_devices=1)
    arrays, w = {}, {}
    given = {name: np.ascontiguousarray(inputs[name]) for name in _INS}
    given["rope_cos"], given["rope_sin"] = rope_tables()
    for name, a in given.items():
        arrays[f"in_{name}"] = a
        w[name] = nc.dram_tensor(f"in_{name}", a.shape, mybir.dt.from_np(a.dtype), kind="ExternalInput").ap()
    out = nc.dram_tensor("out_x", (1, T, D), F32, kind="ExternalOutput").ap()
    program(nc, w, out)
    r = _run(nc, [arrays], core_ids=[0])
    return r.results[0]["out_x"]
```

```python
from contextlib import ExitStack

import numpy as np

import concourse.bass as bass
from concourse import mybir

ALU = mybir.AluOpType
ACT = mybir.ActivationFunctionType
F32 = mybir.dt.float32
F32R = mybir.dt.float32r

P = 128
T = 512
D = 1024
NT = D // P
LAYERS = 2
HEADS = 4
BLK = T // P
FF = 4
EPS = 1e-6
ACT_LAYER, DVE_LAYER, DVE_GROUP = 36, 375, 7
NEG = -1e30
CONV_M, CONV_C = 4, 31

SHARED = 6
SHARES = NT - SHARED
TAPS = (CONV_C - 1) * SHARES
TAPS_FROM = 21
EARLY_TAPS = 14
LATE_TAPS = (12, 24, 27)

RING = 4
KC = 4
CW = 256
AHEAD = 3

I_IN, I_V, I_Q, I_K, I_GATE, I_OUT, I_FF = 0, 32, 34, 36, 38, 40, 56
FF_CHUNKS = 16
LAYER_CHUNKS = I_FF + FF * FF_CHUNKS
GATE_CHUNKS = (I_GATE, I_GATE + 1)
O_GLUB, O_GLUA, O_XM, O_Z, O_V, O_Q, O_K, O_HEAD, O_OUTA, O_OUTH, O_FF = 0, 8, 16, 24, 32, 40, 48, 56, 72, 80, 88
FF_TILES = 16
LAYER_TILES = O_FF + FF * FF_TILES
ADA_UNITS, ADA_FIRST, ADA_MIXER = 12, 4, 8

V_BADA, V_GPREM, V_GPOSTM, V_GPREF, V_GPOSTF, V_BCM, V_GMH, V_BDW, V_GCN, V_BCN = 0, 48, 56, 64, 72, 80, 88, 96, 104, 112
V_WCM, V_WDW = 128, 160
PARAM_DMAS = 15


class Signal:

    def __init__(self, sem, layer=0, group=0):
        self.sem, self.layer, self.group = sem, layer, group


class Place:

    def __init__(self, layer=0, group=None):
        self.layer, self.group = layer, group

    def value(self, signal, n):
        v = n
        if signal.layer:
            v = self.layer * signal.layer + v
        if signal.group and self.group is not None:
            v = self.group * signal.group + v
        return v


class Steps:

    def __init__(self, eng, sem):
        self.eng, self.sem, self.n, self.loops, self.began = eng, sem, 0, [], []

    def did(self, instruction):
        instruction.then_inc(self.sem, 1)
        self.n += 1
        return self.n

    def wait(self, n=None):
        v = self.n if n is None else n
        for register, per in self.loops:
            v = register * per + v
        self.eng.wait_ge(self.sem, v)

    def enter(self, register, per):
        self.loops.append((register, per))
        self.began.append(self.n)

    def leave(self, times):
        _, per = self.loops.pop()
        start = self.began.pop()
        assert self.n - start == per, (self.eng, self.n - start, per)
        self.n = start + per * times


class Region:

    def __init__(self, tensors, starts):
        self.tensors, self.starts = tensors, starts

    def __getitem__(self, at):
        rows, columns = at
        k = max(k for k in range(len(self.tensors)) if self.starts[k] <= columns.start)
        start = self.starts[k]
        assert columns.stop <= self.starts[k + 1]
        return self.tensors[k][rows, columns.start - start:columns.stop - start]


def rope_tables():
    inv = np.float32(1.0) / np.power(np.float32(10000.0), np.arange(0, 64, 2, dtype=np.float32) / np.float32(64))
    angle = np.arange(T, dtype=np.float32)[None, :] * inv.astype(np.float32)[:, None]
    return np.cos(angle).astype(np.float32), np.sin(angle).astype(np.float32)


class Plan:

    def __init__(self, plain=(), width={}):
        self.plain, self.width = plain, width
        self.used, self.tile = [0], {}

    def split(self, i):
        return i + 1 - sum(g <= i for g in self.plain)

    def chunk(self, tiles, finished=()):
        for at, n in finished:
            self.tile[n] = self.used[-1] + at + 1
        self.used.append(self.used[-1] + tiles)

    def pair(self, n):
        self.chunk(2)
        self.chunk(2, [(0, n), (1, n + 1)])


def layer_plan():
    plan = Plan(GATE_CHUNKS)
    for p in range(16):
        plan.pair(2 * p)
    for c in range(6):
        plan.chunk(4, [(j, O_V + 4 * c + j) for j in range(4)])
    plan.chunk(1)
    plan.chunk(1)
    for p in range(8):
        plan.pair(O_OUTA + 2 * p)
    for p in range(FF * FF_CHUNKS // 2):
        plan.pair(O_FF + 2 * p)
    assert len(plan.used) == LAYER_CHUNKS + 1
    return plan


LAYER = layer_plan()

HD, IH, TOPK = 64, 8, 128
IK = HD + IH
W_SCALE = IH ** -0.5 * HD ** -0.5
SELECTED = float(np.float32(-3e38))
PROJ = ([(768, CW), (1024, CW), (1280, IK), (0, CW), (256, CW), (512, CW), (1352, CW), (1608, CW), (1864, CW)]
        + [(2120 + p * CW, CW) for p in range(8)])
J_BRANCH = 2 * len(PROJ)
J_OUT = J_BRANCH + 8
J_FF = J_OUT + 8
U_IQ, U_IK, U_AQ, U_AK, U_AV, U_BQ, U_BK, U_BV, U_GA = 0, 4, 5, 9, 10, 11, 15, 16, 17
U_ATT, U_BR, U_OUT, U_FF = 33, 49, 65, 73
U_LAST = U_FF + FF * FF_TILES
UNITS = 2 * BLK * 8
FIRST_OF = [2 * p - (p > 2) for p in range(len(PROJ))]
PAIR_OF = {o + m: p for p, o in enumerate(FIRST_OF) for m in range(2 if p != 2 else 1)}
ROPED = [0, 1, 2, 3, 5, 6, 7, 8, U_AK, 11, 12, 13, 14, U_BK]
ROPE_SUMS = []
for _o in ROPED:
    ROPE_SUMS.append((ROPE_SUMS[-1] if ROPE_SUMS else 0) + (4 if _o in (U_AK, U_BK) else 1))
_cuts = [0, 4, 8, 10, 13, 16, 19, 22, 24]
SCORES_AFTER = list(zip(_cuts, _cuts[1:]))


def unit_keys(u):
    qb = u // 8 % BLK
    return (min(qb + 1, 2) if u < UNITS // 2 else qb + 1) * P


def second_plan():
    plan = Plan(width={4: IK, 5: IK})
    for p, o in enumerate(FIRST_OF):
        if PROJ[p][1] == CW:
            plan.pair(o)
        else:
            plan.chunk(1)
            plan.chunk(1, [(0, o)])
    for c in range(8):
        plan.chunk(2, [(m, U_BR + 2 * c + m) for m in range(2)])
    for p in range(4):
        plan.pair(U_OUT + 2 * p)
    for p in range(FF * FF_CHUNKS // 2):
        plan.pair(U_FF + 2 * p)
    return plan


SECOND = second_plan()
USED_FIRST = 2 * RING


def program(nc, w, out):
    ctx = ExitStack()
    with ctx:
        def sb(name, shape, dt=F32):
            return ctx.enter_context(nc.sbuf_tensor(name, shape, dt))

        def ps(name):
            return ctx.enter_context(nc.psum_tensor(name, [P, T], F32))

        def sem(name):
            return ctx.enter_context(nc.semaphore(name))

        SLOT = NT * T
        AROW, XROW = T + CONV_C - 1, T + CONV_M - 1
        SA, SB_, SC, SD = 0, SLOT, 2 * SLOT, 3 * SLOT
        SE = SD + NT * AROW
        SF = SE + NT * XROW
        SG, SH = SF + SLOT, SF + 2 * SLOT
        starts = [SA, SB_, SC, SD, SE, SF, SG, SH, SH + SLOT]
        slots_f, slots_r = [], []
        for k, (start, end) in enumerate(zip(starts, starts[1:])):
            with nc.sbuf_tensor(f"slot{k}_f", [P, end - start], F32) as slot_f:
                slots_f.append(slot_f)
            slots_r.append(sb(f"slot{k}_r", [P, end - start], F32R))
        region_f, region_r = Region(slots_f, starts), Region(slots_r, starts)

        def tile(slot, t, n=T):
            return region_f[:, slot + t * T:slot + t * T + n]

        def tile_r(slot, t):
            return region_r[:, slot + t * T:slot + (t + 1) * T]

        with nc.sbuf_tensor("ring_f", [P, RING, KC, CW], F32) as ring_f:
            pass
        ring_low = sb("ring_low", [P, RING, KC, CW], F32R)
        ring_high = sb("ring_high", [P, RING, KC, CW], F32R)
        X = sb("X", [P, NT, T])
        ident = sb("ident", [P, P])
        ones = sb("ones", [P, P])
        upper = sb("upper", [P, P])
        cols = sb("cols", [P, T])
        diagonal_own = sb("diagonals", [P, T])
        root = sb("root", [P, BLK * NT])
        var_cols = sb("var_cols", [P, BLK * NT])
        inv_cols = sb("inv_cols", [P, BLK * NT])
        tmp_cols = sb("tmp_cols", [P, BLK * NT])
        sqt = sb("sqt", [P, 2, T])
        va = sb("va", [P, 2, T])
        mod = sb("mod", [P, 48])
        scale = sb("scale", [P, 4 * NT])
        shift = sb("shift", [P, 2 * NT])
        cact = sb("cact", [P, NT])
        small = sb("small", [P, 64])
        zero = small[:, 0:1]
        bgate = small[0:8, 1:2]
        eps_col = small[:, 2:3]
        one_col = small[:, 3:4]
        idle = small[:, 4:5]
        a_cols = small[:, 8:24]
        em_cols = small[:, 24:40]
        rden_cols = small[:, 40:44]

        PB = [ps(f"product{i}") for i in range(4)]
        PM = [ps(f"side{i}") for i in range(4)]

        rb = PM[2][:]

        diagonals = [diagonal_own[:], va[:, 0, :]]

        x_rows = region_f[:, SA:SA + BLK * D].rearrange("p (s d) -> p s d", s=BLK)
        c_rows = va[0:NT, 0, 0:P]

        def gate_weights(slot, n):
            return slot.rearrange("p k c -> p (k c)")[:, 0:n * 8 * HEADS].rearrange("p (a c) -> p a c", a=n)

        def gated(t, a=0, n=AROW):
            return region_f[:, SD + t * AROW + a:SD + t * AROW + a + n]

        def xm(t, a=0, n=XROW):
            return region_f[:, SE + t * XROW + a:SE + t * XROW + a + n]

        rows = region_f[:, SH:SH + T].rearrange("p (r c) -> p r c", r=4)
        ada_acc = region_f[:, SH + T:SH + 2 * T]
        ada_raw = [region_f[:, SG + b * 4 * T:SG + (b + 1) * 4 * T].rearrange("p (k c) -> p k c", k=4)
                   for b in range(2)]
        vtok = region_f[:, SA:SA + BLK * D].rearrange("p (s c) -> p s c", s=BLK)
        a_row = region_f[0:HEADS, SB_:SB_ + T]
        negM = region_f[0:HEADS, SB_ + T:SB_ + 2 * T]
        m_row = region_f[0:HEADS, SB_ + 2 * T:SB_ + 3 * T]
        one_row = region_f[0:HEADS, SB_ + 3 * T:SB_ + 4 * T]
        prob = region_f[:, SB_ + 4 * T:SB_ + 8 * T].rearrange("p (j c) -> p j c", j=BLK)
        wexp = [region_f[:, SE + b * T:SE + (b + 1) * T] for b in range(2)]
        rden = [region_f[:, SE + (2 + b) * T:SE + (3 + b) * T] for b in range(2)]
        dg = [region_f[:, SE + 6 * T + b * P:SE + 6 * T + (b + 1) * P] for b in range(4)]
        gt, gu, glf, gb = (region_f[0:n, SB_ + k * T:SB_ + (k + 1) * T] for k, n in ((4, 8), (5, HEADS), (6, HEADS),
                                                                                     (7, HEADS)))
        tap = [sqt[:, 0, :], sqt[:, 1, :], va[:, 0, :], va[:, 1, :]]

        C4, S4, IKD = tile(SC, 0), tile(SC, 1), tile(SC, 2)
        VT = [tile(SC, 3), tile(SC, 4)]
        score = tile(SC, 5)
        relu_s = [tile(SC, 6), tile(SC, 7)]
        OSB = [tile(SC, 0), tile(SC, 1)]
        AM = [None, tile(SH, 0), tile(SH, 1), tile(SH, 2)]
        mask_pair = tile(SH, 3, 2 * P)
        mask_before, mask_own = mask_pair[:, 0:P], mask_pair[:, P:2 * P]
        vectors_2 = region_f[:, SH + 3 * T + 2 * P:SH + 4 * T]
        index_w = vectors_2[:, 0:BLK * IH]
        stats = vectors_2[:, 32:64]
        neg_sink, sink_exp, recip, top8 = (vectors_2[:, 64 + 8 * k:72 + 8 * k] for k in range(4))
        idx_gain, idx_move = vectors_2[0:HD, 96:97], vectors_2[0:HD, 97:98]
        sink_row = vectors_2[0:1, 100:108]
        ik_raw, ik_tmp, ik_rstd, ik_c = (tile(SH, 4 + k)[0:IK if k == 0 else HD, :] for k in range(4))
        rows_2 = region_f[0:3 * NT, SH + 7 * T:SH + 7 * T + P]
        PT = [tile(SH, 4 + k) for k in range(4)]
        LG = [sqt[:, 0, :], sqt[:, 1, :], va[:, 0, :], va[:, 1, :]]
        out_rows = region_f[:, SC:SC + BLK * D].rearrange("p (s d) -> p s d", s=BLK)

        def AKD(g):
            return tile(SD, 4 + g)

        def BKD(g):
            return tile(SD, 6 + g)

        def neg_max(u):
            return stats[:, u // 8 % 2 * 8 + u % 8:u // 8 % 2 * 8 + u % 8 + 1]

        def exp_sum(u):
            return stats[:, 16 + u // 8 % 2 * 8 + u % 8:16 + u // 8 % 2 * 8 + u % 8 + 1]

        def ot_part(region, slot, wd):
            at = slot + (4 if wd < 4 else 0) * T
            return region[:, at:at + 4 * T].rearrange("p (j t) -> p j t", j=4)[:, :, wd % 4 * P:(wd % 4 + 1) * P]

        per = LAYER_CHUNKS // RING
        loaded = [Signal(sem(f"chunk_loaded{s}"), 16 * per, 16 * FF_CHUNKS // RING) for s in range(RING)]
        high_ready = Signal(sem("weight_high_ready"), LAYER_CHUNKS - len(GATE_CHUNKS), FF_CHUNKS)
        low_ready = Signal(sem("weight_low_ready"), LAYER_CHUNKS - len(GATE_CHUNKS), FF_CHUNKS)
        done = Signal(sem("product_done"), LAYER.used[-1], 2 * FF_CHUNKS)
        head_done = Signal(sem("head_product_done"), 3 * HEADS)
        taken = [Signal(sem(f"product_taken{b}"), LAYER_TILES // 4, FF_TILES // 4) for b in range(4)]
        consts = Signal(sem("constants_ready"))
        x_loaded = Signal(sem("x_loaded"))
        c_cols = Signal(sem("c_columns"))
        c_act = Signal(sem("c_activated"))
        xt_done = Signal(sem("x_transposed"))
        params_loaded = Signal(sem("params_loaded"), 16 * PARAM_DMAS)
        cols_done = Signal(sem("param_columns_done"), 1)
        ada_loaded = [Signal(sem(f"ada_loaded{b}"), 16 * ADA_UNITS, 16) for b in range(2)]
        ada_used = Signal(sem("ada_used"), ADA_UNITS, 1)
        ada_summed = Signal(sem("ada_summed"), ADA_UNITS, 1)
        ada_cols = Signal(sem("ada_columns"), ADA_UNITS, 1)
        sq_ready = Signal(sem("square_ready"), 32)
        sq_sums = Signal(sem("square_sums"), 4 * (NT - 1))
        pair_sums = Signal(sem("head_square_sums"), HEADS)
        sq_summed = Signal(sem("squares_summed"), 4)
        r_ready = Signal(sem("rstd_ready"), 4)
        x_ready = Signal(sem("x_ready"), 16)
        hv_ready = Signal(sem("h_value_ready"), 16)
        hh_ready = Signal(sem("h_high_ready"), 16)
        hs_ready = Signal(sem("h_split_ready"), 16)
        xmh_ready = Signal(sem("xm_high_ready"), 8)
        xms_ready = Signal(sem("xm_split_ready"), 8)
        c4_ready = Signal(sem("short_conv_ready"), 8)
        xc_ready = Signal(sem("xc_ready"), 8)
        xch_ready = Signal(sem("xc_high_ready"), 8)
        xcs_ready = Signal(sem("xc_split_ready"), 8)
        gates_done = Signal(sem("gates_done"), 1)
        gates_biased = Signal(sem("gates_biased"), 1)
        fg_done = Signal(sem("forget_rows_done"), 1)
        lsig_ready = Signal(sem("softplus_ready"), 1)
        mrow_ready = Signal(sem("stabilizer_rows_ready"), 1)
        acol_done = Signal(sem("a_columns_done"), 1)
        acol_ready = Signal(sem("a_columns_ready"), 2)
        vtr_done = Signal(sem("value_transposes_done"), 8)
        v_ready = Signal(sem("values_ready"), 8)
        bc_done = Signal(sem("stabilizer_broadcast_done"), HEADS)
        dg_ready = Signal(sem("diagonal_exponent_ready"), 4 * HEADS)
        w_ready = Signal(sem("decay_weights_ready"), 4 * HEADS)
        qk_done = Signal(sem("qk_done"), 4 * HEADS)
        p_ready = Signal(sem("weighted_scores_ready"), 4 * HEADS)
        rden_ready = Signal(sem("denominator_inverse"), HEADS)
        den_spread = Signal(sem("denominator_spread"), HEADS)
        root_ready = Signal(sem("root_ready"), 4)
        r_small = Signal(sem("token_rstd_ready"), 4)
        croot_ready = Signal(sem("group_root_ready"), 1)
        crn_small = Signal(sem("group_token_rstd"), NT)
        hroot_ready = Signal(sem("head_root_ready"), 1)
        hrn_small = Signal(sem("head_token_rstd"), HEADS)
        hrn_ready = Signal(sem("head_rstd_spread"), HEADS)
        hm_mean = Signal(sem("head_mean_done"), HEADS)
        xcn_ready = Signal(sem("head_centred"), 8)
        sqn_ready = Signal(sem("head_squares"), 8)
        hm_var = Signal(sem("head_variance_done"), HEADS)
        hy_ready = Signal(sem("head_out_ready"), 8)
        hyh_ready = Signal(sem("head_out_high"), 8)
        hys_ready = Signal(sem("head_out_split"), 8)
        cv_ready = Signal(sem("long_conv_ready"), SHARED)
        tap_first = Signal(sem("first_taps_ready"), SHARES)
        tap_ready = Signal(sem("tap_product_ready"), TAPS)
        tap_used = Signal(sem("tap_product_added"), TAPS)
        cmean = Signal(sem("group_mean_done"), 8)
        cxc_ready = Signal(sem("group_centred"), 8)
        csq_ready = Signal(sem("group_squares"), 8)
        cvar = Signal(sem("group_variance_done"), 8)
        crn_ready = Signal(sem("group_rstd_ready"), 8)
        cy_ready = Signal(sem("group_normed"), 8)
        ca_ready = Signal(sem("conv_out_ready"), 8)
        cah_ready = Signal(sem("conv_out_high"), 8)
        cas_ready = Signal(sem("conv_out_split"), 8)
        relu_ready = Signal(sem("relu_ready"), 8 * FF, 8)
        fh_ready = Signal(sem("hidden_high"), 8 * FF, 8)
        fs_ready = Signal(sem("hidden_split"), 8 * FF, 8)
        y_cleared = Signal(sem("y_cleared"), 1)
        params_2 = Signal(sem("second_params_loaded"))
        rope_loaded = Signal(sem("rope_tables_loaded"))
        masks_ready = Signal(sem("masks_ready"))
        cols_2 = Signal(sem("second_columns_done"))
        swapped = Signal(sem("rope_swapped"))
        roped = Signal(sem("rope_sums"))
        iw_done = Signal(sem("index_weights_done"))
        ik_mean = Signal(sem("index_key_mean"))
        ik_centred = Signal(sem("index_key_centred"))
        ik_squared = Signal(sem("index_key_squares"))
        ik_var = Signal(sem("index_key_variance"))
        ik_rstd_ready = Signal(sem("index_key_rstd"))
        ik_normed = Signal(sem("index_key_normed"))
        ik_swapped = Signal(sem("index_key_swapped"))
        ik_ready = Signal(sem("index_key_ready"))
        vt_done = Signal(sem("token_values_done"))
        vt_ready = Signal(sem("token_values_ready"))
        score_done = Signal(sem("index_score_done"))
        score_relu = Signal(sem("index_relu_ready"))
        relu_used = Signal(sem("index_relu_used"))
        qk_2 = Signal(sem("logits_done"))
        logit_ready = Signal(sem("masked_logits_ready"))
        exp_ready = Signal(sem("exp_ready"))
        pt_done = Signal(sem("probs_transposed"))
        pv_done = Signal(sem("attention_product_done"))
        sink_diff = Signal(sem("sink_difference"))
        sink_ready = Signal(sem("sink_exp_ready"))
        ot_done = Signal(sem("output_transposed"))
        ot_high = Signal(sem("output_high"))
        mix_value = Signal(sem("mixed_value"))
        mix_high = Signal(sem("mixed_high"))
        mix_split = Signal(sem("mixed_split"))
        final_ready = Signal(sem("final_norm_ready"))
        rows_done = Signal(sem("result_rows_done"))
        pt_ready = [Signal(sem(f"transposed_probs_ready{e}")) for e in range(2)]
        out_ready = [Signal(sem(f"result_rows_ready{e}")) for e in range(2)]
        act_sem = sem("scalar_steps")
        dve_sem = sem("vector_steps")
        pool_sem = sem("gpsimd_steps")
        stored = sem("stored")
        passed = sem("waits_passed")

        def chunk_slot(i):
            return i % RING

        def head_square(t):
            return tile(SB_, t)

        def head_mean_bank(hd):
            return (PB[2], PB[3], PM[2], PM[3])[hd]

        def conv_mean_bank(t):
            return PM[1] if t < SHARED else PM[t % 2]

        def square(m, t):
            return tile(SH if m == 1 else SF, t)

        def wait(eng, place, signal, n):
            eng.wait_ge(signal.sem, place.value(signal, n))

        def settled(eng):
            eng.sem_inc(passed, 1)

        def wait_loaded(eng, place, i):
            wait(eng, place, loaded[chunk_slot(i)], 16 * (i // RING + 1))

        def wait_used(eng, place, plan, i):
            counted = plan.used[i + 1] if i >= 0 else 2 * (i + 1)
            wait(eng, place, done, USED_FIRST + counted)

        def wait_done(eng, place, plan, o):
            wait(eng, place, done, USED_FIRST + plan.tile[o])

        def wait_taken(eng, place, o):
            wait(eng, place, taken[o % 4], o // 4 + 2)

        def wait_bank(eng, place, o):
            wait(eng, place, taken[o % 4], o // 4 + 1)

        def bank(o):
            return PB[o % 4]


        block = ctx.enter_context(nc.Block())

        @block.sync
        def _(sp):
            place = Place()

            def rows_of(ap):
                return ap.rearrange("(k p) c -> p k c", p=P)

            def load(plan, i, src, dst=None):
                wait_used(sp, place, plan, i - RING)
                settled(sp)
                slot = ring_f[:, chunk_slot(i), :, :]
                sp.dma_start(slot if dst is None else dst(slot), src).then_inc(loaded[chunk_slot(i)].sem, 16)

            def load_pair(plan, i, matrix, row, col, between=None):
                for kh in range(2):
                    load(plan, i + kh, rows_of(matrix(row + kh * KC * P, col)))
                    if kh == 0 and between is not None:
                        between()

            def load_ada(layer, unit, k):
                for b in range(2):
                    wait(sp, place, (ada_used, ada_summed)[b], k + 1)
                    settled(sp)
                    src = w["w_ada"][layer, b * 4 * P:(b + 1) * 4 * P, unit_cols(unit)]
                    sp.dma_start(ada_raw[b], rows_of(src)).then_inc(ada_loaded[b].sem, 16)

            def unit_cols(unit):
                return bass.ds(unit * T, T)

            def load_group(plan, i0, first, second, g, k_ada=None):
                for p in range(4):
                    load_pair(plan, i0 + 2 * p, lambda r, c: first(r, c), 0, g * D + p * CW)
                    if k_ada is not None and p == 1:
                        load_ada(1, g, k_ada)
                for p in range(4):
                    load_pair(plan, i0 + 8 + 2 * p, lambda r, c: second(r, c), g * D, p * CW)

            sp.dma_start(x_rows, w["x"][0].rearrange("(s p) d -> p s d", p=P)).then_inc(x_loaded.sem, 16)
            sp.dma_start(c_rows, w["c"][0].rearrange("(t p) -> t p", p=P)).then_inc(x_loaded.sem, 16)
            for unit in range(ADA_FIRST):
                load_ada(0, unit, unit)

            with sp.Fori(0, LAYERS) as l:
                place = Place(l)
                vectors = [("b_ada", V_BADA), ("g_pre_mix", V_GPREM), ("g_post_mix", V_GPOSTM),
                           ("g_pre_mlp", V_GPREF), ("g_post_mlp", V_GPOSTF), ("b_conv_m", V_BCM),
                           ("g_mh", V_GMH), ("b_dw", V_BDW), ("g_cn", V_GCN), ("b_cn", V_BCN)]

                def param(dst, src):
                    sp.dma_start(dst, src).then_inc(params_loaded.sem, 16)

                def load_params():
                    for name, at in vectors:
                        src = w[name][l].rearrange("(t p) -> t p", p=P)
                        param(rows[at:at + src.shape[0], 0, :], src)
                    param(rows[0:32, 1, :], w["w_conv_m"][l].rearrange("k (t p) -> (k t) p", p=P))
                    for r, k0, k1, at in ((1, 0, 12, 32), (2, 12, 28, 0), (3, 28, CONV_C, 0)):
                        param(rows[at:at + (k1 - k0) * NT, r, :],
                              w["w_dw"][l, k0:k1].rearrange("k (t p) -> (k t) p", p=P))
                    param(bgate, w["b_gates"][l].rearrange("(g a) -> g a", a=1))

                def w_in(r, c):
                    return w["w_in"][l, r:r + KC * P, c:c + CW]

                for p in range(16):
                    col = (3 * D, 2 * D, 0, D)[p // 4] + p % 4 * CW
                    load_pair(LAYER, 2 * p, w_in, 0, col, load_params if p == 1 else None)
                    if p < ADA_MIXER:
                        load_ada(l, ADA_FIRST + p, ADA_FIRST + p)
                for i0, name in ((I_V, "w_v"), (I_Q, "w_q"), (I_K, "w_k")):
                    for c in range(2):
                        load(LAYER, i0 + c, w[name][l, 2 * c:2 * c + 2].rearrange("h (k p) e -> p (h k) e", p=P))
                for c, (r0, r1) in enumerate(((0, 2048), (2048, 3072))):
                    n = (r1 - r0) // T
                    load(LAYER, I_GATE + c,
                         w["w_gates"][l, r0:r1, :].rearrange("(a p h) g -> p a (h g)", p=P, h=HEADS),
                         lambda slot: gate_weights(slot, n))
                for part, row in ((I_OUT, D), (I_OUT + 8, 0)):
                    for p in range(4):
                        load_pair(LAYER, part + 2 * p, lambda r, c: w["w_out"][l, r:r + KC * P, c:c + CW], row, p * CW)
                with sp.Fori(0, FF) as g:
                    place = Place(l, g)
                    load_group(LAYER, I_FF,
                               lambda r, c: w["w_ff1"][l, r:r + KC * P, bass.ds(c, CW)],
                               lambda r, c: w["w_ff2"][l, bass.ds(r, KC * P), c:c + CW],
                               g, ADA_FIRST + ADA_MIXER)
                place = Place(l)
            place = Place(LAYERS)

            def w_in_2(n):
                def rows(r, c):
                    return w["w_in_2"][0, r:r + KC * P, c:c + n]
                return rows

            for p, (col, n) in enumerate(PROJ):
                if n == CW:
                    load_pair(SECOND, 2 * p, w_in_2(n), 0, col)
                else:
                    for kh in range(2):
                        load(SECOND, 2 * p + kh, rows_of(w_in_2(n)(kh * KC * P, col)), lambda slot: slot[:, :, 0:n])
                if p == 1:
                    for r, name in enumerate(("attn_norm_w_2", "mlp_norm_w_2", "final_norm_w_2")):
                        src = w[name][0] if r < 2 else w[name]
                        sp.dma_start(rows_2[r * NT:(r + 1) * NT, :],
                                     src.rearrange("(t p) -> t p", p=P)).then_inc(params_2.sem, 16)
                    sp.dma_start(idx_gain, w["idx_k_norm_w_2"][0].rearrange("(g a) -> g a", a=1)).then_inc(params_2.sem, 16)
                    sp.dma_start(idx_move, w["idx_k_norm_b_2"][0].rearrange("(g a) -> g a", a=1)).then_inc(params_2.sem, 16)
                    sp.dma_start(sink_row, w["sinks_2"]).then_inc(params_2.sem, 16)
                    for q in range(4):
                        sp.dma_start(C4[q * 32:(q + 1) * 32, :], w["rope_cos"][:, :]).then_inc(rope_loaded.sem, 16)
                        sp.dma_start(S4[q * 32:(q + 1) * 32, :], w["rope_sin"][:, :]).then_inc(rope_loaded.sem, 16)
            for p in range(4):
                for b, name in enumerate(("w_branch_a_2", "w_branch_b_2")):
                    load(SECOND, J_BRANCH + 2 * p + b, rows_of(w[name][0, :, p * CW:(p + 1) * CW]))
            for p in range(4):
                load_pair(SECOND, J_OUT + 2 * p, lambda r, c: w["w_out_2"][0, r:r + KC * P, c:c + CW], 0, p * CW)
            with sp.Fori(0, FF) as g:
                place = Place(LAYERS, g)
                load_group(SECOND, J_FF,
                           lambda r, c: w["w_up_2"][0, r:r + KC * P, bass.ds(c, CW)],
                           lambda r, c: w["w_down_2"][0, bass.ds(r, KC * P), c:c + CW], g)
            for half in range(2):
                for e in range(2):
                    sp.wait_ge(out_ready[e].sem, 2 * (half + 1))
                sp.dma_start(out[0, :, half * T:(half + 1) * T].rearrange("(s p) d -> p s d", p=P),
                             out_rows[:, :, half * T:(half + 1) * T]).then_inc(stored, 16)
            sp.wait_ge(stored, 32)

        @block.gpsimd
        def _(pool):
            pool.memset(ones[:], 1.0).then_inc(pool_sem, 1)
            pool.memset(ident[:], 0.0).then_inc(pool_sem, 1)
            pool.memset(upper[:], 0.0).then_inc(pool_sem, 1)
            pool.memset(small[:], 0.0).then_inc(pool_sem, 1)
            pool.wait_ge(pool_sem, 4)
            pool.memset(eps_col, EPS).then_inc(pool_sem, 1)
            pool.memset(one_col, 1.0).then_inc(pool_sem, 1)
            pool.affine_select(out=ident[:], in_=ident[:], compare_op=ALU.not_equal, fill=1.0, base=0,
                               pattern=[[-1, P]], channel_multiplier=1).then_inc(pool_sem, 1)
            pool.affine_select(out=upper[:], in_=upper[:], compare_op=ALU.is_ge, fill=NEG, base=0,
                               pattern=[[1, P]], channel_multiplier=-1).then_inc(pool_sem, 1)
            pool.wait_ge(pool_sem, 8)
            pool.sem_inc(consts.sem, 1)
            pool.sem_inc(done.sem, USED_FIRST)
            pool.sem_inc(ada_used.sem, 1)
            pool.sem_inc(ada_summed.sem, 1)
            for b in range(4):
                pool.sem_inc(taken[b].sem, 1)

            def low_part(place, plan, i):
                if i in plan.plain:
                    return
                n = plan.width.get(i, CW)
                s = chunk_slot(i)
                wait(pool, place, high_ready, plan.split(i))
                pool.tensor_tensor(ring_low[:, s, :, 0:n], ring_f[:, s, :, 0:n], ring_high[:, s, :, 0:n].bitcast(F32),
                                   ALU.subtract).then_inc(low_ready.sem, 1)

            def sum_squares(place, m):
                for t in range(1, NT):
                    wait(pool, place, sq_ready, 8 * m + t + 1)
                    if t > 1:
                        wait(pool, place, sq_sums, (NT - 1) * m + t - 1)
                    pool.tensor_tensor(square(m, 0), square(m, 0), square(m, t), ALU.add).then_inc(sq_sums.sem, 1)

            class Taps:

                def __init__(self):
                    self.added = 0

                def add(self, place, n):
                    for u in range(self.added, min(self.added + n, TAPS)):
                        t = SHARED + u % SHARES
                        if u < SHARES:
                            wait(pool, place, tap_first, u + 1)
                        else:
                            wait(pool, place, tap_used, u + 1 - SHARES)
                        wait(pool, place, tap_ready, u + 1)
                        pool.tensor_tensor(tile(SC, t), tile(SC, t), tap[u % 4], ALU.add).then_inc(tap_used.sem, 1)
                    self.added = min(self.added + n, TAPS)

            with pool.Fori(0, LAYERS) as l:
                taps = Taps()
                for i in range(I_GATE):
                    if i == AHEAD:
                        sum_squares(Place(l), 0)
                    low_part(Place(l), LAYER, i)
                    if i >= TAPS_FROM:
                        taps.add(Place(l), 1)
                taps.add(Place(l), TAPS)
                for i in range(I_OUT, I_OUT + AHEAD):
                    low_part(Place(l), LAYER, i)
                for hd in range(HEADS):
                    place = Place(l)
                    wait(pool, place, sqn_ready, 2 * hd + 2)
                    pool.tensor_tensor(head_square(2 * hd), head_square(2 * hd), head_square(2 * hd + 1),
                                       ALU.add).then_inc(pair_sums.sem, 1)
                for i in range(I_OUT + AHEAD, I_FF):
                    low_part(Place(l), LAYER, i)
                sum_squares(Place(l), 1)
                sum_squares(Place(l), 2)
                with pool.Fori(0, FF) as g:
                    for i in range(I_FF, I_FF + FF_CHUNKS):
                        low_part(Place(l, g), LAYER, i)
                sum_squares(Place(l), 3)
            place = Place(LAYERS)
            low_part(place, SECOND, 0)
            pool.memset(mask_pair, 0.0).then_inc(pool_sem, 1)
            pool.wait_ge(pool_sem, 9)
            pool.affine_select(out=mask_own, in_=mask_own, compare_op=ALU.is_ge, fill=NEG, base=0,
                               pattern=[[-1, P]], channel_multiplier=1).then_inc(masks_ready.sem, 1)
            pool.affine_select(out=mask_before, in_=mask_before, compare_op=ALU.is_ge, fill=NEG, base=-1,
                               pattern=[[1, P]], channel_multiplier=-1).then_inc(masks_ready.sem, 1)
            for i in range(1, J_FF):
                if i == AHEAD:
                    sum_squares(place, 0)
                low_part(place, SECOND, i)
            sum_squares(place, 1)
            with pool.Fori(0, FF) as g:
                for i in range(J_FF, J_FF + FF_CHUNKS):
                    low_part(Place(LAYERS, g), SECOND, i)
            sum_squares(place, 2)

        @block.scalar
        def _(act):
            steps = Steps(act, act_sem)

            def high_part(place, plan, i):
                if i in plan.plain:
                    return
                n = plan.width.get(i, CW)
                s = chunk_slot(i)
                wait_loaded(act, place, i)
                act.activation(ring_high[:, s, :, 0:n], ring_f[:, s, :, 0:n], ACT.Copy).then_inc(high_ready.sem, 1)

            class Ahead:

                def __init__(self, plan, made):
                    self.plan, self.made = plan, made

                def of(self, place, i, last=None):
                    upto = i + AHEAD + 1
                    if last is not None:
                        upto = min(upto, last)
                    while self.made < upto:
                        high_part(place, self.plan, self.made)
                        self.made += 1

            def square_root_next():
                steps.did(act.activation(idle, zero, ACT.Sqrt))
                steps.wait()

            def deviation(place, sums, n, signal):
                act.activation(root[:, 0:sums.shape[1]], sums, ACT.Sqrt, bias=eps_col,
                               scale=1.0 / n).then_inc(signal.sem, 1)

            def norm_stats(place, m, src, ready):
                for t in range(NT):
                    ready(t)
                    act.activation(square(m, t), src(t), ACT.Square).then_inc(sq_ready.sem, 1)
                square_root_next()
                wait(act, place, sq_summed, m + 1)
                deviation(place, PM[3][:, 0:BLK], D, root_ready)

            def split_high(place, n, gain=None, move=None):
                for t in range(NT):
                    wait(act, place, hv_ready, 8 * n + t + 1)
                    if gain is not None:
                        v = va[:, t % 2, :]
                        steps.did(act.activation(v, v, ACT.Identity, scale=gain(t), bias=move(t)))
                        steps.wait()
                    act.activation(tile_r(SA, t), va[:, t % 2, :], ACT.Copy).then_inc(hh_ready.sem, 1)

            def mlp_group(place, plan, ahead, i0, o0, sums=None, last=None):
                for t in range(NT):
                    ahead.of(place, i0 + t, last)
                    wait_done(act, place, plan, o0 + t)
                    if t >= 2:
                        wait_taken(act, place, o0 + t - 2)
                    act.activation(sqt[:, t % 2, :], bank(o0 + t)[:], ACT.Relu).then_inc(relu_ready.sem, 1)
                    if t:
                        hidden_high(place, o0, t - 1)
                hidden_high(place, o0, NT - 1)
                if sums is None:
                    ahead.of(place, i0 + FF_CHUNKS - 1, last)
                else:
                    m, src = sums

                    def summed(t):
                        ahead.of(place, i0 + NT + t, last)
                        wait_taken(act, place, o0 + NT + t)

                    norm_stats(place, m, src, summed)

            def hidden_high(place, o0, t):
                wait_taken(act, place, o0 + t)
                act.activation(tile_r(SC, t), va[:, t % 2, :], ACT.Copy).then_inc(fh_ready.sem, 1)

            def conv_high(place, t):
                wait(act, place, ca_ready, t + 1)
                act.activation(tile_r(SD, t), tile(SC, t), ACT.Copy).then_inc(cah_ready.sem, 1)

            class Taps:

                def __init__(self):
                    self.made = 0

                def first(self, place):
                    for t in range(SHARED, NT):
                        wait_taken(act, place, O_GLUA + t)
                        act.activation(tile(SC, t), gated(t, 0, T), ACT.Identity, bias=cols[:, V_BDW + t:V_BDW + t + 1],
                                       scale=cols[:, V_WDW + t:V_WDW + t + 1]).then_inc(tap_first.sem, 1)

                def make(self, place, n):
                    for u in range(self.made, min(self.made + n, TAPS)):
                        k, t = 1 + u // SHARES, SHARED + u % SHARES
                        if u >= 4:
                            wait(act, place, tap_used, u - 3)
                        at = V_WDW + k * NT + t
                        act.activation(tap[u % 4], gated(t, k, T), ACT.Identity,
                                       scale=cols[:, at:at + 1]).then_inc(tap_ready.sem, 1)
                    self.made = min(self.made + n, TAPS)

            act.wait_ge(consts.sem, 1)
            act.wait_ge(c_cols.sem, 1)
            act.activation(cact[:], PM[0][:, 0:NT], ACT.Silu).then_inc(c_act.sem, 1)
            for i in range(AHEAD):
                high_part(Place(), LAYER, i)

            with act.Fori(0, LAYERS) as l:
                place = Place(l)
                steps.enter(l, ACT_LAYER)
                ahead = Ahead(LAYER, AHEAD)
                norm_stats(place, 0, lambda t: X[:, t, :], lambda t: wait(act, place, x_ready, t + 1))
                split_high(place, 0, lambda t: scale[:, t:t + 1], lambda t: shift[:, t:t + 1])
                for t in range(NT):
                    ahead.of(place, t)
                    wait_done(act, place, LAYER, O_GLUB + t)
                    act.activation(tile(SC, t), bank(t)[:], ACT.Sigmoid).then_inc(taken[t % 4].sem, 1)
                taps = Taps()
                for t in range(NT):
                    ahead.of(place, 16 + t)
                    wait_done(act, place, LAYER, O_XM + t)
                    act.activation(xm(t, CONV_M - 1, T), bank(t)[:], ACT.Copy).then_inc(taken[t % 4].sem, 1)
                    if t == 0:
                        taps.first(place)
                    taps.make(place, 1)
                for t in range(NT):
                    ahead.of(place, 24 + t)
                    if t == NT - 3:
                        for u in range(NT):
                            wait(act, place, c4_ready, u + 1)
                            act.activation(tile(SF, u), tile(SF, u), ACT.Silu,
                                           bias=cols[:, V_BCM + u:V_BCM + u + 1]).then_inc(xc_ready.sem, 1)
                    wait_done(act, place, LAYER, O_Z + t)
                    act.activation(tile(SH, t), bank(t)[:], ACT.Sigmoid).then_inc(taken[t % 4].sem, 1)
                    taps.make(place, 1)
                for t in range(NT):
                    act.activation(tile_r(SA, t), xm(t, CONV_M - 1, T), ACT.Copy).then_inc(xmh_ready.sem, 1)
                for t in range(NT):
                    if t == 4:
                        ahead.of(place, 33)
                    wait_done(act, place, LAYER, O_V + t)
                    wait(act, place, xms_ready, t + 1)
                    act.activation(xm(t, CONV_M - 1, T), bank(t)[:], ACT.Copy).then_inc(taken[t % 4].sem, 1)
                for t in range(NT):
                    wait(act, place, xc_ready, t + 1)
                    act.activation(tile_r(SA, t), tile(SF, t), ACT.Copy).then_inc(xch_ready.sem, 1)
                for t in range(NT):
                    ahead.of(place, I_Q + t // 4)
                    wait_done(act, place, LAYER, O_Q + t)
                    act.activation(tile(SG, t), bank(t)[:], ACT.Copy).then_inc(taken[t % 4].sem, 1)
                wait(act, place, xcs_ready, NT)
                for t in range(NT):
                    ahead.of(place, I_K + t // 4)
                    wait_done(act, place, LAYER, O_K + t)
                    act.activation(tile(SF, t), bank(t)[:], ACT.Copy).then_inc(taken[t % 4].sem, 1)
                for j in range(8):
                    wait(act, place, vtr_done, j + 1)
                    act.activation(vtok[:, j // 2, j % 2 * T:(j % 2 + 1) * T], PM[2 + j % 2][:],
                                   ACT.Copy).then_inc(v_ready.sem, 1)
                    taps.make(place, 1)
                wait(act, place, fg_done, 1)
                steps.did(act.activation(gu, PM[1][0:HEADS, :], ACT.Abs))
                steps.wait()
                steps.did(act.activation(gu, gu, ACT.Exp, scale=-1.0))
                steps.wait()
                act.activation(gu, gu, ACT.Ln, bias=one_col[0:HEADS]).then_inc(lsig_ready.sem, 1)
                wait(act, place, acol_done, 1)
                act.activation(a_cols, PM[1][:, 0:BLK * HEADS], ACT.Copy).then_inc(acol_ready.sem, 1)
                act.activation(em_cols, PM[1][:, BLK * HEADS:2 * BLK * HEADS], ACT.Exp, scale=-1.0).then_inc(acol_ready.sem, 1)
                ahead.of(place, I_OUT - 1)

                def decay(h, j):
                    u = 4 * h + j
                    a_col = a_cols[:, j * HEADS + h:j * HEADS + h + 1]
                    if u >= 2:
                        wait(act, place, p_ready, u - 1)
                    if j == 0:
                        wait(act, place, dg_ready, 4 * h + BLK)
                    if j < BLK - 1:
                        steps.did(act.activation(wexp[u % 2][:, P:T - j * P], PM[0][:, (j + 1) * P:T],
                                                 ACT.Exp, bias=a_col))
                        steps.wait()
                    act.activation(wexp[u % 2][:, 0:P], dg[j], ACT.Exp).then_inc(w_ready.sem, 1)
                    taps.make(place, 3)

                wait(act, place, acol_ready, 2)
                decay(0, 0)
                decay(0, 1)
                for h in range(HEADS):
                    decay(h, 2)
                    decay(h, 3)
                    if h < HEADS - 1:
                        decay(h + 1, 0)
                        decay(h + 1, 1)
                    wait(act, place, den_spread, h + 1)
                    if h >= 2:
                        wait_taken(act, place, O_HEAD + 4 * h - 8)
                        wait_taken(act, place, O_HEAD + 4 * h - 7)
                    o = O_HEAD + 4 * h + 3
                    act.activation(rden[h % 2], bank(o)[:], ACT.Copy).then_inc(taken[o % 4].sem, 1)
                wait(act, place, tap_used, TAPS)
                for t in range(NT):
                    wait(act, place, cxc_ready, t + 1)
                    if t >= 2:
                        wait(act, place, cvar, t - 1)
                    act.activation(sqt[:, t % 2, :], tile(SC, t), ACT.Square).then_inc(csq_ready.sem, 1)
                square_root_next()
                wait(act, place, cvar, NT)
                deviation(place, PM[3][:, 0:BLK * NT], P, croot_ready)
                for t in range(NT):
                    wait(act, place, cy_ready, t + 1)
                    act.activation(tile(SC, t), tile(SC, t), ACT.Silu, scale=cols[:, V_GCN + t:V_GCN + t + 1],
                                   bias=cols[:, V_BCN + t:V_BCN + t + 1]).then_inc(ca_ready.sem, 1)
                    if t:
                        conv_high(place, t - 1)
                conv_high(place, NT - 1)
                ahead.of(place, I_OUT)
                for t in range(NT):
                    wait(act, place, xcn_ready, t + 1)
                    act.activation(head_square(t), tile(SF, t), ACT.Square).then_inc(sqn_ready.sem, 1)

                def conv_share(t):
                    ahead.of(place, I_OUT + t)
                    wait_done(act, place, LAYER, O_OUTA + t)
                    act.activation(tile(SE, t), bank(t)[:], ACT.Copy).then_inc(taken[t % 4].sem, 1)

                def head_out_high(t):
                    wait(act, place, hy_ready, t + 1)
                    act.activation(tile_r(SG, t), va[:, t % 2, :], ACT.Copy).then_inc(hyh_ready.sem, 1)

                square_root_next()
                wait(act, place, hm_var, HEADS)
                wait(act, place, crn_small, 1)
                deviation(place, PM[2][:, 0:BLK * HEADS], 2 * P, hroot_ready)
                for t in range(4):
                    conv_share(t)
                for t in range(4):
                    head_out_high(t)
                conv_share(4)
                conv_share(5)
                for t in range(4, NT):
                    head_out_high(t)
                conv_share(6)
                conv_share(7)

                def summed(t):
                    ahead.of(place, I_OUT + NT + t)
                    wait_taken(act, place, O_OUTH + t)

                norm_stats(place, 1, lambda t: tile(SE, t), summed)
                norm_stats(place, 2, lambda t: X[:, t, :], lambda t: wait(act, place, x_ready, 8 + t + 1))
                split_high(place, 1, lambda t: scale[:, 2 * NT + t:2 * NT + t + 1],
                           lambda t: shift[:, NT + t:NT + t + 1])
                with act.Fori(0, FF - 1) as g:
                    steps.enter(g, 0)
                    mlp_group(Place(l, g), LAYER, Ahead(LAYER, I_FF + AHEAD), I_FF, O_FF)
                    steps.leave(FF - 1)
                mlp_group(Place(l, FF - 1), LAYER, Ahead(LAYER, I_FF + AHEAD), I_FF, O_FF, (3, lambda t: tile(SE, t)))
                steps.leave(LAYERS)
            place = Place(LAYERS)
            ahead = Ahead(SECOND, AHEAD)
            norm_stats(place, 0, lambda t: X[:, t, :], lambda t: wait(act, place, x_ready, t + 1))
            split_high(place, 0)

            def swap(src, dst, signal, quadrants=4):
                for q in range(quadrants):
                    p0, p1 = q * 32, (q ^ 1) * 32
                    act.activation(dst[p0:p0 + 32, :], src[p1:p1 + 32, :], ACT.Copy).then_inc(signal.sem, 1)

            def rope(r):
                o = ROPED[r]
                ahead.of(place, 2 * PAIR_OF[o])
                wait_done(act, place, SECOND, o)
                if r >= 2:
                    act.wait_ge(roped.sem, ROPE_SUMS[r - 2])
                swap(bank(o), sqt[:, r % 2, :], swapped)

            for r in range(4):
                rope(r)
            wait_done(act, place, SECOND, U_IK)
            act.activation(ik_raw, bank(U_IK)[0:IK, :], ACT.Copy).then_inc(taken[U_IK % 4].sem, 1)
            rope(4)
            rope(5)
            act.wait_ge(ik_centred.sem, 1)
            act.activation(ik_tmp, ik_c, ACT.Square).then_inc(ik_squared.sem, 1)
            rope(6)
            rope(7)
            act.wait_ge(ik_var.sem, 1)
            steps.did(act.activation(ik_rstd, PM[2][0:HD, :], ACT.Ln, bias=eps_col[0:HD], scale=1.0 / HD))
            steps.wait()
            act.activation(ik_rstd, ik_rstd, ACT.Exp, scale=-0.5).then_inc(ik_rstd_ready.sem, 1)
            act.wait_ge(ik_normed.sem, 1)
            swap(ik_c, ik_tmp, ik_swapped, 2)
            rope(8)

            def token_values(k, o):
                ahead.of(place, 2 * PAIR_OF[o])
                wait_done(act, place, SECOND, o)
                act.activation(relu_s[k], bank(o)[:], ACT.Copy).then_inc(taken[o % 4].sem, 1)

            def values_out(k):
                act.wait_ge(vt_done.sem, k + 1)
                act.activation(VT[k], PM[3][:], ACT.Copy).then_inc(vt_ready.sem, 1)

            token_values(0, U_AV)
            rope(9)
            rope(10)
            values_out(0)
            rope(11)
            rope(12)
            rope(13)
            token_values(1, U_BV)
            u = 0
            for t in range(2 * NT):
                o = U_GA + t
                ahead.of(place, 2 * PAIR_OF[o])
                wait_done(act, place, SECOND, o)
                act.activation(tile(SF, t), bank(o)[:], ACT.Sigmoid).then_inc(taken[o % 4].sem, 1)
                if t == 1:
                    values_out(1)
                if t % 2:
                    for u in range(*SCORES_AFTER[t // 2]):
                        n = (u // 8 + 2) * P
                        act.wait_ge(score_done.sem, u + 1)
                        if u >= 2:
                            act.wait_ge(relu_used.sem, u - 1)
                        else:
                            act.wait_ge(vt_ready.sem, 2)
                        act.activation(relu_s[u % 2][:, 0:n], PM[u % 2][:, 0:n], ACT.Relu).then_inc(score_relu.sem, 1)
            ahead.of(place, J_BRANCH - 1)

            def scores_out(u):
                n = unit_keys(u)
                act.wait_ge(pt_done.sem, u + 1)
                if u >= 4:
                    act.wait_ge(pv_done.sem, u - 3)
                act.activation(PT[u % 4][:, 0:n], PM[2 + u % 2][:, 0:n], ACT.Copy).then_inc(pt_ready[0].sem, 1)

            def out_high(wd):
                act.wait_ge(ot_done.sem, wd + 1)
                o = U_ATT + 2 * wd + 1
                act.activation(ot_part(region_r, SA, wd), bank(o)[:].rearrange("p (j q) -> p j q", j=4),
                               ACT.Copy).then_inc(ot_high.sem, 1)

            for u in range(UNITS + 3):
                wd, h = u // 8, u % 8
                if u < UNITS:
                    n = unit_keys(u)
                    act.wait_ge(logit_ready.sem, u + 1)
                    act.activation(LG[u % 4][:, 0:n], LG[u % 4][:, 0:n], ACT.Exp, bias=neg_max(u), scale=-1.0,
                                   accum_out=exp_sum(u)).then_inc(exp_ready.sem, 1)
                if u % 2 == 1 and u - 1 < UNITS:
                    scores_out(u - 1)
                if u < UNITS and h == 7 and wd < 4:
                    act.wait_ge(sink_diff.sem, wd + 1)
                    act.activation(sink_exp, sink_exp, ACT.Exp).then_inc(sink_ready.sem, 1)
                if h == 5 and wd:
                    out_high(wd - 1)
            out_high(7)
            for t in range(NT):
                o = U_BR + 4 * (t // 2) + t % 2
                ahead.of(place, J_BRANCH + t // 2 * 2 + 1)
                act.wait_ge(mix_value.sem, t + 1)
                act.activation(tile_r(SC, t), va[:, t % 2, :], ACT.Copy).then_inc(mix_high.sem, 1)

            def summed(t):
                ahead.of(place, J_OUT + t)
                wait_taken(act, place, U_OUT + t)

            norm_stats(place, 1, lambda t: X[:, t, :], summed)
            split_high(place, 1)
            with act.Fori(0, FF - 1) as g:
                steps.enter(g, 0)
                mlp_group(Place(LAYERS, g), SECOND, Ahead(SECOND, J_FF + AHEAD), J_FF, U_FF)
                steps.leave(FF - 1)
            mlp_group(Place(LAYERS, FF - 1), SECOND, Ahead(SECOND, J_FF + AHEAD), J_FF, U_FF,
                      (2, lambda t: X[:, t, :]), J_FF + FF_CHUNKS)
            for t in range(0, NT, 2):
                act.wait_ge(rows_done.sem, t + 1)
                o = U_LAST + t
                act.activation(out_rows[:, :, t * P:(t + 1) * P], bank(o)[:].rearrange("p (s c) -> p s c", s=BLK),
                               ACT.Copy).then_inc(out_ready[0].sem, 1)

        @block.vector
        def _(dve):
            steps = Steps(dve, dve_sem)

            def ada_unit(place, k, dst):
                for b in range(2):
                    wait(dve, place, ada_loaded[b], 16 * (k + 1))
                    for kk in range(4):
                        c_col = cact[:, 4 * b + kk:4 * b + kk + 1]
                        if b + kk:
                            if kk:
                                steps.wait()
                            else:
                                wait(dve, place, ada_used, k + 2)
                            ins = dve.scalar_tensor_tensor(ada_acc, ada_raw[b][:, kk, :], c_col, ada_acc,
                                                           ALU.mult, ALU.add)
                        else:
                            ins = dve.tensor_scalar(ada_acc, ada_raw[b][:, kk, :], c_col, None, ALU.mult)
                        if kk < 3:
                            steps.did(ins)
                        elif b == 0:
                            ins.then_inc(ada_used.sem, 1)
                        else:
                            ins.then_inc(ada_summed.sem, 1)
                wait(dve, place, ada_cols, k + 1)
                settled(dve)
                steps.did(dve.tensor_copy(dst, PM[1][:, 0:4]))

            def refine(sums, n, count):
                r, v, y, q = (a[:, 0:count] for a in (root, var_cols, inv_cols, tmp_cols))
                steps.did(dve.tensor_scalar(v, sums[:, 0:count], 1.0 / n, EPS, ALU.mult, ALU.add))
                steps.did(dve.reciprocal(y, r))
                steps.wait()
                steps.did(dve.tensor_tensor(q, y, y, ALU.mult))
                steps.wait()
                steps.did(dve.tensor_tensor(q, q, v, ALU.mult))
                steps.wait()
                steps.did(dve.tensor_scalar(q, q, -0.5, 1.5, ALU.mult, ALU.add))
                steps.wait()
                steps.did(dve.tensor_tensor(y, y, q, ALU.mult))
                steps.wait()

            def on_diagonals(k, columns, signal):
                dve.tensor_tensor(diagonals[k].rearrange("p (s t) -> p s t", s=BLK),
                                  ident[:].unsqueeze(1).to_broadcast([P, BLK, P]),
                                  columns.unsqueeze(2).to_broadcast([P, BLK, P]), ALU.mult).then_inc(signal.sem, 1)

            def token_rstd(place, m):
                wait(dve, place, root_ready, m + 1)
                settled(dve)
                refine(PM[3], D, BLK)
                on_diagonals(0, inv_cols[:, 0:BLK], r_small)
                wait(dve, place, r_ready, m + 1)

            def normalise(place, m, n):
                token_rstd(place, m)

                def value(t):
                    dve.tensor_tensor(va[:, t % 2, :], X[:, t, :], rb, ALU.mult).then_inc(hv_ready.sem, 1)

                def low(t):
                    wait(dve, place, hh_ready, 8 * n + t + 1)
                    dve.tensor_tensor(tile_r(SB_, t), va[:, t % 2, :], tile_r(SA, t).bitcast(F32),
                                      ALU.subtract).then_inc(hs_ready.sem, 1)

                value(0)
                for t in range(NT):
                    if t + 1 < NT:
                        if t:
                            wait(dve, place, hs_ready, 8 * n + t)
                        value(t + 1)
                    low(t)

            def residual(place, m, gain):
                token_rstd(place, m)
                for t in range(0, NT, 2):
                    for u in (t, t + 1):
                        steps.did(dve.tensor_tensor(tile(SE, u), tile(SE, u), rb, ALU.mult))
                    for u in (t, t + 1):
                        steps.wait(steps.n - 1 + u - t)
                        dve.scalar_tensor_tensor(X[:, u, :], tile(SE, u), gain(u), X[:, u, :],
                                                 ALU.mult, ALU.add).then_inc(x_ready.sem, 1)

            def mlp_group(place, plan, o0, k0, between=None, dst=lambda t: tile(SE, t)):
                def low(t):
                    wait(dve, place, fh_ready, k0 + t + 1)
                    dve.tensor_tensor(tile_r(SD, t), va[:, t % 2, :], tile_r(SC, t).bitcast(F32),
                                      ALU.subtract).then_inc(fs_ready.sem, 1)

                for t in range(NT):
                    wait(dve, place, relu_ready, k0 + t + 1)
                    if t >= 2:
                        wait(dve, place, fs_ready, k0 + t - 1)
                    dve.scalar_tensor_tensor(va[:, t % 2, :], bank(o0 + t)[:], 0.0, sqt[:, t % 2, :],
                                             ALU.max, ALU.mult).then_inc(taken[(o0 + t) % 4].sem, 1)
                    if t:
                        low(t - 1)
                low(NT - 1)
                if between is not None:
                    between()
                for t in range(NT):
                    o = o0 + NT + t
                    wait_done(dve, place, plan, o)
                    dve.tensor_tensor(dst(t), bank(o)[:], dst(t), ALU.add).then_inc(taken[o % 4].sem, 1)

            def clear_y(place):
                steps.did(dve.memset(region_f[:, SE:SE + SLOT], 0.0))

            def conv_pair(place, t0, taps, weight, src, dst, bias, signal, begin=0, end=None):
                end = taps if end is None else end
                if begin:
                    steps.wait()
                for k in range(begin, end):
                    for t in (t0, t0 + 1):
                        wk = cols[:, weight + k * NT + t:weight + k * NT + t + 1]
                        if k == 0:
                            ins = dve.tensor_scalar(tile(dst, t), src(t, k, T), wk, bias(t), ALU.mult, ALU.add)
                        else:
                            if k > begin:
                                steps.wait(steps.n - 1 if k < taps - 1 or t == t0 else steps.n)
                            ins = dve.scalar_tensor_tensor(tile(dst, t), src(t, k, T), wk, tile(dst, t),
                                                           ALU.mult, ALU.add)
                        if k < taps - 1:
                            steps.did(ins)
                        else:
                            ins.then_inc(signal.sem, 1)

            def long_conv(place, t0, begin=0, end=None):
                conv_pair(place, t0, CONV_C, V_WDW, gated, SC, lambda t: cols[:, V_BDW + t:V_BDW + t + 1], cv_ready,
                          begin, end)

            dve.wait_ge(consts.sem, 1)
            for t in range(NT):
                wait(dve, Place(), xt_done, t + 1)
                dve.tensor_copy(X[:, t, :], PB[t % 4][:]).then_inc(x_ready.sem, 1)
            dve.wait_ge(c_act.sem, 1)
            for k in range(ADA_FIRST):
                ada_unit(Place(), k, mod[:, 4 * k:4 * k + 4])

            with dve.Fori(0, LAYERS) as l:
                place = Place(l)
                steps.enter(l, DVE_LAYER)
                wait(dve, place, cols_done, 1)
                steps.did(dve.tensor_copy(cols[:, 0:V_BCN + NT], PM[0][:, 0:V_BCN + NT]))
                steps.did(dve.tensor_copy(cols[:, V_WCM:V_WDW + CONV_C * NT], PM[0][:, V_WCM:V_WDW + CONV_C * NT]))
                steps.wait()
                steps.did(dve.tensor_tensor(mod[:, 0:16], mod[:, 0:16], cols[:, V_BADA:V_BADA + 16], ALU.add))
                steps.wait()
                steps.did(dve.scalar_tensor_tensor(scale[:, 0:NT], mod[:, 8:16], 1.0, cols[:, V_GPREM:V_GPREM + NT],
                                                   ALU.add, ALU.mult))
                steps.did(dve.tensor_copy(shift[:, 0:NT], mod[:, 0:NT]))
                steps.wait()
                normalise(place, 0, 0)
                steps.did(dve.memset(region_f[:, SD:SE].rearrange("p (t c) -> p t c", t=NT)[:, :, 0:CONV_C - 1], 0.0))
                steps.did(dve.memset(region_f[:, SE:SF].rearrange("p (t c) -> p t c", t=NT)[:, :, 0:CONV_M - 1], 0.0))
                for p in range(ADA_MIXER):
                    k = ADA_FIRST + p
                    ada_unit(place, k, mod[:, 4 * k:4 * k + 4])
                    if p >= 4:
                        for t in (2 * (p - 4), 2 * (p - 4) + 1):
                            wait_taken(dve, place, O_GLUB + t)
                            wait_done(dve, place, LAYER, O_GLUA + t)
                            dve.tensor_tensor(gated(t, CONV_C - 1, T), bank(t)[:], tile(SC, t),
                                              ALU.mult).then_inc(taken[t % 4].sem, 1)
                steps.wait()
                steps.did(dve.tensor_tensor(mod[:, 16:48], mod[:, 16:48], cols[:, V_BADA + 16:V_BADA + 48], ALU.add))
                steps.wait()
                for dst, m, g in ((1, 2, V_GPOSTM), (3, 5, V_GPOSTF)):
                    steps.did(dve.tensor_tensor(scale[:, dst * NT:(dst + 1) * NT], mod[:, m * NT:(m + 1) * NT],
                                                cols[:, g:g + NT], ALU.mult))
                steps.did(dve.scalar_tensor_tensor(scale[:, 2 * NT:3 * NT], mod[:, 4 * NT:5 * NT], 1.0,
                                                   cols[:, V_GPREF:V_GPREF + NT], ALU.add, ALU.mult))
                steps.did(dve.tensor_copy(shift[:, NT:2 * NT], mod[:, 3 * NT:4 * NT]))
                wait_taken(dve, place, O_GLUA + 6)
                wait_taken(dve, place, O_GLUA + 7)
                long_conv(place, 0, 0, EARLY_TAPS)
                for t in range(0, NT, 2):
                    for u in (t, t + 1):
                        wait_taken(dve, place, O_XM + u)
                    conv_pair(place, t, CONV_M, V_WCM, xm, SF, lambda u: zero, c4_ready)
                long_conv(place, 0, EARLY_TAPS)
                long_conv(place, 2, 0, LATE_TAPS[0])
                for t in range(NT):
                    wait(dve, place, xmh_ready, t + 1)
                    dve.tensor_tensor(tile_r(SB_, t), xm(t, CONV_M - 1, T), tile_r(SA, t).bitcast(F32),
                                      ALU.subtract).then_inc(xms_ready.sem, 1)
                long_conv(place, 2, LATE_TAPS[0], LATE_TAPS[1])
                for t in range(NT):
                    wait(dve, place, xch_ready, t + 1)
                    dve.tensor_tensor(tile_r(SB_, t), tile(SF, t), tile_r(SA, t).bitcast(F32),
                                      ALU.subtract).then_inc(xcs_ready.sem, 1)
                long_conv(place, 4)
                wait(dve, place, gates_done, 1)
                dve.tensor_scalar(gt, PM[0][0:8, :], bgate, None, ALU.add).then_inc(gates_biased.sem, 1)
                steps.did(dve.memset(one_row, 1.0))
                wait(dve, place, lsig_ready, 1)
                steps.did(dve.scalar_tensor_tensor(glf, PM[1][0:HEADS, :], 0.0, gu, ALU.min, ALU.subtract))
                steps.wait()
                steps.did(dve.tensor_tensor_scan(gb, one_row, glf, 0.0, ALU.mult, ALU.add))
                steps.wait()
                wait(dve, place, gates_biased, 1)
                steps.did(dve.tensor_tensor(a_row, gt[0:HEADS], gb, ALU.subtract))
                steps.wait()
                steps.did(dve.tensor_tensor_scan(negM, a_row, a_row, 0.0, ALU.max, ALU.max))
                steps.wait()
                steps.did(dve.tensor_tensor(m_row, gb, negM, ALU.add))
                steps.wait()
                dve.tensor_scalar(negM, negM, -1.0, None, ALU.mult).then_inc(mrow_ready.sem, 1)
                long_conv(place, 2, LATE_TAPS[1], LATE_TAPS[2])

                def diagonal(h):
                    wait(dve, place, bc_done, h + 1)
                    for j in range(BLK):
                        a_col = a_cols[:, j * HEADS + h:j * HEADS + h + 1]
                        dve.scalar_tensor_tensor(dg[j], PM[0][:, j * P:(j + 1) * P], a_col, upper[:],
                                                 ALU.add, ALU.add).then_inc(dg_ready.sem, 1)

                def conv_centre(t):
                    wait(dve, place, cmean, t + 1)
                    dve.scalar_tensor_tensor(tile(SC, t), conv_mean_bank(t)[:], -1.0 / P, tile(SC, t), ALU.mult,
                                             ALU.add).then_inc(cxc_ready.sem, 1)

                wait(dve, place, acol_ready, 2)
                diagonal(0)
                for h in range(HEADS):
                    for j in range(BLK):
                        u = 4 * h + j
                        wait(dve, place, w_ready, u + 1)
                        wait(dve, place, qk_done, u + 1)
                        if h and j == 0:
                            wait(dve, place, head_done, 3 * h)
                        dve.scalar_tensor_tensor(prob[:, j, j * P:T], PM[2 + j % 2][:, 0:T - j * P], 1.0 / 16,
                                                 wexp[u % 2][:, 0:T - j * P], ALU.mult,
                                                 ALU.mult).then_inc(p_ready.sem, 1)
                    for t in range(2 * h, min(2 * h + 2, SHARED)):
                        conv_centre(t)
                    if h == 0:
                        long_conv(place, 2, LATE_TAPS[2])
                    o = O_HEAD + 4 * h
                    wait(dve, place, head_done, 3 * h + 3)
                    den = tmp_cols[:, 0:BLK]
                    steps.did(dve.scalar_tensor_tensor(den, bank(o + 2)[:, 0:BLK], -1.0,
                                                       em_cols.rearrange("p (s h) -> p s h", h=HEADS)[:, :, h],
                                                       ALU.mult, ALU.max))
                    steps.wait()
                    dve.tensor_tensor(den, bank(o + 2)[:, 0:BLK], den, ALU.max).then_inc(taken[(o + 2) % 4].sem, 1)
                    wait_taken(dve, place, o + 2)
                    if h:
                        wait(dve, place, den_spread, h)
                    steps.did(dve.reciprocal(rden_cols, den))
                    steps.wait()
                    on_diagonals(0, rden_cols, rden_ready)
                    if h < HEADS - 1:
                        diagonal(h + 1)
                    wait_taken(dve, place, o + 3)
                    for e in range(2):
                        t = 2 * h + e
                        dve.tensor_tensor(tile(SF, t), bank(o + e)[:], rden[h % 2], ALU.mult).then_inc(
                            taken[(o + e) % 4].sem, 1)
                for t in range(SHARED, NT):
                    conv_centre(t)
                wait(dve, place, croot_ready, 1)
                settled(dve)
                refine(PM[3], P, BLK * NT)
                wait(dve, place, den_spread, HEADS)
                on_diagonals(0, inv_cols[:, 0:BLK], crn_small)
                on_diagonals(1, inv_cols[:, BLK:2 * BLK], crn_small)
                for t in range(NT):
                    wait(dve, place, crn_ready, t + 1)
                    if t + 2 < NT:
                        on_diagonals(t % 2, inv_cols[:, (t + 2) * BLK:(t + 3) * BLK], crn_small)
                    wait(dve, place, cxc_ready, t + 1)
                    dve.tensor_tensor(tile(SC, t), tile(SC, t), PM[t % 2][:], ALU.mult).then_inc(cy_ready.sem, 1)
                for t in range(NT):
                    wait(dve, place, cah_ready, t + 1)
                    dve.tensor_tensor(region_r[:, SC + t * T:SC + (t + 1) * T], tile(SC, t),
                                      tile_r(SD, t).bitcast(F32), ALU.subtract).then_inc(cas_ready.sem, 1)
                    wait(dve, place, hm_mean, t // 2 + 1)
                    wait_taken(dve, place, O_HEAD + 4 * (t // 2) + t % 2)
                    dve.scalar_tensor_tensor(tile(SF, t), head_mean_bank(t // 2)[:], -1.0 / (2 * P), tile(SF, t),
                                             ALU.mult, ALU.add).then_inc(xcn_ready.sem, 1)
                wait(dve, place, hroot_ready, 1)
                settled(dve)
                wait(dve, place, crn_small, NT)
                refine(PM[2], 2 * P, BLK * HEADS)
                wait(dve, place, crn_ready, NT)
                for hd in range(2):
                    on_diagonals(hd, inv_cols[:, hd * BLK:(hd + 1) * BLK], hrn_small)
                for hd in range(2, HEADS):
                    wait(dve, place, hrn_ready, hd - 1)
                    on_diagonals(hd - 2, inv_cols[:, hd * BLK:(hd + 1) * BLK], hrn_small)
                wait(dve, place, hrn_ready, HEADS)

                def head_low(t):
                    wait(dve, place, hyh_ready, t + 1)
                    dve.tensor_tensor(tile_r(SF, t), va[:, t % 2, :], tile_r(SG, t).bitcast(F32),
                                      ALU.subtract).then_inc(hys_ready.sem, 1)

                for t in range(NT):
                    if t >= 2:
                        wait(dve, place, hys_ready, t - 1)
                    steps.did(dve.tensor_tensor(va[:, t % 2, :], tile(SF, t), PM[t // 2][:], ALU.mult))
                    steps.wait()
                    dve.scalar_tensor_tensor(va[:, t % 2, :], va[:, t % 2, :], cols[:, V_GMH + t:V_GMH + t + 1],
                                             tile(SH, t), ALU.mult, ALU.mult).then_inc(hy_ready.sem, 1)
                    if t:
                        head_low(t - 1)
                head_low(NT - 1)
                for t in range(NT):
                    wait_taken(dve, place, O_OUTA + t)
                    wait_done(dve, place, LAYER, O_OUTH + t)
                    dve.tensor_tensor(tile(SE, t), bank(t)[:], tile(SE, t), ALU.add).then_inc(taken[t % 4].sem, 1)
                residual(place, 1, lambda t: scale[:, NT + t:NT + t + 1])
                normalise(place, 2, 1)
                clear_y(place)
                with dve.Fori(0, FF) as g:
                    steps.enter(g, DVE_GROUP)
                    inner = Place(l, g)
                    mlp_group(inner, LAYER, O_FF, 0,
                              lambda: ada_unit(inner, ADA_FIRST + ADA_MIXER, mod[:, bass.ds(g * 4, 4)]))
                    steps.leave(FF)
                residual(place, 3, lambda t: scale[:, 3 * NT + t:3 * NT + t + 1])
                steps.leave(LAYERS)
            place = Place(LAYERS)
            dve.wait_ge(cols_2.sem, 1)
            steps.did(dve.tensor_copy(cols[:, 0:3 * NT], PM[0][:, 0:3 * NT]))
            steps.did(dve.tensor_scalar(neg_sink, PM[0][:, 3 * NT:4 * NT], -1.0, None, ALU.mult))
            steps.wait()

            def normalise_2(m, n, gain):
                token_rstd(place, m)

                def value(t):
                    dve.scalar_tensor_tensor(va[:, t % 2, :], X[:, t, :], cols[:, gain + t:gain + t + 1], rb,
                                             ALU.mult, ALU.mult).then_inc(hv_ready.sem, 1)

                value(0)
                for t in range(NT):
                    if t + 1 < NT:
                        if t:
                            wait(dve, place, hs_ready, 8 * n + t)
                        value(t + 1)
                    wait(dve, place, hh_ready, 8 * n + t + 1)
                    dve.tensor_tensor(tile_r(SB_, t), va[:, t % 2, :], tile_r(SA, t).bitcast(F32),
                                      ALU.subtract).then_inc(hs_ready.sem, 1)

            normalise_2(0, 0, 0)
            wait(dve, place, hs_ready, NT)

            def rope(r, dst):
                o = ROPED[r]
                v, s = va[:, r % 2, :], sqt[:, r % 2, :]
                dve.wait_ge(swapped.sem, 4 * (r + 1))
                if r >= 2:
                    dve.wait_ge(roped.sem, ROPE_SUMS[r - 2])
                dve.tensor_tensor(v, bank(o)[:], C4, ALU.mult).then_inc(taken[o % 4].sem, 1)
                steps.did(dve.tensor_tensor(s, s, S4, ALU.mult))
                steps.wait()
                wait_taken(dve, place, o)
                for to, p0, p1 in dst:
                    dve.tensor_tensor(to, v[p0:p1, :], s[p0:p1, :], ALU.add).then_inc(roped.sem, 1)

            def key_parts(kd):
                return [(kd(g)[e * HD:(e + 1) * HD, :], g * HD, (g + 1) * HD) for g in range(2) for e in range(2)]

            dve.wait_ge(rope_loaded.sem, 16 * 8)
            for q in (0, 2):
                s = S4[q * 32:(q + 1) * 32, :]
                steps.did(dve.tensor_scalar(s, s, -1.0, None, ALU.mult))
            steps.wait()
            for r in range(4):
                rope(r, [(tile(SE, r), 0, P)])
            dve.wait_ge(ik_mean.sem, 1)
            dve.wait_ge(iw_done.sem, 1)
            steps.did(dve.tensor_scalar(index_w, PM[0][:, 0:BLK * IH], W_SCALE, None, ALU.mult))
            dve.scalar_tensor_tensor(ik_c, PM[1][0:HD, :], -1.0 / HD, ik_raw[0:HD, :], ALU.mult,
                                     ALU.add).then_inc(ik_centred.sem, 1)
            for r in range(4, 8):
                rope(r, [(tile(SD, r - 4), 0, P)])
            dve.wait_ge(ik_rstd_ready.sem, 1)
            steps.did(dve.tensor_tensor(ik_c, ik_c, ik_rstd, ALU.mult))
            steps.wait()
            dve.tensor_scalar(ik_c, ik_c, idx_gain, idx_move, ALU.mult, ALU.add).then_inc(ik_normed.sem, 1)
            dve.wait_ge(ik_swapped.sem, 2)
            steps.did(dve.tensor_tensor(ik_c, ik_c, C4[0:HD, :], ALU.mult))
            steps.did(dve.tensor_tensor(ik_tmp, ik_tmp, S4[0:HD, :], ALU.mult))
            steps.wait()
            for e in range(2):
                dve.tensor_tensor(IKD[e * HD:(e + 1) * HD, :], ik_c, ik_tmp, ALU.add).then_inc(ik_ready.sem, 1)
            rope(8, key_parts(AKD))
            for r in range(9, 13):
                rope(r, [(tile(SE, r - 5), 0, P)])
            rope(13, key_parts(BKD))

            ROUNDS = TOPK // 8

            def select(qb, k):
                sc = score[:, 0:(qb + 1) * P]
                steps.wait()
                steps.did(dve.max(top8, sc))
                steps.wait()
                steps.did(dve.match_replace(sc, top8, sc, SELECTED))
                if k == ROUNDS - 1:
                    steps.wait()
                    steps.did(dve.tensor_scalar(AM[qb][:, 0:(qb + 1) * P], sc, SELECTED, NEG, ALU.is_gt, ALU.mult))
                    steps.wait()

            dve.wait_ge(masks_ready.sem, 2)
            for u in range(3 * IH):
                qb, h = u // IH + 1, u % IH
                n = (qb + 1) * P
                sc = score[:, 0:n]
                wcol = index_w[:, qb * IH + h:qb * IH + h + 1]
                dve.wait_ge(score_relu.sem, u + 1)
                if h == 0:
                    if u:
                        steps.wait()
                    ins = dve.tensor_scalar(sc, relu_s[u % 2][:, 0:n], wcol, None, ALU.mult)
                else:
                    dve.wait_ge(relu_used.sem, u)
                    ins = dve.scalar_tensor_tensor(sc, relu_s[u % 2][:, 0:n], wcol, sc, ALU.mult, ALU.add)
                ins.then_inc(relu_used.sem, 1)
                if h < IH - 1:
                    continue
                dve.wait_ge(relu_used.sem, u + 1)
                own = score[:, n - P:n]
                steps.did(dve.tensor_tensor(own, own, mask_own, ALU.add))
                if qb < BLK - 1:
                    for k in range(ROUNDS):
                        select(qb, k)

            def logits(u):
                n = unit_keys(u)
                wd, h = u // 8, u % 8
                qb = wd % 4
                if wd < 4:
                    mask = mask_own if qb == 0 else mask_pair
                    first = neg_sink[:, h:h + 1]
                else:
                    mask = mask_own if qb == 0 else AM[qb][:, 0:n]
                    first = -SELECTED
                dve.wait_ge(qk_2.sem, u + 1)
                if u >= 4:
                    dve.wait_ge(pt_done.sem, u - 3)
                dve.tensor_tensor_reduce(LG[u % 4][:, 0:n], PM[u % 2][:, 0:n], mask, -1.0 / 8, first,
                                         ALU.add, ALU.min, neg_max(u)).then_inc(logit_ready.sem, 1)

            def scores_out(u):
                n = unit_keys(u)
                dve.wait_ge(pt_done.sem, u + 1)
                if u >= 4:
                    dve.wait_ge(pv_done.sem, u - 3)
                dve.tensor_copy(PT[u % 4][:, 0:n], PM[2 + u % 2][:, 0:n]).then_inc(pt_ready[1].sem, 1)

            def block_out(wd):
                par = wd % 2 * 8
                sums = stats[:, 16 + par:24 + par]
                dve.wait_ge(exp_ready.sem, 8 * wd + 8)
                if wd < 4:
                    dve.wait_ge(sink_ready.sem, wd + 1)
                    steps.did(dve.tensor_tensor(sums, sums, sink_exp, ALU.add))
                    steps.wait()
                steps.did(dve.reciprocal(recip, sums))
                steps.wait()
                o = U_ATT + 2 * wd
                dve.wait_ge(pv_done.sem, 8 * wd + 8)
                if wd >= 2:
                    dve.wait_ge(ot_done.sem, wd - 1)
                dve.tensor_tensor(OSB[wd % 2].rearrange("p (h d) -> p h d", h=8),
                                  bank(o)[:].rearrange("p (h d) -> p h d", h=8),
                                  recip.unsqueeze(2).to_broadcast([P, 8, HD]), ALU.mult).then_inc(taken[o % 4].sem, 1)

            def out_low(wd):
                o = U_ATT + 2 * wd + 1
                dve.wait_ge(ot_high.sem, wd + 1)
                dve.tensor_tensor(ot_part(region_r, SB_, wd), bank(o)[:].rearrange("p (j q) -> p j q", j=4),
                                  ot_part(region_r, SA, wd).bitcast(F32), ALU.subtract).then_inc(taken[o % 4].sem, 1)

            for u in range(UNITS + 4):
                wd, h = u // 8, u % 8
                if u < UNITS:
                    logits(u)
                    if u < ROUNDS:
                        select(BLK - 1, u)
                    if h == 7 and wd < 4:
                        dve.wait_ge(logit_ready.sem, u + 1)
                        par = wd % 2 * 8
                        dve.tensor_tensor(sink_exp, stats[:, par:8 + par], neg_sink, ALU.subtract).then_inc(sink_diff.sem, 1)
                if u % 2 == 0 and 0 <= u - 1 < UNITS:
                    scores_out(u - 1)
                if wd and h == 2:
                    block_out(wd - 1)
                if wd and h == 6:
                    out_low(wd - 1)
            out_low(7)
            for t in range(NT + 1):
                if t < NT:
                    ya = U_BR + 4 * (t // 2) + t % 2
                    yb = ya + 2
                    if t >= 2:
                        dve.wait_ge(mix_split.sem, t - 1)
                    wait_done(dve, place, SECOND, ya)
                    dve.tensor_tensor(va[:, t % 2, :], bank(ya)[:], tile(SF, t), ALU.mult).then_inc(taken[ya % 4].sem, 1)
                    wait_done(dve, place, SECOND, yb)
                    dve.tensor_tensor(sqt[:, t % 2, :], bank(yb)[:], tile(SG, t), ALU.mult).then_inc(taken[yb % 4].sem, 1)
                    wait_taken(dve, place, ya)
                    wait_taken(dve, place, yb)
                    dve.tensor_tensor(va[:, t % 2, :], va[:, t % 2, :], sqt[:, t % 2, :], ALU.add).then_inc(mix_value.sem, 1)
                if t:
                    dve.wait_ge(mix_high.sem, t)
                    dve.tensor_tensor(tile_r(SD, t - 1), va[:, (t - 1) % 2, :], tile_r(SC, t - 1).bitcast(F32),
                                      ALU.subtract).then_inc(mix_split.sem, 1)
            for t in range(NT):
                o = U_OUT + t
                wait_done(dve, place, SECOND, o)
                dve.tensor_tensor(X[:, t, :], bank(o)[:], X[:, t, :], ALU.add).then_inc(taken[o % 4].sem, 1)
            normalise_2(1, 1, NT)
            with dve.Fori(0, FF - 1) as g:
                steps.enter(g, 0)
                mlp_group(Place(LAYERS, g), SECOND, U_FF, 0, dst=lambda t: X[:, t, :])
                steps.leave(FF - 1)
            mlp_group(Place(LAYERS, FF - 1), SECOND, U_FF, 0, dst=lambda t: X[:, t, :])

            def rows_out(t):
                o = U_LAST + t
                dve.wait_ge(rows_done.sem, t + 1)
                dve.tensor_copy(out_rows[:, :, t * P:(t + 1) * P],
                                bank(o)[:].rearrange("p (s c) -> p s c", s=BLK)).then_inc(out_ready[1].sem, 1)

            token_rstd(place, 2)
            for t in range(NT):
                dve.scalar_tensor_tensor(tile(SE, t), X[:, t, :], cols[:, 2 * NT + t:2 * NT + t + 1], rb,
                                         ALU.mult, ALU.mult).then_inc(final_ready.sem, 1)
                if t % 2 and t >= 3:
                    rows_out(t - 2)
            rows_out(NT - 1)

        @block.tensor
        def _(pe):
            def product(out_ap, high, low, rhs_high, rhs_low, start, stop):
                pe.matmul(out_ap, high, rhs_high, start=start, stop=False)
                pe.matmul(out_ap, low, rhs_high, start=False, stop=False)
                return pe.matmul(out_ap, high, rhs_low, start=False, stop=stop)

            def use_chunk(place, plan, i, jobs, need=None, width=P):
                wait(pe, place, low_ready, plan.split(i))
                s = chunk_slot(i)
                for o, parts, start, stop in jobs:
                    if start:
                        wait_bank(pe, place, o)
                    for n, (kk, c, (hs, ls), k) in enumerate(parts):
                        if need is not None:
                            need(k)
                        ins = product(bank(o)[0:width, :], ring_high[:, s, kk, c:c + width], ring_low[:, s, kk, c:c + width],
                                      tile_r(hs, k), tile_r(ls, k), start and n == 0, stop and n == len(parts) - 1)
                    ins.then_inc(done.sem, 1)

            def use_pair(place, plan, i, o, slots, need=None):
                for kh in range(2):
                    use_chunk(place, plan, i + kh,
                              [(o + m, [(kk, m * P, slots, KC * kh + kk) for kk in range(KC)], kh == 0, kh == 1)
                               for m in range(2)], need)

            class Need:

                def __init__(self, waiting):
                    self.waiting, self.seen = waiting, set()

                def __call__(self, k):
                    if k not in self.seen:
                        self.seen.add(k)
                        self.waiting(k)

            def token_sums(sums, squares, start, stop):
                for s in range(BLK):
                    ins = pe.matmul(sums[:, s:s + 1], squares[:, s * P:(s + 1) * P], ones[:, 0:1],
                                    start=start and s == 0, stop=stop and s == BLK - 1)
                return ins

            def spread(dst, diagonal):
                return pe.matmul(dst[:], ones[:], diagonal, start=True, stop=True)

            def norm_sums(place, m):
                wait(pe, place, sq_sums, (NT - 1) * (m + 1))
                token_sums(PM[3], square(m, 0), True, True).then_inc(sq_summed.sem, 1)
                wait(pe, place, r_small, m + 1)
                spread(PM[2], diagonals[0]).then_inc(r_ready.sem, 1)

            def ada_columns(place, k):
                wait(pe, place, ada_summed, k + 2)
                for c in range(4):
                    ins = pe.matmul(PM[1][:, c:c + 1], ada_acc[:, c * P:(c + 1) * P], ones[:, 0:1], start=True, stop=True)
                ins.then_inc(ada_cols.sem, 1)

            def mlp_group(place, plan, i0, o0, k0, between=None):
                h = Need(lambda k: wait(pe, place, hs_ready, 8 + k + 1))
                for p in range(4):
                    use_pair(place, plan, i0 + 2 * p, o0 + 2 * p, (SA, SB_), h)
                f = Need(lambda k: wait(pe, place, fs_ready, k0 + k + 1))
                for p in range(4):
                    use_pair(place, plan, i0 + 8 + 2 * p, o0 + NT + 2 * p, (SC, SD), f)
                    if p == 0 and between is not None:
                        between()

            pe.wait_ge(consts.sem, 1)
            pe.wait_ge(x_loaded.sem, 32)
            pe.transpose(PM[0][:, 0:NT], c_rows, ident[0:NT, 0:NT]).then_inc(c_cols.sem, 1)
            for t in range(NT):
                if t >= 4:
                    pe.wait_ge(x_ready.sem, t - 3)
                for s in range(BLK):
                    ins = pe.transpose(PB[t % 4][:, s * P:(s + 1) * P], x_rows[:, s, t * P:(t + 1) * P], ident[:])
                ins.then_inc(xt_done.sem, 1)
            for k in range(ADA_FIRST):
                ada_columns(Place(), k)

            with pe.Fori(0, LAYERS) as l:
                place = Place(l)
                wait(pe, place, params_loaded, 16 * PARAM_DMAS)
                settled(pe)
                for r, n in ((0, V_BCN + NT), (1, P), (2, P), (3, (CONV_C - 28) * NT)):
                    ins = pe.transpose(PM[0][:, r * P:r * P + n], rows[0:n, r, :], ident[0:n, 0:n])
                ins.then_inc(cols_done.sem, 1)
                norm_sums(place, 0)
                h = Need(lambda k: wait(pe, place, hs_ready, k + 1))
                for p in range(16):
                    use_pair(place, LAYER, 2 * p, 2 * p, (SA, SB_), h)
                    if p < ADA_MIXER:
                        ada_columns(place, ADA_FIRST + p)
                for i0, o0, ready in ((I_V, O_V, xms_ready), (I_Q, O_Q, xcs_ready), (I_K, O_K, xcs_ready)):
                    x = Need(lambda k: wait(pe, place, ready, k + 1))
                    for c in range(2):
                        use_chunk(place, LAYER, i0 + c,
                                  [(o0 + 2 * hd + e, [(2 * (hd - 2 * c) + kt, e * P, (SA, SB_), 2 * hd + kt)
                                                      for kt in range(2)], True, True)
                                   for hd in (2 * c, 2 * c + 1) for e in range(2)], x)
                def value_transposes(j):
                    if j == 0:
                        for t in range(4, NT):
                            wait_taken(pe, place, O_V + t)
                    if j >= 2:
                        wait(pe, place, v_ready, j - 1)
                    for q in range(4):
                        ins = pe.transpose(PM[2 + j % 2][:, q * P:(q + 1) * P],
                                           xm(4 * (j % 2) + q, CONV_M - 1 + j // 2 * P, P), ident[:])
                    ins.then_inc(vtr_done.sem, 1)

                n = 0
                for i, kinds in ((I_GATE, (0, 1)), (I_GATE + 1, (2,))):
                    wait_loaded(pe, place, i)
                    weights = gate_weights(ring_f[:, chunk_slot(i), :, :], 2 * len(kinds))
                    for a, kind in enumerate(kinds):
                        o0 = (O_Q, O_K, O_V)[kind]
                        for dt in range(2):
                            for hd in range(HEADS):
                                t = 2 * hd + dt
                                wait_taken(pe, place, o0 + t)
                                src = (tile(SG, t), tile(SF, t), xm(t, CONV_M - 1, T))[kind]
                                ins = pe.matmul(PM[0][0:8, :], weights[:, 2 * a + dt, 8 * hd:8 * hd + 8], src,
                                                start=n == 0, stop=n == 3 * NT - 1)
                                n += 1
                                if a == len(kinds) - 1 and dt == 1 and hd == HEADS - 1:
                                    ins.then_inc(done.sem, 1)
                                if n % 3 == 0:
                                    value_transposes(n // 3 - 1)
                wait_used(pe, place, LAYER, I_GATE + 1)
                pe.sem_inc(gates_done.sem, 1)
                wait(pe, place, gates_biased, 1)
                pe.matmul(PM[1][0:P - HEADS, :], ident[0:8, HEADS:P], gt, start=True, stop=True).then_inc(fg_done.sem, 1)
                wait(pe, place, mrow_ready, 1)
                settled(pe)
                for s in range(BLK):
                    for n, row in enumerate((a_row, m_row)):
                        at = (n * BLK + s) * HEADS
                        ins = pe.transpose(PM[1][:, at:at + HEADS], row[:, s * P:(s + 1) * P], ident[0:HEADS, 0:HEADS])
                ins.then_inc(acol_done.sem, 1)
                wait(pe, place, v_ready, 8)

                def stabiliser(hd):
                    if hd:
                        wait(pe, place, w_ready, 4 * hd)
                    pe.matmul(PM[0][:], ident[0:HEADS, hd:hd + 1].to_broadcast([HEADS, P]), negM,
                              start=True, stop=True).then_inc(bc_done.sem, 1)

                def scores(hd, j):
                    u = 4 * hd + j
                    if u >= 2:
                        wait(pe, place, p_ready, u - 1)
                    for e in range(2):
                        ins = pe.matmul(PM[2 + j % 2][:, 0:T - j * P], tile(SF, 2 * hd + e)[:, j * P:(j + 1) * P],
                                        tile(SG, 2 * hd + e)[:, j * P:T], start=e == 0, stop=e == 1)
                    ins.then_inc(qk_done.sem, 1)

                def conv_mean(t):
                    if t < SHARED:
                        wait(pe, place, cv_ready, t + 1)
                    else:
                        wait(pe, place, tap_used, TAPS - SHARES + t - SHARED + 1)
                    if t == 0:
                        wait(pe, place, acol_ready, 2)
                    elif t == SHARED:
                        wait(pe, place, w_ready, 4 * HEADS)
                    else:
                        wait(pe, place, cxc_ready, t if t < SHARED else t - 1)
                    pe.matmul(conv_mean_bank(t)[:], ones[:], tile(SC, t), start=True, stop=True).then_inc(cmean.sem, 1)

                stabiliser(0)
                scores(0, 0)
                scores(0, 1)
                for hd in range(HEADS):
                    o = O_HEAD + 4 * hd
                    if 2 * hd < SHARED:
                        conv_mean(2 * hd)
                    for e in range(2):
                        wait_bank(pe, place, o + e)
                    for j in range(BLK):
                        wait(pe, place, p_ready, 4 * hd + j + 1)
                        for e in range(2):
                            ins = pe.matmul(bank(o + e)[:, j * P:T], vtok[:, j, (2 * hd + e) * P:(2 * hd + e + 1) * P],
                                            prob[:, j, j * P:T], start=j == 0, stop=j == BLK - 1)
                            if j == BLK - 1:
                                ins.then_inc(head_done.sem, 1)
                        if j + 2 < BLK:
                            scores(hd, j + 2)
                    wait_bank(pe, place, o + 2)
                    for s in range(BLK):
                        for j in range(s + 1):
                            ins = pe.matmul(bank(o + 2)[:, s:s + 1], prob[:, j, s * P:(s + 1) * P], ones[:, 0:1],
                                            start=j == 0, stop=j == s)
                    ins.then_inc(head_done.sem, 1)
                    if 2 * hd < SHARED:
                        conv_mean(2 * hd + 1)
                    if hd < HEADS - 1:
                        stabiliser(hd + 1)
                        scores(hd + 1, 0)
                        scores(hd + 1, 1)
                    wait(pe, place, rden_ready, hd + 1)
                    wait_bank(pe, place, o + 3)
                    spread(bank(o + 3), diagonals[0]).then_inc(den_spread.sem, 1)
                for t in range(SHARED, NT):
                    conv_mean(t)
                for t in range(NT):
                    wait(pe, place, csq_ready, t + 1)
                    token_sums(PM[3][:, t * BLK:(t + 1) * BLK], sqt[:, t % 2, :], True, True).then_inc(cvar.sem, 1)

                def head_mean(hd):
                    for e in range(2):
                        wait_taken(pe, place, O_HEAD + 4 * hd + e)
                    for e in range(2):
                        ins = pe.matmul(head_mean_bank(hd)[:], ones[:], tile(SF, 2 * hd + e), start=e == 0, stop=e == 1)
                    ins.then_inc(hm_mean.sem, 1)

                head_mean(0)
                for t in range(NT):
                    wait(pe, place, crn_small, t + 1)
                    if t >= 2:
                        wait(pe, place, cy_ready, t - 1)
                    spread(PM[t % 2], diagonals[t % 2]).then_inc(crn_ready.sem, 1)
                    if t % 2 and t < 2 * HEADS - 1:
                        head_mean(t // 2 + 1)
                a = Need(lambda k: wait(pe, place, cas_ready, k + 1))
                for p in range(4):
                    use_pair(place, LAYER, I_OUT + 2 * p, O_OUTA + 2 * p, (SD, SC), a)
                    if p == 0:
                        for hd in range(HEADS):
                            wait(pe, place, pair_sums, hd + 1)
                            token_sums(PM[2][:, hd * BLK:(hd + 1) * BLK], head_square(2 * hd), True, True).then_inc(
                                hm_var.sem, 1)
                    if p == 1:
                        for hd in range(HEADS):
                            wait(pe, place, hrn_small, hd + 1)
                            spread(PM[hd], diagonals[hd % 2]).then_inc(hrn_ready.sem, 1)
                y = Need(lambda k: wait(pe, place, hys_ready, k + 1))
                for p in range(4):
                    use_pair(place, LAYER, I_OUT + 8 + 2 * p, O_OUTH + 2 * p, (SG, SF), y)
                norm_sums(place, 1)
                norm_sums(place, 2)
                with pe.Fori(0, FF) as g:
                    inner = Place(l, g)
                    mlp_group(inner, LAYER, I_FF, O_FF, 0, lambda: ada_columns(inner, ADA_FIRST + ADA_MIXER))
                norm_sums(place, 3)
            place = Place(LAYERS)
            pe.wait_ge(params_2.sem, 16 * 6)
            pe.transpose(PM[0][:, 0:3 * NT], rows_2, ident[0:3 * NT, 0:3 * NT])
            pe.matmul(PM[0][:, 3 * NT:4 * NT], ones[0:1, :], sink_row, start=True, stop=True).then_inc(cols_2.sem, 1)
            norm_sums(place, 0)
            need = Need(lambda k: wait(pe, place, hs_ready, k + 1))

            def values(k):
                o = (U_AV, U_BV)[k]
                wait_taken(pe, place, o)
                if k:
                    pe.wait_ge(vt_ready.sem, k)
                for s in range(BLK):
                    ins = pe.transpose(PM[3][:, s * P:(s + 1) * P], relu_s[k][:, s * P:(s + 1) * P], ident[:])
                ins.then_inc(vt_done.sem, 1)

            for p, (col, n) in enumerate(PROJ):
                o = FIRST_OF[p]
                if n == CW:
                    use_pair(place, SECOND, 2 * p, o, (SA, SB_), need)
                else:
                    for kh in range(2):
                        use_chunk(place, SECOND, 2 * p + kh,
                                  [(o, [(kk, 0, (SA, SB_), KC * kh + kk) for kk in range(KC)], kh == 0, kh == 1)],
                                  need, n)
                if p == 3:
                    wait_taken(pe, place, U_IK)
                    for s in range(BLK):
                        ins = pe.transpose(PM[0][:, s * IH:(s + 1) * IH], ik_raw[HD:IK, s * P:(s + 1) * P],
                                           ident[HD:IK, HD:IK])
                    ins.then_inc(iw_done.sem, 1)
                    pe.matmul(PM[1][0:HD, :], ones[0:HD, 0:HD], ik_raw[0:HD, :], start=True, stop=True).then_inc(ik_mean.sem, 1)
                if p == 4:
                    pe.wait_ge(ik_squared.sem, 1)
                    pe.matmul(PM[2][0:HD, :], ones[0:HD, 0:HD], ik_tmp, start=True, stop=True).then_inc(ik_var.sem, 1)
                if p == 6:
                    values(0)
                if p == 9:
                    values(1)
                if p >= 9:
                    for u in range(*SCORES_AFTER[p - 9]):
                        qb, h = u // IH + 1, u % IH
                        b = h % 2 * HD
                        if u == 0:
                            pe.wait_ge(ik_ready.sem, 2)
                        if u >= 2:
                            pe.wait_ge(score_relu.sem, u - 1)
                        pe.matmul(PM[u % 2][:, 0:(qb + 1) * P], tile(SE, h // 2)[b:b + HD, qb * P:(qb + 1) * P],
                                  IKD[b:b + HD, 0:(qb + 1) * P], start=True, stop=True).then_inc(score_done.sem, 1)

            def unit(u):
                wd, h = u // 8, u % 8
                return wd, h, wd % 4, h // 4, wd >= 4

            def qk(u):
                wd, h, qb, kv, a = unit(u)
                n = unit_keys(u)
                b = h % 2 * HD
                q = tile(SD if a else SE, h // 2 + (0 if a else 4))[b:b + HD, qb * P:(qb + 1) * P]
                k0 = 0 if a else max(qb - 1, 0) * P
                if u >= 2:
                    pe.wait_ge(logit_ready.sem, u - 1)
                else:
                    pe.wait_ge(roped.sem, ROPE_SUMS[-1])
                    pe.wait_ge(score_relu.sem, 3 * IH)
                pe.matmul(PM[u % 2][:, 0:n], q, (AKD if a else BKD)(kv)[b:b + HD, k0:k0 + n],
                          start=True, stop=True).then_inc(qk_2.sem, 1)

            def transposes(u):
                pe.wait_ge(exp_ready.sem, u + 1)
                if u >= 2:
                    pe.wait_ge(pt_ready[u % 2].sem, u // 2)
                else:
                    pe.wait_ge(vt_ready.sem, 2)
                for s in range(unit_keys(u) // P):
                    ins = pe.transpose(PM[2 + u % 2][:, s * P:(s + 1) * P], LG[u % 4][:, s * P:(s + 1) * P], ident[:])
                ins.then_inc(pt_done.sem, 1)

            def pv(u):
                wd, h, qb, kv, a = unit(u)
                n = unit_keys(u) // P
                o = U_ATT + 2 * wd
                pe.wait_ge(pt_ready[u % 2].sem, u // 2 + 1)
                if h == 0:
                    wait_bank(pe, place, o)
                k0 = 0 if a else max(qb - 1, 0)
                for s in range(n):
                    ins = pe.matmul(bank(o)[:, h * HD:(h + 1) * HD], PT[u % 4][:, s * P:(s + 1) * P],
                                    VT[0 if a else 1][:, (k0 + s) * P + kv * HD:(k0 + s) * P + (kv + 1) * HD],
                                    start=s == 0, stop=s == n - 1)
                ins.then_inc(pv_done.sem, 1)

            def back(wd):
                o = U_ATT + 2 * wd
                wait_taken(pe, place, o)
                wait_bank(pe, place, o + 1)
                for j in range(4):
                    ins = pe.transpose(bank(o + 1)[:, j * P:(j + 1) * P], OSB[wd % 2][:, j * P:(j + 1) * P], ident[:])
                ins.then_inc(ot_done.sem, 1)

            qk(0)
            qk(1)
            for u in range(UNITS + 5):
                if u + 2 < UNITS:
                    qk(u + 2)
                if u < UNITS:
                    transposes(u)
                if 0 <= u - 1 < UNITS:
                    pv(u - 1)
                if u >= 8 and u % 8 == 4:
                    back(u // 8 - 1)
            for wd in range(8):
                wait_taken(pe, place, U_ATT + 2 * wd + 1)
            for p in range(4):
                for b in range(2):
                    o = U_BR + 4 * p + 2 * b
                    use_chunk(place, SECOND, J_BRANCH + 2 * p + b,
                              [(o + m, [(kk, m * P, (SA, SB_), 4 * b + kk) for kk in range(KC)], True, True)
                               for m in range(2)])
            mixed = Need(lambda k: pe.wait_ge(mix_split.sem, k + 1))
            for p in range(4):
                use_pair(place, SECOND, J_OUT + 2 * p, U_OUT + 2 * p, (SC, SD), mixed)
            norm_sums(place, 1)
            with pe.Fori(0, FF - 1) as g:
                mlp_group(Place(LAYERS, g), SECOND, J_FF, U_FF, 0)
            mlp_group(Place(LAYERS, FF - 1), SECOND, J_FF, U_FF, 0)
            norm_sums(place, 2)
            for t in range(NT):
                o = U_LAST + t
                pe.wait_ge(final_ready.sem, t + 1)
                if t < 4:
                    wait_bank(pe, place, o)
                else:
                    pe.wait_ge(out_ready[t % 2].sem, (t - 4) // 2 + 1)
                for s in range(BLK):
                    ins = pe.transpose(bank(o)[:, s * P:(s + 1) * P], tile(SE, t)[:, s * P:(s + 1) * P], ident[:])
                ins.then_inc(rows_done.sem, 1)



_INS = ['x', 'c', 'w_ada', 'b_ada', 'g_pre_mix', 'g_post_mix', 'g_pre_mlp', 'g_post_mlp', 'w_in', 'w_conv_m', 'b_conv_m',
        'w_q', 'w_k', 'w_v', 'w_gates', 'b_gates', 'g_mh', 'w_dw', 'b_dw', 'g_cn', 'b_cn', 'w_out', 'w_ff1', 'w_ff2',
        'attn_norm_w_2', 'w_in_2', 'idx_k_norm_w_2', 'idx_k_norm_b_2', 'sinks_2', 'w_branch_a_2', 'w_branch_b_2',
        'w_out_2', 'mlp_norm_w_2', 'w_up_2', 'w_down_2', 'final_norm_w_2']


def kernel(**inputs):
    import concourse.bacc as _bacc
    from concourse.bass_utils import run_bass_kernel_spmd as _run

    nc = _bacc.Bacc("TRN2", target_bir_lowering=False, num_devices=1)
    arrays, w = {}, {}
    given = {name: np.ascontiguousarray(inputs[name]) for name in _INS}
    given["rope_cos"], given["rope_sin"] = rope_tables()
    for name, a in given.items():
        arrays[f"in_{name}"] = a
        w[name] = nc.dram_tensor(f"in_{name}", a.shape, mybir.dt.from_np(a.dtype), kind="ExternalInput").ap()
    out = nc.dram_tensor("out_x", (1, T, D), F32, kind="ExternalOutput").ap()
    program(nc, w, out)
    r = _run(nc, [arrays], core_ids=[0])
    return r.results[0]["out_x"]
```
